# Optimizing a Trainium2 kernel written in Bass

```python
import math
import jax, jax.numpy as jnp
from jax import lax
import numpy as np

D_MODEL = 1024
BATCH = 1
SEQ = 256
DEPTH = 1

PLE_DIM = 256
D_FF = 2816
FFN_RES_WEIGHT = 0.5
NORM_EPS = 1e-6
Q_BLOCK = 128

MLA_HEADS = 8
MLA_NOPE = 64
MLA_ROPE = 32
MLA_QK = MLA_NOPE + MLA_ROPE
MLA_V = 64
Q_LORA = 384
KV_LORA = 256
ROPE_BASE = 10000.0

SB_HEADS = 8
SB_HEAD_DIM = 64
SB_WIDTH = SB_HEADS * SB_HEAD_DIM
MLA_WIDTH = MLA_HEADS * MLA_V

COL_CQ = Q_LORA
COL_CKV = KV_LORA
COL_KROPE = MLA_ROPE
COL_SB = 3 * SB_WIDTH
COL_GATES = 2 * D_MODEL
IN_COLS = COL_CQ + COL_CKV + COL_KROPE + COL_SB + COL_GATES
SPLITS = list(np.cumsum([COL_CQ, COL_CKV, COL_KROPE, COL_SB])[:])


def rms_norm(x, g):
    xf = x.astype(jnp.float32)
    r = lax.rsqrt(jnp.mean(xf * xf, axis=-1, keepdims=True) + NORM_EPS)
    return (xf * r).astype(x.dtype) * g

def apply_rope(x, positions):
    r = x.shape[-1]
    inv_freq = ROPE_BASE ** (-jnp.arange(0, r, 2, dtype=jnp.float32) / r)
    ang = positions.astype(jnp.float32)[..., None] * inv_freq
    cos = jnp.cos(ang)[:, :, None, :].astype(x.dtype)
    sin = jnp.sin(ang)[:, :, None, :].astype(x.dtype)
    x1, x2 = x[..., : r // 2], x[..., r // 2:]
    return jnp.concatenate([x1 * cos - x2 * sin, x2 * cos + x1 * sin], axis=-1)

def swiglu(u, w_in, w_out):
    a, b = jnp.split(u @ w_in, 2, axis=-1)
    return (jax.nn.silu(a) * b) @ w_out

def causal_softmax_attention(q, k, v):
    s_len = q.shape[2]
    scale = 1.0 / math.sqrt(q.shape[-1])
    outs = []
    for i in range(s_len // Q_BLOCK):
        k_len = (i + 1) * Q_BLOCK
        qb = q[:, :, i * Q_BLOCK:(i + 1) * Q_BLOCK]
        kb, vb = k[:, :, :k_len], v[:, :, :k_len]
        sc = jnp.einsum('bhqd,bhkd->bhqk', qb, kb).astype(jnp.float32) * scale
        q_pos = i * Q_BLOCK + jnp.arange(Q_BLOCK)
        mask = jnp.arange(k_len)[None, :] <= q_pos[:, None]
        w = jax.nn.softmax(jnp.where(mask, sc, -jnp.inf), axis=-1)
        outs.append(jnp.einsum('bhqk,bhkd->bhqd', w.astype(vb.dtype), vb))
    return jnp.concatenate(outs, axis=2)

def stick_breaking_attention(q, k, v):
    s_len = q.shape[2]
    scale = 1.0 / math.sqrt(q.shape[-1])
    outs = []
    for i in range(s_len // Q_BLOCK):
        k_len = (i + 1) * Q_BLOCK
        qb = q[:, :, i * Q_BLOCK:(i + 1) * Q_BLOCK]
        kb, vb = k[:, :, :k_len], v[:, :, :k_len]
        z = jnp.einsum('bhqd,bhkd->bhqk', qb, kb).astype(jnp.float32) * scale
        q_pos = i * Q_BLOCK + jnp.arange(Q_BLOCK)
        mask = jnp.arange(k_len)[None, :] < q_pos[:, None]
        log_1m = jnp.where(mask, jax.nn.log_sigmoid(-z), 0.0)
        suffix = lax.cumsum(log_1m, axis=3, reverse=True) - log_1m
        a = jnp.where(mask, jnp.exp(jax.nn.log_sigmoid(z) + suffix), 0.0)
        outs.append(jnp.einsum('bhqk,bhkd->bhqd', a.astype(vb.dtype), vb))
    return jnp.concatenate(outs, axis=2)

def first_inputs(seed: int = 0) -> dict:
    key = jax.random.key(seed)
    ks = iter(jax.random.split(key, 32))
    f32 = jnp.float32

    def w(shape, fan_in):
        return jax.random.normal(next(ks), (DEPTH,) + shape, f32) * fan_in ** -0.5

    def gain(n):
        return 1.0 + 0.02 * jax.random.normal(next(ks), (DEPTH, n), f32)

    x = jax.random.normal(next(ks), (BATCH, SEQ, D_MODEL), f32)
    p = jax.random.normal(next(ks), (DEPTH, BATCH, SEQ, PLE_DIM), f32)
    offset = jax.random.randint(next(ks), (BATCH, 1), 0, 1024, dtype=jnp.int32)
    positions = offset + jnp.arange(SEQ, dtype=jnp.int32)[None, :]
    return {
        "x": x,
        "p": p,
        "positions": positions,
        "ffn1_norm": gain(D_MODEL),
        "ffn1_w_in": w((D_MODEL, 2 * D_FF), D_MODEL),
        "ffn1_w_out": w((D_FF, D_MODEL), D_FF),
        "mix_norm": gain(D_MODEL),
        "w_in": w((D_MODEL, IN_COLS), D_MODEL),
        "q_latent_norm": gain(Q_LORA),
        "w_q_up": w((Q_LORA, MLA_HEADS * MLA_QK), Q_LORA),
        "kv_latent_norm": gain(KV_LORA),
        "w_kv_up": w((KV_LORA, MLA_HEADS * (MLA_NOPE + MLA_V)), KV_LORA),
        "q_head_norm": gain(MLA_QK),
        "k_head_norm": gain(MLA_QK),
        "w_branch_mla": w((MLA_WIDTH, D_MODEL), MLA_WIDTH),
        "w_branch_sb": w((SB_WIDTH, D_MODEL), SB_WIDTH),
        "w_out": w((D_MODEL, D_MODEL), D_MODEL),
        "ffn2_norm": gain(D_MODEL),
        "ffn2_w_in": w((D_MODEL, 2 * D_FF), D_MODEL),
        "ffn2_w_out": w((D_FF, D_MODEL), D_FF),
        "ple_norm": gain(D_MODEL),
        "w_ple_gate": w((D_MODEL, D_MODEL), D_MODEL),
        "w_ple_proj": w((PLE_DIM, D_MODEL), PLE_DIM),
    }

def first_block(x, p, positions, ffn1_norm, ffn1_w_in, ffn1_w_out, mix_norm, w_in,
              q_latent_norm, w_q_up, kv_latent_norm, w_kv_up, q_head_norm, k_head_norm,
              w_branch_mla, w_branch_sb, w_out, ffn2_norm, ffn2_w_in, ffn2_w_out,
              ple_norm, w_ple_gate, w_ple_proj):
    b, s, _ = x.shape
    h = x
    for i in range(DEPTH):
        h = h + FFN_RES_WEIGHT * swiglu(rms_norm(h, ffn1_norm[i]), ffn1_w_in[i], ffn1_w_out[i])

        u = rms_norm(h, mix_norm[i])
        proj = u @ w_in[i]
        c_q, c_kv, k_rope, sb_qkv, gates = jnp.split(proj, SPLITS, axis=-1)

        q = (rms_norm(c_q, q_latent_norm[i]) @ w_q_up[i]).reshape(b, s, MLA_HEADS, MLA_QK)
        kv = (rms_norm(c_kv, kv_latent_norm[i]) @ w_kv_up[i]).reshape(b, s, MLA_HEADS, MLA_NOPE + MLA_V)
        k_nope, v_mla = kv[..., :MLA_NOPE], kv[..., MLA_NOPE:]
        k_r = jnp.broadcast_to(k_rope[:, :, None, :], (b, s, MLA_HEADS, MLA_ROPE))
        k = jnp.concatenate([k_nope, k_r], axis=-1)
        q = rms_norm(q, q_head_norm[i])
        k = rms_norm(k, k_head_norm[i])
        q = jnp.concatenate([q[..., :MLA_NOPE], apply_rope(q[..., MLA_NOPE:], positions)], axis=-1)
        k = jnp.concatenate([k[..., :MLA_NOPE], apply_rope(k[..., MLA_NOPE:], positions)], axis=-1)
        o_mla = causal_softmax_attention(q.transpose(0, 2, 1, 3), k.transpose(0, 2, 1, 3),
                                         v_mla.transpose(0, 2, 1, 3))
        o_mla = o_mla.transpose(0, 2, 1, 3).reshape(b, s, MLA_WIDTH)

        sq, sk, sv = [t.reshape(b, s, SB_HEADS, SB_HEAD_DIM).transpose(0, 2, 1, 3)
                      for t in jnp.split(sb_qkv, 3, axis=-1)]
        o_sb = stick_breaking_attention(sq, sk, sv)
        o_sb = o_sb.transpose(0, 2, 1, 3).reshape(b, s, SB_WIDTH)

        g_mla, g_sb = jnp.split(jax.nn.sigmoid(gates), 2, axis=-1)
        merged = g_mla * (o_mla @ w_branch_mla[i]) + g_sb * (o_sb @ w_branch_sb[i])
        h = h + merged @ w_out[i]

        h = h + FFN_RES_WEIGHT * swiglu(rms_norm(h, ffn2_norm[i]), ffn2_w_in[i], ffn2_w_out[i])

        ple_gate = jax.nn.sigmoid(rms_norm(h, ple_norm[i]) @ w_ple_gate[i])
        h = h + ple_gate * (p[i] @ w_ple_proj[i])
    return h


CHUNK = 64
EPS = 1e-6
N_HEADS = 16
N_KV_HEADS = 4
HEAD_DIM = 64
ROPE_DIM = HEAD_DIM // 4
ROPE_THETA = 500000.0
IDX_HEADS = 8
IDX_DIM = 64
TOPK_MAX = 256
SSD_D_INNER = 2 * D_MODEL
SSD_HEAD_DIM = 64
SSD_HEADS = SSD_D_INNER // SSD_HEAD_DIM
SSD_GROUPS = 4
SSD_STATE = 128
SSD_CONV = 4
SSD_XBC = SSD_D_INNER + 2 * SSD_GROUPS * SSD_STATE
N_EXPERT_GROUPS = 4
EXPERTS_PER_GROUP = 8
EXPERT_TOPK = 2
EXPERT_HIDDEN = 256
Q_W = N_HEADS * HEAD_DIM
KV_W = N_KV_HEADS * HEAD_DIM
IQ_W = IDX_HEADS * IDX_DIM
SPLITS_2 = (Q_W, KV_W, KV_W, IQ_W, IDX_DIM, IDX_HEADS, SSD_D_INNER, SSD_XBC, SSD_HEADS, D_MODEL, D_MODEL)
IN_PROJ_W = sum(SPLITS_2)


def rmsnorm(x, g):
    xf = x.astype(jnp.float32)
    y = xf * lax.rsqrt(jnp.mean(xf * xf, axis=-1, keepdims=True) + EPS)
    return (y * g.astype(jnp.float32)).astype(x.dtype)

def rope_partial(x, pos):
    half = ROPE_DIM // 2
    inv = ROPE_THETA ** (-jnp.arange(half, dtype=jnp.float32) * 2.0 / ROPE_DIM)
    ang = pos.astype(jnp.float32)[:, None] * inv[None, :]
    cos = jnp.cos(ang)[:, None, :]
    sin = jnp.sin(ang)[:, None, :]
    xr = x[..., :ROPE_DIM].astype(jnp.float32)
    x1, x2 = xr[..., :half], xr[..., half:]
    rot = jnp.concatenate([x1 * cos - x2 * sin, x2 * cos + x1 * sin], axis=-1)
    return jnp.concatenate([rot.astype(x.dtype), x[..., ROPE_DIM:]], axis=-1)

def dsa_attention(q, k, v, iq, ik, iw):
    Bsz, T = q.shape[0], q.shape[1]
    topk = min(TOPK_MAX, T // 4)
    nblk = T // Q_BLOCK
    grp = N_HEADS // N_KV_HEADS
    key_chunk = jnp.arange(T) // CHUNK
    ikf = ik.astype(jnp.float32)

    def to_blocks(a):
        return a.reshape(Bsz, nblk, Q_BLOCK, *a.shape[2:]).swapaxes(0, 1)

    def one_block(args):
        qb, iqb, iwb, start = args
        q_chunk = (start + jnp.arange(Q_BLOCK)) // CHUNK
        admissible = key_chunk[None, :] <= q_chunk[:, None]
        rel = jax.nn.relu(jnp.einsum('bqhd,bsd->bqhs', iqb.astype(jnp.float32), ikf) * IDX_DIM ** -0.5)
        score = jnp.einsum('bqhs,bqh->bqs', rel, iwb.astype(jnp.float32) * IDX_HEADS ** -0.5)
        score = jnp.where(admissible[None], score, -jnp.inf)
        top_s, sel = lax.top_k(score, topk)
        valid = jnp.isfinite(top_s)
        k_sel = jax.vmap(lambda kk, ii: kk[ii])(k, sel)
        v_sel = jax.vmap(lambda vv, ii: vv[ii])(v, sel)
        qg = qb.reshape(Bsz, Q_BLOCK, N_KV_HEADS, grp, HEAD_DIM).astype(jnp.float32)
        logits = jnp.einsum('bqhgd,bqkhd->bqhgk', qg, k_sel.astype(jnp.float32)) * HEAD_DIM ** -0.5
        logits = jnp.where(valid[:, :, None, None, :], logits, -jnp.inf)
        p = jax.nn.softmax(logits, axis=-1)
        o = jnp.einsum('bqhgk,bqkhd->bqhgd', p, v_sel.astype(jnp.float32))
        return o.reshape(Bsz, Q_BLOCK, N_HEADS * HEAD_DIM).astype(q.dtype)

    starts = jnp.arange(nblk, dtype=jnp.int32) * Q_BLOCK
    out = lax.map(one_block, (to_blocks(q), to_blocks(iq), to_blocks(iw), starts))
    return out.swapaxes(0, 1).reshape(Bsz, T, N_HEADS * HEAD_DIM)

def causal_depthwise_conv(x, w, b):
    y = lax.conv_general_dilated(x, w[:, None, :], window_strides=(1,),
                                 padding=[(w.shape[0] - 1, 0)],
                                 dimension_numbers=('NWC', 'WIO', 'NWC'),
                                 feature_group_count=x.shape[-1])
    return y + b

def ssd_chunked(xh, dt, A, Bm, Cm):
    Bsz, T, H, P = xh.shape
    nc = T // CHUNK
    R = H // SSD_GROUPS
    x = (xh * dt[..., None]).reshape(Bsz, nc, CHUNK, SSD_GROUPS, R, P)
    a_cs = jnp.cumsum((dt * A).reshape(Bsz, nc, CHUNK, SSD_GROUPS, R), axis=2)
    Bc = Bm.reshape(Bsz, nc, CHUNK, SSD_GROUPS, SSD_STATE)
    Cc = Cm.reshape(Bsz, nc, CHUNK, SSD_GROUPS, SSD_STATE)
    seg = a_cs[:, :, :, None] - a_cs[:, :, None, :]
    causal = jnp.tril(jnp.ones((CHUNK, CHUNK), dtype=bool))[None, None, :, :, None, None]
    decay = jnp.exp(jnp.where(causal, seg, -jnp.inf))
    cb = jnp.einsum('bclgn,bcsgn->bclsg', Cc, Bc)
    y_diag = jnp.einsum('bclsg,bclsgr,bcsgrp->bclgrp', cb, decay, x)
    decay_to_end = jnp.exp(a_cs[:, :, -1:] - a_cs)
    states = jnp.einsum('bclgn,bclgr,bclgrp->bcgrpn', Bc, decay_to_end, x)
    chunk_decay = jnp.exp(a_cs[:, :, -1])

    def step(h, inp):
        dec, st = inp
        return dec[..., None, None] * h + st, h

    h0 = jnp.zeros((Bsz, SSD_GROUPS, R, P, SSD_STATE), jnp.float32)
    _, prev = lax.scan(step, h0, (chunk_decay.swapaxes(0, 1), states.swapaxes(0, 1)))
    prev = prev.swapaxes(0, 1)
    y_off = jnp.einsum('bclgn,bcgrpn,bclgr->bclgrp', Cc, prev, jnp.exp(a_cs))
    return (y_diag + y_off).reshape(Bsz, T, H, P)

def gated_group_rmsnorm(y, z, g):
    yf = y.astype(jnp.float32) * jax.nn.silu(z.astype(jnp.float32))
    yg = yf.reshape(*yf.shape[:-1], SSD_GROUPS, -1)
    yg = yg * lax.rsqrt(jnp.mean(yg * yg, axis=-1, keepdims=True) + EPS)
    return yg.reshape(yf.shape) * g.astype(jnp.float32)

def hier_moe(h, w_rg, b_rg, w_re, b_re, w_gate, w_up, w_down):
    Bsz, T, D = h.shape
    hf = h.reshape(-1, D)
    g_logits = (hf @ w_rg + b_rg).astype(jnp.float32)
    g_prob = jax.nn.softmax(g_logits, axis=-1)
    g_idx = jnp.argmax(g_logits, axis=-1)
    g_w = jnp.take_along_axis(g_prob, g_idx[:, None], axis=-1)
    e_logits = (hf @ w_re + b_re).astype(jnp.float32).reshape(-1, N_EXPERT_GROUPS, EXPERTS_PER_GROUP)
    e_in = jnp.take_along_axis(e_logits, g_idx[:, None, None], axis=1)[:, 0]
    top_v, top_i = lax.top_k(e_in, EXPERT_TOPK)
    top_p = jax.nn.softmax(top_v, axis=-1)
    within = jnp.sum(jax.nn.one_hot(top_i, EXPERTS_PER_GROUP, dtype=jnp.float32) * top_p[..., None], axis=1)
    combine = jax.nn.one_hot(g_idx, N_EXPERT_GROUPS, dtype=jnp.float32)[:, :, None] * (g_w * within)[:, None, :]
    combine = combine.astype(hf.dtype)
    out = jnp.zeros_like(hf)
    for g in range(N_EXPERT_GROUPS):
        a = jnp.einsum('nd,edf->nef', hf, w_gate[g])
        u = jnp.einsum('nd,edf->nef', hf, w_up[g])
        act = jax.nn.silu(a) * u * combine[:, g, :, None]
        out = out + jnp.einsum('nef,efd->nd', act, w_down[g])
    return out.reshape(Bsz, T, D)

def second_inputs(seed: int = 0) -> dict:
    key = jax.random.key(seed)
    ks = jax.random.split(key, 24)
    L = DEPTH
    f32 = jnp.float32

    def nrm(k, shape, scale):
        return jax.random.normal(k, shape, f32) * scale

    def gain(k, n):
        return 1.0 + 0.02 * jax.random.normal(k, (L, n), f32)

    dt0 = jnp.exp(jax.random.uniform(ks[8], (L, SSD_HEADS), f32, math.log(1e-3), math.log(1e-1)))
    return {
        "x": nrm(ks[0], (BATCH, SEQ, D_MODEL), 1.0),
        "attn_norm": gain(ks[1], D_MODEL),
        "w_in": nrm(ks[2], (L, D_MODEL, IN_PROJ_W), D_MODEL ** -0.5),
        "q_norm": gain(ks[3], HEAD_DIM),
        "k_norm": gain(ks[4], HEAD_DIM),
        "idx_k_norm": gain(ks[5], IDX_DIM),
        "conv_w": nrm(ks[6], (L, SSD_CONV, SSD_XBC), SSD_CONV ** -0.5),
        "conv_b": nrm(ks[7], (L, SSD_XBC), 0.02),
        "dt_bias": dt0 + jnp.log(-jnp.expm1(-dt0)),
        "a_log": jnp.log(jax.random.uniform(ks[9], (L, SSD_HEADS), f32, 1.0, 16.0)),
        "d_skip": 1.0 + 0.1 * jax.random.normal(ks[10], (L, SSD_HEADS), f32),
        "ssd_norm": gain(ks[11], SSD_D_INNER),
        "w_attn_branch": nrm(ks[12], (L, Q_W, D_MODEL), Q_W ** -0.5),
        "w_ssd_branch": nrm(ks[13], (L, SSD_D_INNER, D_MODEL), SSD_D_INNER ** -0.5),
        "w_out": nrm(ks[14], (L, D_MODEL, D_MODEL), D_MODEL ** -0.5),
        "ffn_norm": gain(ks[15], D_MODEL),
        "w_route_group": nrm(ks[16], (L, D_MODEL, N_EXPERT_GROUPS), D_MODEL ** -0.5),
        "b_route_group": nrm(ks[17], (L, N_EXPERT_GROUPS), 0.01),
        "w_route_expert": nrm(ks[18], (L, D_MODEL, N_EXPERT_GROUPS * EXPERTS_PER_GROUP), D_MODEL ** -0.5),
        "b_route_expert": nrm(ks[19], (L, N_EXPERT_GROUPS * EXPERTS_PER_GROUP), 0.01),
        "w_gate": nrm(ks[20], (L, N_EXPERT_GROUPS, EXPERTS_PER_GROUP, D_MODEL, EXPERT_HIDDEN), D_MODEL ** -0.5),
        "w_up": nrm(ks[21], (L, N_EXPERT_GROUPS, EXPERTS_PER_GROUP, D_MODEL, EXPERT_HIDDEN), D_MODEL ** -0.5),
        "w_down": nrm(ks[22], (L, N_EXPERT_GROUPS, EXPERTS_PER_GROUP, EXPERT_HIDDEN, D_MODEL), EXPERT_HIDDEN ** -0.5),
    }

def second_block(x, attn_norm, w_in, q_norm, k_norm, idx_k_norm, conv_w, conv_b, dt_bias, a_log, d_skip,
              ssd_norm, w_attn_branch, w_ssd_branch, w_out, ffn_norm, w_route_group, b_route_group,
              w_route_expert, b_route_expert, w_gate, w_up, w_down):
    Bsz, T, _ = x.shape
    pos = jnp.arange(T)
    offs = np.cumsum(SPLITS_2)[:-1].tolist()
    for l in range(DEPTH):
        h = rmsnorm(x, attn_norm[l])
        proj = h @ w_in[l]
        (q, k, v, iq, ik, iw, z, xbc, dt_raw, gate_a, gate_b) = jnp.split(proj, offs, axis=-1)
        q = rope_partial(rmsnorm(q.reshape(Bsz, T, N_HEADS, HEAD_DIM), q_norm[l]), pos)
        k = rope_partial(rmsnorm(k.reshape(Bsz, T, N_KV_HEADS, HEAD_DIM), k_norm[l]), pos)
        v = v.reshape(Bsz, T, N_KV_HEADS, HEAD_DIM)
        iq = rope_partial(iq.reshape(Bsz, T, IDX_HEADS, IDX_DIM), pos)
        ik = rope_partial(rmsnorm(ik, idx_k_norm[l])[:, :, None, :], pos)[:, :, 0, :]
        y_attn = dsa_attention(q, k, v, iq, ik, iw)
        xbc = jax.nn.silu(causal_depthwise_conv(xbc, conv_w[l], conv_b[l]))
        xs, bs, cs = jnp.split(xbc, [SSD_D_INNER, SSD_D_INNER + SSD_GROUPS * SSD_STATE], axis=-1)
        xh = xs.reshape(Bsz, T, SSD_HEADS, SSD_HEAD_DIM).astype(jnp.float32)
        dt = jax.nn.softplus(dt_raw.astype(jnp.float32) + dt_bias[l].astype(jnp.float32))
        A = -jnp.exp(a_log[l].astype(jnp.float32))
        y_ssd = ssd_chunked(xh, dt, A,
                            bs.reshape(Bsz, T, SSD_GROUPS, SSD_STATE).astype(jnp.float32),
                            cs.reshape(Bsz, T, SSD_GROUPS, SSD_STATE).astype(jnp.float32))
        y_ssd = y_ssd + d_skip[l].astype(jnp.float32)[:, None] * xh
        y_ssd = gated_group_rmsnorm(y_ssd.reshape(Bsz, T, SSD_D_INNER), z, ssd_norm[l]).astype(x.dtype)
        merged = jax.nn.sigmoid(gate_a) * (y_attn @ w_attn_branch[l]) + jax.nn.sigmoid(gate_b) * (y_ssd @ w_ssd_branch[l])
        x = x + merged @ w_out[l]
        x = x + hier_moe(rmsnorm(x, ffn_norm[l]), w_route_group[l], b_route_group[l], w_route_expert[l],
                         b_route_expert[l], w_gate[l], w_up[l], w_down[l])
    return x


def setup_inputs(seed=0):
    out = dict(first_inputs(seed))
    for name, value in second_inputs(seed + 1).items():
        if name != "x":
            out[name + "_2"] = value
    return out


def reference(
    x, p, positions, ffn1_norm, ffn1_w_in, ffn1_w_out, mix_norm, w_in, q_latent_norm, w_q_up,
    kv_latent_norm, w_kv_up, q_head_norm, k_head_norm, w_branch_mla, w_branch_sb, w_out,
    ffn2_norm, ffn2_w_in, ffn2_w_out, ple_norm, w_ple_gate, w_ple_proj, attn_norm_2, w_in_2,
    q_norm_2, k_norm_2, idx_k_norm_2, conv_w_2, conv_b_2, dt_bias_2, a_log_2, d_skip_2,
    ssd_norm_2, w_attn_branch_2, w_ssd_branch_2, w_out_2, ffn_norm_2, w_route_group_2,
    b_route_group_2, w_route_expert_2, b_route_expert_2, w_gate_2, w_up_2, w_down_2,
):
    x = first_block(
        x, p, positions, ffn1_norm, ffn1_w_in, ffn1_w_out, mix_norm, w_in, q_latent_norm,
        w_q_up, kv_latent_norm, w_kv_up, q_head_norm, k_head_norm, w_branch_mla, w_branch_sb,
        w_out, ffn2_norm, ffn2_w_in, ffn2_w_out, ple_norm, w_ple_gate, w_ple_proj,
    )
    return second_block(
        x, attn_norm_2, w_in_2, q_norm_2, k_norm_2, idx_k_norm_2, conv_w_2, conv_b_2, dt_bias_2,
        a_log_2, d_skip_2, ssd_norm_2, w_attn_branch_2, w_ssd_branch_2, w_out_2, ffn_norm_2,
        w_route_group_2, b_route_group_2, w_route_expert_2, b_route_expert_2, w_gate_2, w_up_2,
        w_down_2,
    )


_drawn_inputs = setup_inputs


def setup_inputs(seed=0):
    import zlib

    import numpy as np

    out = dict(_drawn_inputs(seed))
    spreads = {}
    factors = {'ffn1_norm': 2.852,
     'mix_norm': 2.894,
     'q_latent_norm': 5.7,
     'kv_latent_norm': 4.305,
     'q_head_norm': 6.384,
     'k_head_norm': 5.091,
     'ffn2_norm': 3.634,
     'ple_norm': 45.32,
     'q_norm_2': 41.453,
     'k_norm_2': 45.699,
     'idx_k_norm_2': 15.123,
     'conv_b_2': 3.037,
     'ssd_norm_2': 26.608,
     'b_route_group_2': 31.72,
     'b_route_expert_2': 32.536,
     'd_skip_2': 2.889,
     'ffn_norm_2': 8.0}
    for name, (base, spread) in spreads.items():
        noise = np.random.default_rng([zlib.crc32(name.encode()), seed]).standard_normal(out[name].shape)
        drawn = base * np.exp(spread * noise) if base else spread * noise
        out[name] = __import__('jax').numpy.asarray(drawn.astype(out[name].dtype))
    for name, factor in factors.items():
        out[name] = (out[name] * factor).astype(out[name].dtype)
    return out
```

```python
from contextlib import ExitStack

import numpy as np

import concourse.bass as bass
from concourse import mybir

ALU = mybir.AluOpType
ACT = mybir.ActivationFunctionType
F32 = mybir.dt.float32
F32R = mybir.dt.float32r
I32 = mybir.dt.int32
AX = mybir.AxisListType.X

P = 128
T = 256
NT = T // P
D = 1024
KD = D // P
FF = 2816
NF = FF // 256
PLE = 256
QL, KVL, ROPE = 384, 256, 32
MH, NOPE, QK = 8, 64, 96
SBW = 512
H2, KVH2, HD = 16, 4, 64
IH = 8
TOPK = 64
KCHUNK = 64
DI, SH, SP, SG, SN = 2048, 32, 64, 4, 128
NX = (DI + 2 * SG * SN) // P
TAPS = 4
NE, EG, EPG, EH = 32, 4, 8, 256
EPS = 1e-6
LOW = -1e30
TAKEN = -3e38

C1_SQ = QL + KVL + ROPE
C1_GATE = C1_SQ + 3 * SBW
C2_K = H2 * HD
C2_V = C2_K + KVH2 * HD
C2_IQ = C2_V + KVH2 * HD
C2_IK = C2_IQ + IH * HD
C2_Z = C2_IK + HD + IH
C2_XBC = C2_Z + DI
C2_DT = C2_XBC + NX * P
C2_GA = C2_DT + SH
C2_GB = C2_GA + D

NSLOT = 3
SLAB = 2048

CONST_AT = {}


def constants():
    j, i = np.arange(P)[:, None], np.arange(P)[None, :]
    wide = lambda a: np.broadcast_to(np.asarray(a, np.float64), (P, np.size(a)))
    ones, zeros = np.ones((P, P)), np.zeros((P, P))
    s = np.arange(T)[None, :]
    half = HD // 4 // 2
    inv2 = 500000.0 ** (-np.arange(half) * 2.0 / (2 * half))
    ang2 = [(np.float32(t * P + np.arange(P))[:, None] * inv2.astype(np.float32)[None, :]).astype(np.float64) for t in range(NT)]
    parts = [
        ("ident", np.eye(P)),
        ("upto", (j <= i) * 1.0),
        ("neg_from", (j >= i) * -1.0),
        ("neg_ones", -ones),
        ("ones", ones),
        ("causal", np.hstack([(i > j) * LOW, zeros, (i > j) * LOW])),
        ("earlier", np.hstack([(j < i) * 1.0, ones, (j < i) * 1.0])),
        ("earlier_bias", np.hstack([(j >= i) * LOW, zeros, (j >= i) * LOW])),
        ("admit", np.hstack([(s[:, :P] // KCHUNK > j // KCHUNK) * LOW, (s // KCHUNK > (j + P) // KCHUNK) * LOW])),
        ("invf", wide(10000.0 ** (-np.arange(0, ROPE, 2) / ROPE))),
        ("cos2", np.hstack([np.cos(a) for a in ang2])),
        ("sin2", np.hstack([np.sin(a) for a in ang2])),
        ("before", wide((np.arange(EPG)[None, :] < np.arange(EPG)[:, None]).ravel())),
    ]
    at = 0
    for name, a in parts:
        CONST_AT[name] = (at, a.shape[1])
        at += a.shape[1]
    return np.hstack([a for _, a in parts]).astype(np.float32)


NCONST = constants().shape[1]


def two_blocks(nc, a, out, scratch):
    with ExitStack() as ctx:
        def sb(name, shape, dt=F32, scope=ctx):
            return scope.enter_context(nc.sbuf_tensor("sb_" + name, shape, dt))

        bank = [ctx.enter_context(nc.psum_tensor(f"bank{i}", [P, 512], F32)) for i in range(8)]

        sems = {}

        norms = ("n1", "n2", "n3", "n4", "n5", "n6")
        ffns = (("ffn1", NF), ("ffn2", NF), ("moe", NE))
        heads = ("hq", "hk", "ik", "k2", "q2")
        turned = ("hq", "hk", "iq", "ik", "k2", "q2")
        attn = (("mla", MH), ("dsa", H2))
        shared = [[("norm_" + k, [(nm + "_" + k, c) for nm in norms]) for k, c in
                   (("ss", NT), ("tr", KD // 2), ("hi", KD), ("r", 1), ("xn", NT), ("lo", KD))],
                  [("ffn_" + k, [(nm + "_" + k, n) for nm, n in ffns]) for k in ("silu", "mul", "h", "hh")],
                  [("ffn_x", [(nm + "_x", 4) for nm, _ in ffns])],
                  [("head_" + k, [(nm + "_" + k, c) for nm in heads]) for k, c in (("sq", NT), ("red", NT), ("r", 1), ("scaled", 2))],
                  [("head_turn", [(nm + "_turn", 6) for nm in turned])],
                  [("attn_" + k, [(nm + "_" + k, c * n // 2) for nm, n in attn]) for k, c in
                   (("s", 2), ("mx", 4), ("nm", 2), ("exp", 4), ("rs", 2), ("pn", 4), ("pt", 2), ("ptc", 2), ("av", 2),
                    ("ohi", 1), ("olo", 1))],
                  [("merge_" + k, [("mg_" + k, 4), ("m2_" + k, 4)]) for k in ("a", "b", "s", "hi", "lo")],
                  [("gate_sig", [("gsig", 4), ("g2sig", 4)]),
                   ("q_tr", [("qt_tr", 4), ("qt2_tr", 4)]), ("q_out", [("qt_ev", 4), ("qt2_ev", 4)]),
                   ("k_tr", [("kt_tr", 4), ("kt2_tr", 2)]), ("k_out", [("kt_ev", 4), ("kt2_ev", 2)]),
                   ("resid", [("x2", 4), ("x4", 4), ("x5", 4)]),
                   ("act_out", [("lat_ev", 3), ("sqk_ev", 4), ("sv_ev", 2), ("q_ev", 4), ("kv_ev", 8), ("gate_ev", 8),
                                ("pp_ev", 4), ("b2_ev", 10)]),
                   ("scores", [("sb_z", 8), ("seg_mm", 16)]), ("logs", [("sb_sp", 8), ("seg", 16)]),
                   ("expo", [("sb_a", 8), ("seg_e", 16)]), ("masked", [("sb_m", 8), ("seg_m", 16)]),
                   ("values", [("sb_av", 8), ("y_mm", 8)]),
                   ("tr", [("lt_tr", 3), ("xs_tr", 8), ("yt_tr", 8)]),
                   ("t_hi", [("lt_hi", 5), ("yt_hi", 16)]), ("t_lo", [("lt_lo", 5), ("yt_lo", 16)])]]
        place = {}
        for sem, stages in sum(shared, []):
            base = 0
            for nm, c in stages:
                place[nm] = sem, base
                base += c

        def S(name):
            sem = place.get(name, (name, 0))[0]
            if sem not in sems:
                sems[sem] = ctx.enter_context(nc.semaphore(sem))
            return sems[sem]

        def reach(name, count):
            base = place.get(name, (name, 0))[1]
            return S(name), count + base if base else count

        raw = sb("raw", [P, NSLOT, SLAB])
        whi = sb("whi", [P, NSLOT, SLAB], F32R)
        wlo = sb("wlo", [P, NSLOT, SLAB], F32R)
        X = sb("X", [P, NT, D])
        Uh = sb("Uh", [P, KD, T], F32R)
        Ul = sb("Ul", [P, KD, T], F32R)
        xn = sb("xn", [P, NT, D])
        C = sb("C", [P, NCONST])
        G = sb("G", [P, 256])
        PB = sb("PB", [P, 520])
        st = sb("st", [P, 320])
        sgh = sb("sgh", [P, 2, 512])
        hh = sb("hh", [P, 512], F32R)
        hl = sb("hl", [P, 512], F32R)
        zero = sb("zero", [P, 512], F32R)
        aw = sb("aw", [P, 6, 384])
        rows1, rows2 = sgh[:, 0, 0:P], sgh[:, 0, P:2 * P]
        pos = sb("pos", [P, NT], I32)
        rope1 = sb("rope1", [P, 8, NT, ROPE // 2])
        COS1, SIN1 = rope1[:, 6], rope1[:, 7]

        def const(name, lo=0, hi=None):
            at, n = CONST_AT[name]
            return C[:, at + lo:at + (n if hi is None else hi)]

        ident = const("ident")

        stat_at = {}

        def stat(name, n):
            if name not in stat_at:
                stat_at[name] = sum(v[1] for v in stat_at.values())
                stat_at[name] = (stat_at[name], n)
            at, _ = stat_at[name]
            assert at + n <= 320
            return st[:, at:at + n]

        gain_rows = [("ffn1_norm", KD), ("mix_norm", KD), ("q_latent_norm", QL // P), ("kv_latent_norm", KVL // P),
                     ("ffn2_norm", KD), ("ple_norm", KD), ("attn_norm_2", KD), ("ffn_norm_2", KD),
                     ("ssd_norm_2", DI // P), ("conv_b_2", NX)]
        gain_at, at = {}, 0
        for name, n in gain_rows:
            gain_at[name] = at
            at += n
        n_rows1 = at
        gain_at["conv_w_2"] = P
        n_rows2 = TAPS * NX

        def gcol(name, i):
            return G[:, gain_at[name] + i:gain_at[name] + i + 1]

        pb_list = [("q_head_norm", QK), ("k_head_norm", QK), ("q_norm_2", HD), ("k_norm_2", HD), ("idx_k_norm_2", HD),
                   ("dt_bias_2", SH), ("a_log_2", SH), ("d_skip_2", SH), ("b_route_group_2", EG), ("b_route_expert_2", NE)]
        pb_at, at = {}, 0
        for name, n in pb_list:
            pb_at[name] = (at, n)
            at += n

        def pb(name):
            at, n = pb_at[name]
            return PB[:, at:at + n]

        with ExitStack() as p1:
            with ExitStack() as pa:
                CQ = sb("CQ", [P, NT, C1_SQ], F32, pa)
                Lh = sb("Lh", [P, 5, T], F32R, pa)
                Ll = sb("Ll", [P, 5, T], F32R, pa)
            GT = sb("GT", [P, 16, T], F32, p1)
            sqT = sb("sqT", [P, 4, T], F32, p1)
            skT = sb("skT", [P, 4, T], F32, p1)
            sv = sb("sv", [P, NT, SBW], F32, p1)
            K1 = sb("K1", [P, NT, MH, QK], F32, p1)
            V1 = sb("V1", [P, NT, MH, 64], F32, p1)
            QT1 = sb("QT1", [QK, MH, T], F32, p1)
            KT1 = sb("KT1", [QK, MH, T], F32, p1)
            OMh = sb("OMh", [P, 4, T], F32R, p1)
            OMl = sb("OMl", [P, 4, T], F32R, p1)
            OSh = sb("OSh", [P, 4, T], F32R, p1)
            OSl = sb("OSl", [P, 4, T], F32R, p1)
        with ExitStack() as p2:
            with ExitStack() as pa:
                OAh = sb("OAh", [P, 8, T], F32R, pa)
                OAl = sb("OAl", [P, 8, T], F32R, pa)
            G2 = sb("G2", [P, 16, T], F32, p2)
            ssm = sb("ssm", [P, 10, SH], F32, p2)
            with ExitStack() as pa:
                QT2 = sb("QT2", [P, H2 // 2, T], F32, pa)
                KT2 = sb("KT2", [P, KVH2, T], F32, pa)
                IQT = sb("IQT", [P, IH // 2, T], F32, pa)
                IKT = sb("IKT", [P, T], F32, pa)
                V2 = sb("V2", [P, NT, KVH2 * HD], F32, pa)
                SELB = sb("SELB", [P, 384], F32, pa)
            XS = sb("XS", [P, NT, DI], F32, p2)
            CBM = sb("CBM", [P, NT, SG, P], F32, p2)
            pad = sb("pad", [P, P], F32, p2)
            with ExitStack() as pa:
                IQ = sb("IQ", [P, NT, IH, HD], F32, pa)
                K2 = sb("K2", [P, NT, KVH2, HD], F32, pa)
                K2d = sb("K2d", [P, NT, KVH2, 2, HD], F32, pa)
                IKd = sb("IKd", [P, NT, 2, HD], F32, pa)
                IKW = sb("IKW", [P, NT, HD + IH], F32, pa)
            with ExitStack() as pa:
                XC = sb("XC", [P, NX, T], F32, pa)
            with ExitStack() as pa:
                ST = sb("ST", [P, SG, 512], F32, pa)
                Xd = sb("Xd", [P, 2, 512], F32, pa)
                Xe = sb("Xe", [P, 512], F32, pa)
                BTM = sb("BTM", [P, SG, SN], F32, pa)
            with ExitStack() as pa:
                YTh = sb("YTh", [P, DI // P, T], F32R, pa)
                YTl = sb("YTl", [P, DI // P, T], F32R, pa)
            COMB = sb("COMB", [P, NE, T], F32, p2)
        COMBW = aw[:, 0:2].rearrange("p a n -> p (a n)")[:, 0:512]
        Q2 = xn[:, :, :].rearrange("p t (h d) -> p t h d", d=HD)
        BA = xn[:, :, :].rearrange("p t (c n) -> p (t c) n", n=T)
        SCO = aw[:, 5]
        CT = sgh[0:NE, 1, 0:T]
        PP = GT[:, 0:8].rearrange("p (t a) n -> p t (a n)", t=NT)
        Q1 = xn[:, :, 0:MH * QK].rearrange("p t (h d) -> p t h d", d=QK)

        def view(name):
            w = a[name]
            return w[0].rearrange("(k p) n -> p k n", p=P)

        slab_of, slabs, loops = {}, [], {}

        def slab(name, src, kc, ncol):
            slab_of[name] = len(slabs)
            slabs.append((src, kc, ncol))

        def slab_loop(name, n, gate, up, down):
            slab_of[name] = len(slabs)
            loops[len(slabs)] = (n, gate, up, down)
            slabs.extend([(None, KD, 256)] * (3 * n))

        def ffn_loop(name, w_in, w_out):
            wi = a[w_in][0].rearrange("(k p) (h c n) -> h c p k n", p=P, h=2, n=256)
            wo = a[w_out][0].rearrange("(c k p) n -> c p k n", p=P, k=2)
            slab_loop(name, NF, lambda i: wi[0, i], lambda i: wi[1, i], lambda i: wo[i])

        ffn_loop("ffn1", "ffn1_w_in", "ffn1_w_out")
        w = view("w_in")
        for i, (lo, hi) in enumerate([(0, 256), (256, 512), (512, C1_SQ)]):
            slab(f"lat{i}", w[:, :, lo:hi], KD, hi - lo)
        for j, nm in enumerate(("sq", "sk", "sv")):
            for i in range(2):
                lo = C1_SQ + j * SBW + i * 256
                slab(f"{nm}{i}", w[:, :, lo:lo + 256], KD, 256)
        for i in range(2):
            slab(f"qup{i}", view("w_q_up")[:, :, i * 384:(i + 1) * 384], 3, 384)
        slab("kvup", view("w_kv_up"), 2, 1024)
        for i in range(8):
            slab(f"gate{i}", w[:, :, C1_GATE + i * 256:C1_GATE + (i + 1) * 256], KD, 256)
        for i in range(2):
            for nm, src in (("mla", "w_branch_mla"), ("sbr", "w_branch_sb")):
                slab(f"{nm}{i}", view(src)[:, :, i * 512:(i + 1) * 512], 4, 512)
        for i in range(4):
            slab(f"wout{i}", view("w_out")[:, :, i * 256:(i + 1) * 256], KD, 256)
        ffn_loop("ffn2", "ffn2_w_in", "ffn2_w_out")
        slab("pproj", view("w_ple_proj"), 2, 1024)
        for i in range(4):
            slab(f"pgate{i}", view("w_ple_gate")[:, :, i * 256:(i + 1) * 256], KD, 256)

        w2 = view("w_in_2")
        for i in range(4):
            slab(f"q{i}", w2[:, :, i * 256:(i + 1) * 256], KD, 256)
        for nm, lo, hi in (("k", C2_K, C2_V), ("v", C2_V, C2_IQ), ("iq0", C2_IQ, C2_IQ + 256), ("iq1", C2_IQ + 256, C2_IK),
                           ("ik", C2_IK, C2_Z), ("dt", C2_DT, C2_GA)):
            slab(nm, w2[:, :, lo:hi], KD, hi - lo)
        for i in range(NX // 2):
            slab(f"xbc{i}", w2[:, :, C2_XBC + i * 256:C2_XBC + (i + 1) * 256], KD, 256)
        for i in range(4):
            slab(f"wa{i}", view("w_attn_branch_2")[:, :, i * 256:(i + 1) * 256], KD, 256)
        for i in range(4):
            slab(f"g{i}", w2[:, :, C2_GA + i * 256:C2_GA + (i + 1) * 256], KD, 256)
        for i in range(8):
            slab(f"z{i}", w2[:, :, C2_Z + i * 256:C2_Z + (i + 1) * 256], KD, 256)
        for i in range(4, 8):
            slab(f"g{i}", w2[:, :, C2_GA + i * 256:C2_GA + (i + 1) * 256], KD, 256)
        for i in range(4):
            for k in range(2):
                slab(f"ws{i}{k}", view("w_ssd_branch_2")[:, KD * k:KD * (k + 1), i * 256:(i + 1) * 256], KD, 256)
        for i in range(4):
            slab(f"wo{i}", view("w_out_2")[:, :, i * 256:(i + 1) * 256], KD, 256)
        slab("rg", view("w_route_group_2"), KD, EG)
        slab("re", view("w_route_expert_2"), KD, NE)
        experts = lambda nm, k: a[nm].rearrange("o g e (k p) n -> (o g e) p k n", p=P)
        wg, wu, wd = (experts(nm, 0) for nm in ("w_gate_2", "w_up_2", "w_down_2"))
        slab_loop("moe", NE, lambda e: wg[e], lambda e: wu[e], lambda e: wd[e])

        def slab_cols(i):
            return slabs[i][1] * slabs[i][2] if i not in range_of_loops else SLAB

        range_of_loops = {j for b, l in loops.items() for j in range(b, b + 3 * l[0])}

        def load(sp, i, q=None, src=None):
            kc, ncol = (src.shape[1], src.shape[2]) if src is not None else slabs[i][1:]
            src = slabs[i][0] if src is None else src
            if i >= NSLOT or q is not None:
                sp.wait_ge(*reach("lo_done", i - NSLOT + 1 + (0 if q is None else q * 3)))
            dst = raw[:, i % NSLOT, 0:kc * ncol].rearrange("p (k n) -> p k n", n=ncol)
            sp.dma_start(dst, src).then_inc(S(f"raw_full{i % NSLOT}"), 16)

        def split_hi(i, q=None):
            n = slab_cols(i)
            off = 0 if q is None else q
            nc.scalar.wait_ge(*reach(f"raw_full{i % NSLOT}", 16 * (i // NSLOT + 1) + 16 * off))
            if i >= NSLOT or q is not None:
                nc.scalar.wait_ge(*reach("slab_used", i - NSLOT + 1 + 3 * off))
            nc.scalar.activation(whi[:, i % NSLOT, 0:n], raw[:, i % NSLOT, 0:n], ACT.Copy).then_inc(S("hi_done"), 1)

        def split_lo(i, q=None):
            n = slab_cols(i)
            off = 0 if q is None else q
            nc.vector.wait_ge(*reach("hi_done", i + 1 + 3 * off))
            nc.vector.tensor_tensor(wlo[:, i % NSLOT, 0:n], raw[:, i % NSLOT, 0:n], whi[:, i % NSLOT, 0:n].bitcast(F32),
                                    ALU.subtract).then_inc(S("lo_done"), 1)

        nxt = {"hi": 0, "lo": 0}

        def hi_upto(name, k=0):
            n = min((slab_of[name] if isinstance(name, str) else name) + k + NSLOT, len(slabs))
            while nxt["hi"] < n:
                split_hi(nxt["hi"])
                nxt["hi"] += 1

        def lo_upto(name, k=0):
            n = min((slab_of[name] if isinstance(name, str) else name) + k + NSLOT, len(slabs))
            while nxt["lo"] < n:
                split_lo(nxt["lo"])
                nxt["lo"] += 1

        def used(eng, name, k=0):
            eng.wait_ge(*reach("slab_used", slab_of[name] + k + 1))

        pe, act, dve, pool = nc.tensor, nc.scalar, nc.vector, nc.gpsimd
        owner = [None] * 8

        def claim(b, sem, count):
            if owner[b] is not None:
                pe.wait_ge(*reach(owner[b][0], owner[b][1]))
            owner[b] = (sem, count)

        def mm3(o, lh, ll, rh, rl, start, stop):
            pe.matmul(o, lh, rh, start=start, stop=False, skip_group_check=True)
            pe.matmul(o, lh, rl, start=False, stop=False, skip_group_check=True)
            return pe.matmul(o, ll, rh, start=False, stop=stop, skip_group_check=True)

        def wslab(i, kc, ncol):
            sl = i % NSLOT
            v = lambda w: w[:, sl, 0:kc * ncol].rearrange("p (k n) -> p k n", n=ncol)
            return v(whi), v(wlo)

        def by_feature(i, b, xh, xl, kc, ncol, k0=0, n0=0, n1=None, start=True, stop=True):
            wh, wl = wslab(i, kc, ncol)
            n1 = ncol // P if n1 is None else n1
            for n in range(n0, n1):
                o = bank[b][:, (n - n0) * T:(n - n0 + 1) * T]
                f = slice(n * P, (n + 1) * P)
                for k in range(kc):
                    last = mm3(o, wh[:, k, f], wl[:, k, f], xh[:, k0 + k], xl[:, k0 + k],
                               start and n == n0 and k == 0, stop and k == kc - 1)
            return last

        def by_token(i, b, xh, xl, kc, ncol, k0=0, c0=0, c1=None, tiles=range(NT), step=256, start=True):
            wh, wl = wslab(i, kc, ncol)
            c1 = ncol if c1 is None else c1
            for n, t in enumerate(tiles):
                o = bank[b][:, n * step:n * step + c1 - c0]
                tk = slice(t * P, (t + 1) * P)
                for k in range(kc):
                    last = mm3(o, xh[:, k0 + k, tk], xl[:, k0 + k, tk], wh[:, k, c0:c1], wl[:, k, c0:c1],
                               start and n == 0 and k == 0, k == kc - 1)
            return last

        def need(name):
            pe.wait_ge(*reach("lo_done", slab_of[name] + 1))
            return slab_of[name]

        def act_norm(nm, ready, gain):
            act.wait_ge(*reach(ready[0], ready[1]))
            for t in range(NT):
                act.activation(xn[:, t], X[:, t], ACT.Square, accum_out=stat("norm", 4)[:, t:t + 1]).then_inc(S(nm + "_ss"), 1)
            for j in range(KD // 2):
                act.wait_ge(*reach(nm + "_tr", j + 1))
                for c in range(2):
                    act.activation(Uh[:, 2 * j + c], bank[4 + j][:, c * T:(c + 1) * T], ACT.Copy,
                                   scale=gcol(gain, 2 * j + c)).then_inc(S(nm + "_hi"), 1)

        def pool_rsqrt(r, ss, n, done):
            pool.tensor_scalar(ss, ss, 1.0 / n, EPS, ALU.mult, ALU.add).then_inc(S("pool_chain"), 1)
            pool_chain[0] += 1
            pool.wait_ge(*reach("pool_chain", pool_chain[0]))
            w = ss.shape[1]
            pool.tensor_tensor(r, ss, halves[:, 0:w], ALU.pow).then_inc(S(done), 1)

        pool_chain = [0]
        halves = stat("halves", 32)

        def pool_norm(nm):
            pool.wait_ge(*reach(nm + "_ss", NT))
            pool_rsqrt(stat("norm", 4)[:, 2:4], stat("norm", 4)[:, 0:2], D, nm + "_r")

        def dve_norm(nm, gain):
            dve.wait_ge(*reach(nm + "_r", 1))
            for t in range(NT):
                dve.tensor_scalar(xn[:, t], X[:, t], stat("norm", 4)[:, 2 + t:3 + t], None, ALU.mult).then_inc(S(nm + "_xn"), 1)
            for j in range(KD // 2):
                dve.wait_ge(*reach(nm + "_hi", 2 * j + 2))
                for c in range(2):
                    dve.scalar_tensor_tensor(Ul[:, 2 * j + c], bank[4 + j][:, c * T:(c + 1) * T], gcol(gain, 2 * j + c),
                                             Uh[:, 2 * j + c].bitcast(F32), ALU.mult, ALU.subtract).then_inc(S(nm + "_lo"), 1)

        def pe_norm(nm):
            for j in range(KD // 2):
                claim(4 + j, nm + "_lo", 2 * j + 2)
                for c in range(2):
                    for t in range(NT):
                        pe.wait_ge(*reach(nm + "_xn", t + 1))
                        last = pe.transpose(bank[4 + j][:, c * T + t * P:c * T + (t + 1) * P],
                                            xn[:, t, (2 * j + c) * P:(2 * j + c + 1) * P], ident)
                last.then_inc(S(nm + "_tr"), 1)
            pe.wait_ge(*reach(nm + "_lo", KD))

        def gate_slab(b, i):
            return b if isinstance(i, int) and i == 0 else 3 * i + (b - 1)

        def pe_ffn(nm, n):
            b = slab_of[nm]
            for k in range(4):
                claim(k, nm + "_x", k + 1)
                pe.matmul(bank[k][:, :], zero[:, 0:P], zero[:, :], start=True, stop=False, skip_group_check=True)
            claim(4, nm + "_silu", n)
            claim(5, nm + "_mul", n)

            def up(i, g, q=None):
                off = 0 if q is None else 3 * q
                for j, done in enumerate(("_silu", "_mul")):
                    pe.wait_ge(*reach("lo_done", g + j + 1 + off))
                    if i is not None:
                        pe.wait_ge(*reach(nm + done, i))
                    by_feature(g + j, 4 + j, Uh, Ul, KD, 256).then_inc(S("slab_used"), 1)

            def down(i, g, q=None, last=False):
                pe.wait_ge(*reach("lo_done", g + 1 + (0 if q is None else 3 * q)))
                pe.wait_ge(*reach(nm + "_h", i + 1))
                wh, wl = wslab(g, 2, 1024)
                for t in range(NT):
                    for half in range(2):
                        for k in range(2):
                            f = slice(k * T + t * P, k * T + (t + 1) * P)
                            c = slice(half * 512, (half + 1) * 512)
                            m = mm3(bank[2 * t + half][:, :], hh[:, f], hl[:, f], wh[:, k, c], wl[:, k, c], False, last and k == 1)
                m.then_inc(S("slab_used"), 1)

            up(None, b)
            up(1, b + 2)
            down(0, b + 4)
            with pe.Fori(1, n - 1) as i:
                up(i + 1, b + 2, i)
                down(i, b + 4, i)
            down(n - 1, b + 3 * n - 1, None, True)

        def act_ffn(nm, n, moe=False):
            b = slab_of[nm]

            def silu(i, used_by):
                act.wait_ge(*reach("slab_used", used_by))
                if not (isinstance(i, int) and i == 0):
                    act.wait_ge(*reach(nm + ("_comb" if moe else "_mul"), i))
                act.activation(sgh[:, 0], bank[4][:, :], ACT.Silu).then_inc(S(nm + "_silu"), 1)

            hi_upto(nm)
            silu(0, b + 1)
            for k in range(3):
                split_hi(b + 3 + k)
            with act.Fori(1, n - 1) as i:
                silu(i, i * 3 + b)
                for k in range(3):
                    split_hi(b + 3 + k, i)
            nxt["hi"] = b + 3 * n
            silu(n - 1, b + 3 * (n - 1))

        def dve_ffn(nm, n, moe=False):
            b = slab_of[nm]

            def mul(i, used_by):
                dve.wait_ge(*reach("slab_used", used_by))
                dve.wait_ge(*reach(nm + ("_comb" if moe else "_silu"), i + 1))
                if not (isinstance(i, int) and i == 0):
                    dve.wait_ge(*reach(nm + "_h", i))
                src = sgh[:, 0] if not moe else COMBW
                dve.tensor_tensor(sgh[:, 1], src, bank[5][:, :], ALU.mult).then_inc(S(nm + "_mul"), 1)

            lo_upto(nm)
            mul(0, b + 2)
            for k in range(3):
                split_lo(b + 3 + k)
            with dve.Fori(1, n - 1) as i:
                mul(i, i * 3 + b + 1)
                for k in range(3):
                    split_lo(b + 3 + k, i)
            nxt["lo"] = b + 3 * n
            mul(n - 1, b + 3 * (n - 1) + 1)
            for t in range(NT):
                for half in range(2):
                    dve.wait_ge(*reach("slab_used", b + 3 * n))
                    dve.scalar_tensor_tensor(X[:, t, half * 512:(half + 1) * 512], bank[2 * t + half][:, :],
                                             1.0 if moe else 0.5, X[:, t, half * 512:(half + 1) * 512],
                                             ALU.mult, ALU.add).then_inc(S(nm + "_x"), 1)

        def pool_ffn(nm, n, moe=False):
            b = slab_of[nm]

            def hidden(i, first=False):
                if moe:
                    pool.wait_ge(*reach(nm + "_silu", i + 1))
                    if not first:
                        pool.wait_ge(*reach(nm + "_mul", i))
                    w_e = COMB[:, i, :]
                    for c in range(2):
                        m = pool.tensor_tensor(COMBW[:, c * T:(c + 1) * T], sgh[:, 0, c * T:(c + 1) * T], w_e, ALU.mult)
                        if c == 1:
                            m.then_inc(S(nm + "_comb"), 1)
                pool.wait_ge(*reach(nm + "_mul", i + 1))
                if not first:
                    pool.wait_ge(*reach("slab_used", i * 3 + b + 2))
                pool.tensor_tensor(hh[:, :], sgh[:, 1], zero[:, :].bitcast(F32), ALU.add).then_inc(S(nm + "_hh"), 1)
                pool.wait_ge(*reach(nm + "_hh", i + 1))
                pool.tensor_tensor(hl[:, :], sgh[:, 1], hh[:, :].bitcast(F32), ALU.subtract).then_inc(S(nm + "_h"), 1)

            hidden(0, True)
            with pool.Fori(1, n) as i:
                hidden(i)

        scr = sgh[:, :, :].rearrange("p a n -> p (a n)")

        def act_head_squares(nm, buf, H, d, after):
            for t in range(NT):
                if t or after:
                    w = (nm + "_red", t) if t else after
                    act.wait_ge(*reach(w[0], w[1]))
                act.activation(scr[:, 0:H * d], buf[:, t].rearrange("p h d -> p (h d)"), ACT.Square).then_inc(S(nm + "_sq"), 1)

        def dve_head_sums(nm, H, d):
            for t in range(NT):
                dve.wait_ge(*reach(nm + "_sq", t + 1))
                dve.tensor_reduce(stat(nm, 2 * H)[:, t * H:(t + 1) * H], scr[:, 0:H * d].rearrange("p (h d) -> p h d", d=d),
                                  AX, ALU.add).then_inc(S(nm + "_red"), 1)

        def pool_head_rsqrt(nm, H, d):
            pool.wait_ge(*reach(nm + "_red", NT))
            pool_rsqrt(stat(nm, NT * H), stat(nm, NT * H), d, nm + "_r")

        def dve_head_scale(nm, buf, H, d, gain, out=None):
            dve.wait_ge(*reach(nm + "_r", 1))
            r = stat(nm, NT * H).rearrange("p (t h) -> p t h", t=NT).unsqueeze(3).to_broadcast([P, NT, H, d])
            g = pb(gain).unsqueeze(1).unsqueeze(1).to_broadcast([P, NT, H, d])
            dve.tensor_tensor(buf, buf, r, ALU.mult).then_inc(S(nm + "_scaled"), 1)
            dve.wait_ge(*reach(nm + "_scaled", 1))
            dve.tensor_tensor(buf, buf, g, ALU.mult).then_inc(S(nm + "_scaled"), 1)
            dve.wait_ge(*reach(nm + "_scaled", 2))

        def dve_rope(nm, buf, H, lo, half, cos, sin):
            n = NT * H * half
            m = [scr[:, k * 256:k * 256 + n].rearrange("p (t h d) -> p t h d", t=NT, h=H) for k in range(4)]
            x1, x2 = buf[:, :, :, lo:lo + half], buf[:, :, :, lo + half:lo + 2 * half]
            c = cos.unsqueeze(2).to_broadcast([P, NT, H, half])
            s_ = sin.unsqueeze(2).to_broadcast([P, NT, H, half])
            for k, (x, f) in enumerate(((x1, c), (x2, s_), (x2, c), (x1, s_))):
                dve.tensor_tensor(m[k], x, f, ALU.mult).then_inc(S(nm + "_turn"), 1)
            dve.wait_ge(*reach(nm + "_turn", 4))
            dve.tensor_tensor(x1, m[0], m[1], ALU.subtract).then_inc(S(nm + "_turn"), 1)
            dve.tensor_tensor(x2, m[2], m[3], ALU.add).then_inc(S(nm + "_turn"), 1)

        def pe_attention(nm, H, qt, kt, v):
            for i in range(H + 3):
                if i < H:
                    claim(i % 3, nm + "_mx", 2 * i + 2)
                    b = bank[i % 3]
                    pe.matmul(b[:, 0:P], qt(i)[:, 0:P], kt(i)[:, 0:P], start=True, stop=True, skip_group_check=True)
                    pe.matmul(b[:, P:3 * P], qt(i)[:, P:T], kt(i), start=False, stop=True,
                              skip_group_check=True).then_inc(S(nm + "_s"), 1)
                if 2 <= i < H + 2:
                    h = i - 2
                    claim(3 + h % 2, nm + "_ptc", h + 1)
                    pe.wait_ge(*reach(nm + "_pn", 2 * h + 2))
                    for k in range(3):
                        last = pe.transpose(bank[3 + h % 2][:, k * P:(k + 1) * P], aw[:, h % 3, k * P:(k + 1) * P], ident)
                    last.then_inc(S(nm + "_pt"), 1)
                if i >= 3:
                    h = i - 3
                    b = 5 + (h // 2) % 2
                    if h % 2 == 0:
                        claim(b, nm + "_olo", h // 2 + 1)
                    pe.wait_ge(*reach(nm + "_ptc", h + 1))
                    o = bank[b][64 * (h % 2):64 * (h % 2) + 64, 0:T]
                    pe.matmul(o, v(h, 0), aw[:, 3 + h % 2, 0:T], start=True, stop=False, skip_group_check=True)
                    pe.matmul(o[:, P:T], v(h, 1), aw[:, 3 + h % 2, T:3 * P], start=False, stop=True,
                              skip_group_check=True).then_inc(S(nm + "_av"), 1)

        def dve_attention(nm, H, bias, scale, outh, outl):
            mx, nmx, sm, rs = (stat(f"att_{k}", 32) for k in range(4))
            for i in range(H + 5):
                if i < H:
                    dve.wait_ge(*reach(nm + "_s", i + 1))
                    if i >= 3:
                        dve.wait_ge(*reach(nm + "_pt", i - 2))
                    for t, (lo, hi) in enumerate(((0, P), (P, 3 * P))):
                        dve.tensor_tensor_reduce(out=aw[:, i % 3, lo:hi], in0=bank[i % 3][:, lo:hi], in1=bias[:, lo:hi],
                                                 scale=1.0, scalar=-3e38, op0=ALU.add, op1=ALU.max,
                                                 accum_out=mx[:, 2 * i + t:2 * i + t + 1]).then_inc(S(nm + "_mx"), 1)
                    dve.wait_ge(*reach(nm + "_mx", 2 * i + 2))
                    dve.tensor_scalar(nmx[:, 2 * i:2 * i + 2], mx[:, 2 * i:2 * i + 2], -scale, None,
                                      ALU.mult).then_inc(S(nm + "_nm"), 1)
                if 1 <= i < H + 1:
                    h = i - 1
                    dve.wait_ge(*reach(nm + "_exp", 2 * h + 2))
                    dve.reciprocal(rs[:, 2 * h:2 * h + 2], sm[:, 2 * h:2 * h + 2]).then_inc(S(nm + "_rs"), 1)
                    dve.wait_ge(*reach(nm + "_rs", h + 1))
                    for t, (lo, hi) in enumerate(((0, P), (P, 3 * P))):
                        dve.tensor_scalar(aw[:, h % 3, lo:hi], aw[:, h % 3, lo:hi], rs[:, 2 * h + t:2 * h + t + 1], None,
                                          ALU.mult).then_inc(S(nm + "_pn"), 1)
                h = i - 4
                if h >= 0 and h % 2 == 1:
                    dve.wait_ge(*reach(nm + "_ohi", h // 2 + 1))
                    dve.tensor_tensor(outl[:, h // 2], bank[5 + (h // 2) % 2][:, 0:T], outh[:, h // 2].bitcast(F32),
                                      ALU.subtract).then_inc(S(nm + "_olo"), 1)

        def act_attention(nm, H, scale, outh):
            nmx, sm = stat("att_1", 32), stat("att_2", 32)
            for i in range(H + 5):
                if i < H:
                    act.wait_ge(*reach(nm + "_nm", i + 1))
                    for t, (lo, hi) in enumerate(((0, P), (P, 3 * P))):
                        act.activation(aw[:, i % 3, lo:hi], aw[:, i % 3, lo:hi], ACT.Exp, bias=nmx[:, 2 * i + t:2 * i + t + 1],
                                       scale=scale, accum_out=sm[:, 2 * i + t:2 * i + t + 1]).then_inc(S(nm + "_exp"), 1)
                if 2 <= i < H + 2:
                    h = i - 2
                    act.wait_ge(*reach(nm + "_pt", h + 1))
                    if h >= 2:
                        act.wait_ge(*reach(nm + "_av", h - 1))
                    act.activation(aw[:, 3 + h % 2, :], bank[3 + h % 2][:, 0:3 * P], ACT.Copy).then_inc(S(nm + "_ptc"), 1)
                h = i - 4
                if h >= 0 and h % 2 == 1:
                    act.wait_ge(*reach(nm + "_av", h + 1))
                    act.activation(outh[:, h // 2], bank[5 + (h // 2) % 2][:, 0:T], ACT.Copy).then_inc(S(nm + "_ohi"), 1)

        def xbc_bank(j):
            return (2, 3, 5, 6)[j] if j < 4 else 7

        awf = aw[:, :].rearrange("p a n -> p (a n)")

        def EM(n):
            return awf[:, n % 4 * 512:(n % 4 + 1) * 512]

        rt_at = {}

        def rt(name, n):
            if name not in rt_at:
                rt_at[name] = sum(v[1] for v in rt_at.values()), n
            at, _ = rt_at[name]
            assert at + n <= 3 * 384
            return awf[:, at:at + n]

        block = ctx.enter_context(nc.Block())

        @block.sync
        def _(sp):
            i = 0
            while i < len(slabs):
                if i in loops:
                    n, gate, up, down = loops[i]
                    load(sp, i, None, gate(0))
                    load(sp, i + 1, None, up(0))
                    load(sp, i + 2, None, gate(1))
                    load(sp, i + 3, None, up(1))
                    load(sp, i + 4, None, down(0))
                    with sp.Fori(1, n - 1) as q:
                        load(sp, i + 2, q, gate(q + 1))
                        load(sp, i + 3, q, up(q + 1))
                        load(sp, i + 4, q, down(q))
                    load(sp, i + 3 * n - 1, None, down(n - 1))
                    i += 3 * n
                else:
                    load(sp, i)
                    i += 1
            sp.wait_ge(*reach("moe_x", 4))
            sp.dma_start(out.rearrange("o (t p) d -> p (o t) d", p=P), X[:]).then_inc(S("out"), 16)
            sp.wait_ge(*reach("out", 16))

        @block.scalar
        def _(_e):
            act.dma_start(C[:], a["const"]).then_inc(S("ld_const"), 16)
            act.dma_start(X[:], a["x"].rearrange("o (t p) d -> p (o t) d", p=P)).then_inc(S("ld_x"), 16)
            for name, n in gain_rows:
                at = gain_at[name]
                act.dma_start(rows1[at:at + n, :], a[name].rearrange("o (c p) -> (o c) p", p=P)).then_inc(S("ld_rows"), 16)
            act.dma_start(rows2[0:n_rows2, :], a["conv_w_2"].rearrange("o t (c p) -> (o t c) p", p=P)).then_inc(S("ld_rows"), 16)
            act.preload_act_table(ACT.Silu)
            act.wait_ge(*reach("ld_x", 16))
            for t in range(NT):
                act.activation(xn[:, t], X[:, t], ACT.Square, accum_out=stat("norm", 4)[:, t:t + 1]).then_inc(S("n1_ss"), 1)
            act.dma_start(pos[:], a["positions"].rearrange("o (t p) -> p (o t)", p=P),
                          allow_slow_non_contiguous=True).then_inc(S("ld_pos"), 16)
            for name, n in pb_list:
                at = pb_at[name][0]
                act.dma_start(PB[:, at:at + n], a[name][0].partition_broadcast(P)).then_inc(S("ld_pb"), 16)
            act.wait_ge(*reach("gains", 2))
            for j in range(KD // 2):
                act.wait_ge(*reach("n1_tr", j + 1))
                for c in range(2):
                    act.activation(Uh[:, 2 * j + c], bank[4 + j][:, c * T:(c + 1) * T], ACT.Copy,
                                   scale=gcol("ffn1_norm", 2 * j + c)).then_inc(S("n1_hi"), 1)
                if j == 0:
                    hi_upto("ffn1")
            act.wait_ge(*reach("angles", 2))
            act.activation(SIN1, rope1[:, 4], ACT.Sin).then_inc(S("rope1"), 1)
            act.activation(COS1, rope1[:, 5], ACT.Sin).then_inc(S("rope1"), 1)
            act_ffn("ffn1", NF)

            act_norm("n2", ("ffn1_x", 4), "mix_norm")
            for i in range(3):
                hi_upto(f"lat{i}")
                used(act, f"lat{i}")
                n = slabs[slab_of[f"lat{i}"]][2]
                act.activation(CQ[:, :, i * 256:i * 256 + n], bank[i].rearrange("p (t n) -> p t n", t=NT)[:, :, 0:n],
                               ACT.Copy).then_inc(S("lat_ev"), 1)
            act.preload_act_table_set("natural_log_exp_and_others")
            act.wait_ge(*reach("lat_ev", 3))
            for t in range(NT):
                act.activation(xn[:, t, 0:QL], CQ[:, t, 0:QL], ACT.Square, accum_out=stat("lat", 4)[:, t:t + 1]).then_inc(S("lat_ss"), 1)
                act.activation(xn[:, t, QL:QL + KVL], CQ[:, t, QL:QL + KVL], ACT.Square,
                               accum_out=stat("lat", 4)[:, 2 + t:3 + t]).then_inc(S("lat_ss"), 1)
            for j, (nm, dst) in enumerate((("sq", sqT), ("sk", skT))):
                for i in range(2):
                    hi_upto(f"{nm}{i}")
                    used(act, f"{nm}{i}")
                    act.activation(dst[:, 2 * i:2 * i + 2].rearrange("p c n -> p (c n)"), bank[3 + 2 * j + i][:, :], ACT.Copy,
                                   scale=0.125 if nm == "sq" else 1.0).then_inc(S("sqk_ev"), 1)
            for i in range(2):
                hi_upto(f"sv{i}")
                used(act, f"sv{i}")
                act.activation(sv[:, :, i * 256:(i + 1) * 256], bank[(7, 0)[i]].rearrange("p (t n) -> p t n", t=NT),
                               ACT.Copy).then_inc(S("sv_ev"), 1)
            for c in range(5):
                act.wait_ge(*reach("lt_tr", c // 2 + 1))
                gain = gcol("q_latent_norm", c) if c < 3 else gcol("kv_latent_norm", c - 3)
                act.activation(Lh[:, c], bank[1 + c // 2][:, c % 2 * T:(c % 2 + 1) * T], ACT.Copy, scale=gain).then_inc(S("lt_hi"), 1)
            for i in range(2):
                hi_upto(f"qup{i}")
                used(act, f"qup{i}")
                for t in range(NT):
                    act.activation(Q1[:, t, 4 * i:4 * i + 4].rearrange("p h d -> p (h d)"), bank[4 + 2 * i + t if i == 0 else t][:, 0:384],
                                   ACT.Copy).then_inc(S("q_ev"), 1)
            hi_upto("kvup")
            used(act, "kvup")
            for t in range(NT):
                for half in range(2):
                    b = bank[(2, 3, 6, 7)[2 * t + half]].rearrange("p (h d) -> p h d", d=P)
                    act.activation(K1[:, t, 4 * half:4 * half + 4, 0:NOPE], b[:, :, 0:NOPE], ACT.Copy).then_inc(S("kv_ev"), 1)
                    act.activation(V1[:, t, 4 * half:4 * half + 4, :], b[:, :, NOPE:P], ACT.Copy).then_inc(S("kv_ev"), 1)
            act.wait_ge(*reach("q_ev", 4))
            act_head_squares("hq", Q1, MH, QK, None)
            act.wait_ge(*reach("kv_ev", 8))
            act.wait_ge(*reach("krope", 1))
            act_head_squares("hk", K1[:], MH, QK, ("hq_red", 2))

            def gate_out(g, b):
                hi_upto(f"gate{g}")
                used(act, f"gate{g}")
                act.activation(GT[:, 2 * g:2 * g + 2].rearrange("p c n -> p (c n)"), bank[b][:, :], ACT.Copy).then_inc(S("gate_ev"), 1)

            for g in range(3):
                gate_out(g, (4, 5, 4)[g])
            for j in range(4):
                act.wait_ge(*reach("qt_tr", j + 1))
                act.activation(QT1[:, 2 * j:2 * j + 2].rearrange("p h n -> p (h n)"), bank[j][0:QK, :], ACT.Copy).then_inc(S("qt_ev"), 1)
            for i in range(8 + 6):
                if i < 8:
                    hi_upto(f"gate{min(7, 3 + i)}")
                    act.wait_ge(*reach("sb_z", i + 1))
                    if i >= 2:
                        act.wait_ge(*reach("sb_sp", i - 1))
                    act.activation(aw[:, i % 2], bank[i % 4][:, 0:384], ACT.Abs).then_inc(S("sb_l"), 1)
                    act.wait_ge(*reach("sb_l", 3 * i + 1))
                    act.activation(aw[:, i % 2], aw[:, i % 2], ACT.Exp, scale=-1.0).then_inc(S("sb_l"), 1)
                    act.wait_ge(*reach("sb_l", 3 * i + 2))
                    act.activation(aw[:, i % 2], aw[:, i % 2], ACT.Ln, bias=1.0).then_inc(S("sb_l"), 1)
                h = i - 3
                if 0 <= h < 8:
                    act.wait_ge(*reach("sb_m", h + 1))
                    act.activation(aw[:, 4 + h % 2], aw[:, 4 + h % 2], ACT.Exp).then_inc(S("sb_a"), 1)
                if i < 5:
                    gate_out(3 + i, 6 + i % 2)
                h = i - 5
                if h >= 0 and h % 2 == 1:
                    act.wait_ge(*reach("sb_av", h + 1))
                    act.activation(OSh[:, h // 2], bank[4 + (h // 2) % 2][:, 0:T], ACT.Copy).then_inc(S("os_hi"), 1)
            hi_upto("mla0")
            act_attention("mla", MH, QK ** -0.5, OMh)
            act.preload_act_table(ACT.Sigmoid)
            act.wait_ge(*reach("gate_ev", 8))
            for q in range(4):
                act.activation(GT[:, 4 * q:4 * q + 4].rearrange("p c n -> p (c n)"), GT[:, 4 * q:4 * q + 4].rearrange("p c n -> p (c n)"),
                               ACT.Sigmoid).then_inc(S("gsig"), 1)
            for q in range(4):
                hi_upto(f"sbr{q // 2}")
                act.wait_ge(*reach("mg_s", q + 1))
                act.activation(Uh[:, 2 * q:2 * q + 2].rearrange("p c n -> p (c n)"), sgh[:, q % 2], ACT.Copy).then_inc(S("mg_hi"), 1)
            hi_upto("wout3")
            act_norm("n3", ("x2", 4), "ffn2_norm")
            act.dma_start(aw[:, 0:2, 0:PLE], a["p"][0, 0].rearrange("(t p) n -> p t n", p=P)).then_inc(S("ld_p"), 16)
            act.preload_act_table(ACT.Silu)
            act_ffn("ffn2", NF)
            act.wait_ge(*reach("p_tr", 1))
            act.activation(OMh[:, 0:2].rearrange("p c n -> p (c n)"), bank[6][:, :], ACT.Copy).then_inc(S("p_hi"), 1)
            act.preload_act_table(ACT.Sigmoid)
            act_norm("n4", ("ffn2_x", 4), "ple_norm")
            hi_upto("pproj")
            used(act, "pproj")
            for c in range(4):
                act.activation(PP[:, :, c * 256:(c + 1) * 256], bank[c].rearrange("p (t n) -> p t n", t=NT), ACT.Copy).then_inc(S("pp_ev"), 1)
            for c in range(4):
                hi_upto(f"pgate{c}")
                used(act, f"pgate{c}")
                if c >= 2:
                    act.wait_ge(*reach("x4", c - 1))
                act.activation(sgh[:, c % 2], bank[4 + c][:, :], ACT.Sigmoid).then_inc(S("pg"), 1)

            act_norm("n5", ("x4", 4), "attn_norm_2")
            act.preload_act_table_set("natural_log_exp_and_others")
            tok = lambda b, n: bank[b].rearrange("p (t n) -> p t n", t=NT)[:, :, 0:n]
            outs = [(f"q{i}", i, xn[:, :, i * 256:(i + 1) * 256], 256) for i in range(4)]
            outs += [("k", 4, K2[:].rearrange("p t h d -> p t (h d)"), 256), ("v", 5, V2[:], 256),
                     ("iq0", 6, IQ[:, :, 0:4].rearrange("p t h d -> p t (h d)"), 256),
                     ("iq1", 7, IQ[:, :, 4:8].rearrange("p t h d -> p t (h d)"), 256),
                     ("ik", 0, IKW[:], HD + IH), ("dt", 1, ssm[:, 0:2], SH)]
            for nm, b, dst, n in outs:
                hi_upto(nm)
                used(act, nm)
                act.activation(dst, tok(b, n), ACT.Copy).then_inc(S("b2_ev"), 1)
            act.wait_ge(*reach("b2_ev", 9))
            act_head_squares("ik", IKW[:, :, 0:HD].unsqueeze(2), 1, HD, None)
            act_head_squares("k2", K2[:], KVH2, HD, ("ik_red", 2))
            act_head_squares("q2", Q2, H2, HD, ("k2_red", 2))
            act.wait_ge(*reach("dt_x", 1))
            act.activation(ssm[:, 2:4], ssm[:, 0:2], ACT.Abs).then_inc(S("dt_l"), 1)
            act.wait_ge(*reach("dt_l", 1))
            act.activation(ssm[:, 2:4], ssm[:, 2:4], ACT.Exp, scale=-1.0).then_inc(S("dt_l"), 1)
            act.wait_ge(*reach("dt_l", 2))
            act.activation(ssm[:, 2:4], ssm[:, 2:4], ACT.Ln, bias=1.0).then_inc(S("dt_l"), 1)
            act.activation(ssm[:, 8], pb("a_log_2"), ACT.Exp).then_inc(S("dt_l"), 1)

            def conv_in(j):
                b = xbc_bank(j)
                hi_upto(f"xbc{j}")
                used(act, f"xbc{j}")
                if j >= 2:
                    act.wait_ge(*reach("conv", 6 * (j - 1)))
                act.activation(sgh[:, j % 2], bank[b][:, :], ACT.Copy).then_inc(S("xb_ev"), 1)
                for c in range(2):
                    ch = 2 * j + c
                    act.activation(XC[:, ch], bank[b][:, c * T:(c + 1) * T], ACT.Identity, bias=gcol("conv_b_2", ch),
                                   scale=gcol("conv_w_2", (TAPS - 1) * NX + ch)).then_inc(S("xb_ev"), 1)

            hi_upto("xbc1")
            for i in range(2):
                act.wait_ge(*reach("iqt_tr", i + 1))
                act.activation(IQT[:, 2 * i:2 * i + 2].rearrange("p c n -> p (c n)"), bank[4 + i][:, :], ACT.Copy).then_inc(S("iqt_ev"), 1)
            hi_upto("xbc2")
            for i in range(4):
                act.wait_ge(*reach("qt2_tr", i + 1))
                act.activation(QT2[:, 2 * i:2 * i + 2].rearrange("p c n -> p (c n)"), bank[(1, 4, 5, 6)[i]][:, :],
                               ACT.Copy).then_inc(S("qt2_ev"), 1)
            for h in range(IH):
                act.wait_ge(*reach("ix_s", h + 1))
                if h >= 3:
                    act.wait_ge(*reach("ix_a", 2 * (h - 2)))
                act.activation(aw[:, h % 3], bank[(7, 0, 1, 4)[h % 4]][:, 0:384], ACT.Relu, scale=HD ** -0.5).then_inc(S("ix_r"), 1)
            for j in range(4):
                hi_upto(f"xbc{j}", 0 if j < 3 else 1)
                conv_in(j)
            nmx, sm = stat("att_1", 32), stat("att_2", 32)
            for i in range(H2 + 5):
                if i < H2:
                    act.wait_ge(*reach("dsa_nm", i + 1))
                    for t, (lo, hi) in enumerate(((0, P), (P, 3 * P))):
                        act.activation(aw[:, i % 3, lo:hi], aw[:, i % 3, lo:hi], ACT.Exp, bias=nmx[:, 2 * i + t:2 * i + t + 1],
                                       scale=HD ** -0.5, accum_out=sm[:, 2 * i + t:2 * i + t + 1]).then_inc(S("dsa_exp"), 1)
                if 2 <= i < H2 + 2:
                    h = i - 2
                    act.wait_ge(*reach("dsa_pt", h + 1))
                    if h >= 2:
                        act.wait_ge(*reach("dsa_av", h - 1))
                    act.activation(aw[:, 3 + h % 2, :], bank[3 + h % 2][:, 0:3 * P], ACT.Copy).then_inc(S("dsa_ptc"), 1)
                h = i - 4
                if h >= 0 and h % 2 == 1:
                    act.wait_ge(*reach("dsa_av", h + 1))
                    act.activation(OAh[:, h // 2], bank[5 + (h // 2) % 2][:, 0:T], ACT.Copy).then_inc(S("dsa_ohi"), 1)
                if 4 + i // 2 < NX // 2 and i % 2 == 0:
                    conv_in(4 + i // 2)
            act.preload_act_table(ACT.Silu)
            act.wait_ge(*reach("conv", 6 * (NX // 2)))
            for q in range(6):
                v = XC[:, 4 * q:4 * q + 4].rearrange("p c n -> p (c n)")
                act.activation(v, v, ACT.Silu).then_inc(S("xc"), 1)
            act.preload_act_table(ACT.Exp)
            hi_upto("wa0")
            for j in range(8):
                act.wait_ge(*reach("xs_tr", j + 1))
                act.activation(XS[:, :, j * 256:(j + 1) * 256], tok(j % 4, 256), ACT.Copy).then_inc(S("xs_ev"), 1)
            act.wait_ge(*reach("bt_tr", 1))
            act.activation(BTM[:].rearrange("p g n -> p (g n)"), bank[4][:, :], ACT.Copy).then_inc(S("bt_ev"), 1)
            act.wait_ge(*reach("acs", 2))
            act.activation(ssm[:, 7], ssm[:, 7], ACT.Exp).then_inc(S("ee"), 1)
            act.activation(ssm[:, 9], ssm[:, 5], ACT.Exp).then_inc(S("ee"), 1)

            def side_out(u):
                nm = f"wa{u}" if u < 4 else f"g{u - 4}"
                hi_upto(nm)
                used(act, nm)
                dst = BA[:, 2 * u:2 * u + 2] if u < 4 else G2[:, 2 * (u - 4):2 * (u - 4) + 2]
                act.activation(dst.rearrange("p c n -> p (c n)"), bank[7][:, :], ACT.Copy).then_inc(S("side_ev"), 1)

            for u in range(8):
                hi_upto(f"wa{u}" if u < 4 else f"g{u - 4}")
                for k in range(2):
                    n = 2 * u + k
                    act.wait_ge(*reach("seg", n + 1))
                    act.activation(EM(n), EM(n), ACT.Exp).then_inc(S("seg_e"), 1)
                if u < 4:
                    act.wait_ge(*reach("st_mm", u + 1))
                    act.activation(ST[:, u], bank[6][:, :], ACT.Copy).then_inc(S("st_ev"), 1)
                side_out(u)
            act.preload_act_table(ACT.Silu)
            for c in range(8):
                hi_upto(f"z{c}")
                used(act, f"z{c}")
                if c >= 2:
                    act.wait_ge(*reach("yz", c - 1))
                else:
                    act.wait_ge(*reach("y", 12))
                act.activation(sgh[:, c % 2], bank[c % 4][:, :], ACT.Silu).then_inc(S("z_s"), 1)
                if c % 2:
                    act.wait_ge(*reach("yz", c + 1))
                    for t in range(NT):
                        act.wait_ge(*reach("yg_ss", 2 * (c // 2) + t)) if c > 1 or t else act.wait_ge(*reach("seg_m", 16))
                        act.activation(awf[:, 0:512], XS[:, t, c // 2 * 512:c // 2 * 512 + 512], ACT.Square,
                                       accum_out=stat("yg", 8)[:, 4 * t + c // 2:4 * t + c // 2 + 1]).then_inc(S("yg_ss"), 1)

            def gate2_out(g):
                hi_upto(f"g{g}")
                used(act, f"g{g}")
                act.activation(G2[:, 2 * g:2 * g + 2].rearrange("p c n -> p (c n)"), bank[4 + g % 4][:, :], ACT.Copy).then_inc(S("g2_ev"), 1)

            for g in range(4, 8):
                gate2_out(g)
            for j in range(8):
                act.wait_ge(*reach("yt_tr", j + 1))
                for c in range(2):
                    act.activation(YTh[:, 2 * j + c], bank[j % 4][:, c * T:(c + 1) * T], ACT.Copy,
                                   scale=gcol("ssd_norm_2", 2 * j + c)).then_inc(S("yt_hi"), 1)
            act.preload_act_table(ACT.Sigmoid)
            act.wait_ge(*reach("side_ev", 8))
            act.wait_ge(*reach("g2_ev", 4))
            for q in range(4):
                v = G2[:, 4 * q:4 * q + 4].rearrange("p c n -> p (c n)")
                act.activation(v, v, ACT.Sigmoid).then_inc(S("g2sig"), 1)
            for q in range(4):
                hi_upto(f"ws{q}1")
                act.wait_ge(*reach("m2_s", q + 1))
                act.activation(Uh[:, 2 * q:2 * q + 2].rearrange("p c n -> p (c n)"), sgh[:, q % 2], ACT.Copy).then_inc(S("m2_hi"), 1)
            hi_upto("wo3")
            act_norm("n6", ("x5", 4), "ffn_norm_2")
            hi_upto("re")
            act.preload_act_table(ACT.Exp)
            act.wait_ge(*reach("r_gl", 1))
            act.activation(rt("gexp", 8), rt("gexp", 8), ACT.Exp).then_inc(S("r_e"), 1)
            act.wait_ge(*reach("r_d", 1))
            act.activation(rt("d", 2), rt("d", 2), ACT.Exp).then_inc(S("r_e"), 1)
            act.preload_act_table(ACT.Silu)
            act.wait_ge(*reach("ct_ev", 1))
            act.dma_start(scratch, CT).then_inc(S("ct_out"), 16)
            act.wait_ge(*reach("ct_out", 16))
            act.dma_start(COMB[:], scratch.partition_broadcast(P)).then_inc(S("ld_comb"), 16)
            act_ffn("moe", NE, True)

        @block.vector
        def _(_e):
            dve.memset(zero[:, :].bitcast(F32), 0.0).then_inc(S("zeroed"), 1)
            n_ld = 16 * (len(gain_rows) + 1)
            for j, (rows, nr, sem) in enumerate(((rows1, n_rows1, "gains"), (rows2, n_rows2, "gains"))):
                dve.wait_ge(*reach("rows_tr", j + 1))
                dve.tensor_copy(G[:, j * P:j * P + nr], bank[j][:, 0:nr]).then_inc(S("gains"), 1)
            dve.wait_ge(*reach("gains", 2))
            dve_norm("n1", "ffn1_norm")
            chain = [0]

            def link(ins):
                chain[0] += 1
                ins.then_inc(S("angle_chain"), 1)
                dve.wait_ge(*reach("angle_chain", chain[0]))

            dve.wait_ge(*reach("ld_pos", 16))
            posf = stat("posf", NT)
            link(dve.tensor_copy(posf, pos[:]))
            ang, k, r, r2 = rope1[:, 0], rope1[:, 1], rope1[:, 4], rope1[:, 5]
            dve.wait_ge(*reach("ld_const", 16))
            for t in range(NT):
                m = dve.tensor_scalar(ang[:, t], const("invf"), posf[:, t:t + 1], None, ALU.mult)
                link(m)
            link(dve.tensor_scalar(k, ang, float(1 / (2 * np.pi)), 12582912.0, ALU.mult, ALU.add))
            link(dve.tensor_scalar(k, k, 12582912.0, None, ALU.subtract))
            c1 = 6.28125
            c2 = float(np.float32(np.floor((2 * np.pi - c1) * 2 ** 17) / 2 ** 17))
            c3 = float(np.float32(2 * np.pi - c1 - c2))
            src = ang
            for n, part in enumerate((c1, c2, c3)):
                dst = (rope1[:, 2], rope1[:, 3], r)[n]
                link(dve.scalar_tensor_tensor(dst, k, -part, src, ALU.mult, ALU.add))
                src = dst
            lim = 3.1415925
            link(dve.tensor_scalar(r2, r, float(np.pi / 2), None, ALU.add))
            link(dve.tensor_scalar(rope1[:, 2], r2, float(np.pi), -float(2 * np.pi), ALU.is_gt, ALU.mult))
            link(dve.tensor_tensor(r2, r2, rope1[:, 2], ALU.add))
            for v in (r, r2):
                dve.tensor_scalar(v, v, lim, -lim, ALU.min, ALU.max).then_inc(S("angles"), 1)
            dve_ffn("ffn1", NF)

            dve.wait_ge(*reach("ffn1_x", 4))
            dve_norm("n2", "mix_norm")
            lo_upto("lat2")
            dve.wait_ge(*reach("lat_r", 2))
            for t in range(NT):
                for k, (lo, hi) in enumerate(((0, QL), (QL, QL + KVL))):
                    dve.tensor_scalar(CQ[:, t, lo:hi], CQ[:, t, lo:hi], stat("lat", 4)[:, 2 * k + t:2 * k + t + 1], None,
                                      ALU.mult).then_inc(S("lat_n"), 1)
            lo_upto("sv1")
            for c in range(5):
                dve.wait_ge(*reach("lt_hi", min(5, c // 2 * 2 + 2)))
                gain = gcol("q_latent_norm", c) if c < 3 else gcol("kv_latent_norm", c - 3)
                dve.scalar_tensor_tensor(Ll[:, c], bank[1 + c // 2][:, c % 2 * T:(c % 2 + 1) * T], gain, Lh[:, c].bitcast(F32),
                                         ALU.mult, ALU.subtract).then_inc(S("lt_lo"), 1)
            lo_upto("kvup")
            dve.wait_ge(*reach("ld_pb", 16 * len(pb_list)))
            dve_head_sums("hq", MH, QK)
            dve_head_sums("hk", MH, QK)
            lo_upto("gate1")
            dve_head_scale("hq", Q1, MH, QK, "q_head_norm")
            dve.wait_ge(*reach("rope1", 2))
            dve_rope("hq", Q1, MH, NOPE, ROPE // 2, COS1, SIN1)
            lo_upto("gate2")
            dve_head_scale("hk", K1[:], MH, QK, "k_head_norm")
            dve.wait_ge(*reach("hq_turn", 6))
            dve_rope("hk", K1[:], MH, NOPE, ROPE // 2, COS1, SIN1)
            for j in range(4):
                dve.wait_ge(*reach("kt_tr", j + 1))
                dve.tensor_copy(KT1[:, 2 * j:2 * j + 2].rearrange("p h n -> p (h n)"), bank[(6, 7, 0, 1)[j]][0:QK, :]).then_inc(S("kt_ev"), 1)
            for i in range(8 + 6):
                if i < 8:
                    lo_upto(f"gate{min(7, 3 + i)}")
                    dve.wait_ge(*reach("sb_l", 3 * i + 3))
                    if i >= 2:
                        dve.wait_ge(*reach("sb_t", i - 1))
                    dve.scalar_tensor_tensor(aw[:, 2 + i % 2], bank[i % 4][:, 0:384], 0.0, aw[:, i % 2], ALU.max,
                                             ALU.add).then_inc(S("sb_sp"), 1)
                h = i - 2
                if 0 <= h < 8:
                    dve.wait_ge(*reach("sb_t", h + 1))
                    if h >= 2:
                        dve.wait_ge(*reach("sb_av", h - 1))
                    dve.scalar_tensor_tensor(aw[:, 4 + h % 2], bank[h % 4][:, 0:384], 0.0, const("earlier_bias"), ALU.min,
                                             ALU.add).then_inc(S("sb_m"), 1)
                h = i - 5
                if h >= 0 and h % 2 == 1:
                    dve.wait_ge(*reach("os_hi", h // 2 + 1))
                    dve.tensor_tensor(OSl[:, h // 2], bank[4 + (h // 2) % 2][:, 0:T], OSh[:, h // 2].bitcast(F32),
                                      ALU.subtract).then_inc(S("os_lo"), 1)
            lo_upto("mla0")
            dve.wait_ge(*reach("sb_av", 8))
            dve_attention("mla", MH, const("causal"), QK ** -0.5, OMh, OMl)
            for q in range(4):
                lo_upto(f"sbr{q // 2}")
                used(dve, f"sbr{q // 2}")
                dve.wait_ge(*reach("gsig", 4))
                ga, gb = (GT[:, 8 * k + 2 * q:8 * k + 2 * q + 2].rearrange("p c n -> p (c n)") for k in range(2))
                dve.tensor_tensor(ga, ga, bank[q][:, :], ALU.mult).then_inc(S("mg_a"), 1)
                dve.tensor_tensor(gb, gb, bank[4 + q][:, :], ALU.mult).then_inc(S("mg_b"), 1)
                dve.wait_ge(*reach("mg_b", q + 1))
                dve.tensor_tensor(sgh[:, q % 2], ga, gb, ALU.add).then_inc(S("mg_s"), 1)
                dve.wait_ge(*reach("mg_hi", q + 1))
                u = slice(2 * q, 2 * q + 2)
                dve.tensor_tensor(Ul[:, u].rearrange("p c n -> p (c n)"), sgh[:, q % 2], Uh[:, u].rearrange("p c n -> p (c n)").bitcast(F32),
                                  ALU.subtract).then_inc(S("mg_lo"), 1)
            for i in range(4):
                lo_upto(f"wout{i}")
                used(dve, f"wout{i}")
                xs_ = X[:, :, i * 256:(i + 1) * 256]
                dve.tensor_tensor(xs_, xs_, bank[i].rearrange("p (t n) -> p t n", t=NT), ALU.add).then_inc(S("x2"), 1)
            dve.wait_ge(*reach("x2", 4))
            dve_norm("n3", "ffn2_norm")
            dve_ffn("ffn2", NF)
            dve.wait_ge(*reach("p_hi", 1))
            dve.tensor_tensor(OMl[:, 0:2].rearrange("p c n -> p (c n)"), bank[6][:, :],
                              OMh[:, 0:2].rearrange("p c n -> p (c n)").bitcast(F32), ALU.subtract).then_inc(S("p_lo"), 1)
            dve.wait_ge(*reach("ffn2_x", 4))
            dve_norm("n4", "ple_norm")
            for c in range(4):
                lo_upto(f"pgate{c}")
                dve.wait_ge(*reach("pg", c + 1))
                dve.wait_ge(*reach("pp_ev", c + 1))
                g3 = sgh[:, c % 2].rearrange("p (t n) -> p t n", t=NT)
                dve.tensor_tensor(g3, g3, PP[:, :, c * 256:(c + 1) * 256], ALU.mult).then_inc(S("pm"), 1)
                dve.wait_ge(*reach("pm", c + 1))
                xs_ = X[:, :, c * 256:(c + 1) * 256]
                dve.tensor_tensor(xs_, xs_, g3, ALU.add).then_inc(S("x4"), 1)

            dve.wait_ge(*reach("x4", 4))
            dve_norm("n5", "attn_norm_2")
            lo_upto("dt")
            dve.wait_ge(*reach("b2_ev", 10))
            cos2, sin2 = (const(n).rearrange("p (t d) -> p t d", t=NT) for n in ("cos2", "sin2"))
            ik4 = IKW[:, :, 0:HD].unsqueeze(2)
            R2 = HD // 4 // 2
            dve_head_sums("ik", 1, HD)
            dve_head_sums("k2", KVH2, HD)
            dve_head_sums("q2", H2, HD)
            iws = stat("iws", NT * IH).rearrange("p (t h) -> p t h", t=NT)
            dve.tensor_scalar(iws, IKW[:, :, HD:], IH ** -0.5, None, ALU.mult).then_inc(S("iws"), 1)
            dve.tensor_tensor(ssm[:, 0:2], ssm[:, 0:2], pb("dt_bias_2").unsqueeze(1).to_broadcast([P, NT, SH]), ALU.add).then_inc(S("dt_x"), 1)
            dve.wait_ge(*reach("q2_red", 2))
            dve_rope("iq", IQ[:], IH, 0, R2, cos2, sin2)
            dve_head_scale("ik", ik4, 1, HD, "idx_k_norm_2")
            dve.wait_ge(*reach("iq_turn", 6))
            dve_rope("ik", ik4, 1, 0, R2, cos2, sin2)
            dve.wait_ge(*reach("ik_turn", 6))
            dve.tensor_copy(IKd[:], IKW[:, :, 0:HD].unsqueeze(2).to_broadcast([P, NT, 2, HD])).then_inc(S("ikd"), 1)
            dve_head_scale("k2", K2[:], KVH2, HD, "k_norm_2")
            dve_rope("k2", K2[:], KVH2, 0, R2, cos2, sin2)
            dve.wait_ge(*reach("k2_turn", 6))
            dve.tensor_copy(K2d[:].rearrange("p t h a d -> p (t h) a d"),
                            K2[:].rearrange("p t h d -> p (t h) d").unsqueeze(2).to_broadcast([P, NT * KVH2, 2, HD])).then_inc(S("k2d"), 1)
            lo_upto("dt", 1)
            dve_head_scale("q2", Q2, H2, HD, "q_norm_2")
            dve_rope("q2", Q2, H2, 0, R2, cos2, sin2)
            dve.wait_ge(*reach("dt_l", 4))
            dve.scalar_tensor_tensor(ssm[:, 0:2], ssm[:, 0:2], 0.0, ssm[:, 2:4], ALU.max, ALU.add).then_inc(S("dt_d"), 1)
            dve.wait_ge(*reach("dt_d", 1))
            dve.scalar_tensor_tensor(ssm[:, 2:4], ssm[:, 0:2], -1.0, ssm[:, 8:9].to_broadcast([P, NT, SH]), ALU.mult,
                                     ALU.mult).then_inc(S("dt_d"), 1)
            lo_upto("xbc1")
            dve.wait_ge(*reach("ikt_tr", 1))
            dve.tensor_copy(IKT[:], bank[6][:, 0:T]).then_inc(S("ikt_ev"), 1)
            for i in range(2):
                dve.wait_ge(*reach("kt2_tr", i + 1))
                dve.tensor_copy(KT2[:, 2 * i:2 * i + 2].rearrange("p c n -> p (c n)"), bank[(7, 0)[i]][:, :]).then_inc(S("kt2_ev"), 1)
            for h in range(IH):
                dve.wait_ge(*reach("ix_r", h + 1))
                for t, (lo, hi) in enumerate(((0, P), (P, 3 * P))):
                    if h:
                        dve.wait_ge(*reach("ix_a", 2 * h - 1 + t))
                    else:
                        dve.wait_ge(*reach("iws", 1))
                    acc = const("admit") if h == 0 else SCO
                    dve.scalar_tensor_tensor(SCO[:, lo:hi], aw[:, h % 3, lo:hi], iws[:, t, h:h + 1], acc[:, lo:hi], ALU.mult,
                                             ALU.add).then_inc(S("ix_a"), 1)
            top8 = stat("top8", 16)
            dve.wait_ge(*reach("ix_a", 2 * IH))
            for r in range(TOPK // 8):
                for t, (lo, hi) in enumerate(((0, P), (P, 3 * P))):
                    if r:
                        dve.wait_ge(*reach("topk_taken", 2 * r - 1 + t))
                    dve.max(top8[:, 8 * t:8 * t + 8], SCO[:, lo:hi]).then_inc(S("topk_max"), 1)
                for t, (lo, hi) in enumerate(((0, P), (P, 3 * P))):
                    dve.wait_ge(*reach("topk_max", 2 * r + 1 + t))
                    dve.match_replace(SCO[:, lo:hi], top8[:, 8 * t:8 * t + 8], SCO[:, lo:hi], TAKEN).then_inc(S("topk_taken"), 1)
                if r == 0:
                    lo_upto("xbc2")
            dve.wait_ge(*reach("topk_taken", 2 * (TOPK // 8)))
            dve.tensor_scalar(SELB[:], SCO, TAKEN / 2, LOW, ALU.is_gt, ALU.mult).then_inc(S("selb"), 1)
            dve.wait_ge(*reach("selb", 1))

            def conv(j):
                for s_ in range(1, TAPS):
                    for c in range(2):
                        ch = 2 * j + c
                        dve.wait_ge(*reach("xb_ev", 3 * j + 3))
                        if s_ > 1:
                            dve.wait_ge(*reach("conv", 6 * j + 2 * (s_ - 2) + c + 1))
                        dve.scalar_tensor_tensor(XC[:, ch, s_:T], sgh[:, j % 2, c * T:(c + 1) * T - s_],
                                                 gcol("conv_w_2", (TAPS - 1 - s_) * NX + ch), XC[:, ch, s_:T], ALU.mult,
                                                 ALU.add).then_inc(S("conv"), 1)

            for j in range(4):
                lo_upto(f"xbc{j}", 0 if j < 3 else 1)
                conv(j)
            mx, nmx, sm, rs = (stat(f"att_{k}", 32) for k in range(4))
            for i in range(H2 + 5):
                if i < H2:
                    dve.wait_ge(*reach("dsa_s", i + 1))
                    if i >= 3:
                        dve.wait_ge(*reach("dsa_pt", i - 2))
                    for t, (lo, hi) in enumerate(((0, P), (P, 3 * P))):
                        dve.tensor_tensor_reduce(out=aw[:, i % 3, lo:hi], in0=bank[i % 3][:, lo:hi], in1=SELB[:, lo:hi],
                                                 scale=1.0, scalar=-3e38, op0=ALU.add, op1=ALU.max,
                                                 accum_out=mx[:, 2 * i + t:2 * i + t + 1]).then_inc(S("dsa_mx"), 1)
                    dve.wait_ge(*reach("dsa_mx", 2 * i + 2))
                    dve.tensor_scalar(nmx[:, 2 * i:2 * i + 2], mx[:, 2 * i:2 * i + 2], -HD ** -0.5, None,
                                      ALU.mult).then_inc(S("dsa_nm"), 1)
                if 1 <= i < H2 + 1:
                    h = i - 1
                    dve.wait_ge(*reach("dsa_exp", 2 * h + 2))
                    dve.reciprocal(rs[:, 2 * h:2 * h + 2], sm[:, 2 * h:2 * h + 2]).then_inc(S("dsa_rs"), 1)
                    dve.wait_ge(*reach("dsa_rs", h + 1))
                    for t, (lo, hi) in enumerate(((0, P), (P, 3 * P))):
                        dve.tensor_scalar(aw[:, h % 3, lo:hi], aw[:, h % 3, lo:hi], rs[:, 2 * h + t:2 * h + t + 1], None,
                                          ALU.mult).then_inc(S("dsa_pn"), 1)
                h = i - 4
                if h >= 0 and h % 2 == 1:
                    dve.wait_ge(*reach("dsa_ohi", h // 2 + 1))
                    dve.tensor_tensor(OAl[:, h // 2], bank[5 + (h // 2) % 2][:, 0:T], OAh[:, h // 2].bitcast(F32),
                                      ALU.subtract).then_inc(S("dsa_olo"), 1)
                if 4 + i // 2 < NX // 2 and i % 2 == 0:
                    lo_upto(f"xbc{4 + i // 2}")
                    conv(4 + i // 2)
            lo_upto("wa0")
            dve.wait_ge(*reach("acs_mm", 1))
            dve.tensor_copy(ssm[:, 4:7].rearrange("p a h -> p (a h)"), bank[5][:, 0:3 * SH]).then_inc(S("acs"), 1)
            dve.wait_ge(*reach("acs", 1))
            dve.tensor_tensor(ssm[:, 7], ssm[:, 6], ssm[:, 4], ALU.subtract).then_inc(S("acs"), 1)
            for t in range(NT):
                dve.wait_ge(*reach("cb_mm", t + 1))
                dve.tensor_tensor(CBM[:, t], bank[(6, 7)[t]].rearrange("p (g n) -> p g n", g=SG),
                                  const("upto").unsqueeze(1).to_broadcast([P, SG, P]), ALU.mult).then_inc(S("cbm"), 1)
            dve.wait_ge(*reach("ee", 1))
            dve.tensor_tensor(ssm[:, 7], ssm[:, 7], ssm[:, 0], ALU.mult).then_inc(S("fe"), 1)
            for u in range(9):
                if u < 8:
                    t, g = divmod(u, 4)
                    lo_upto(f"wa{u}" if u < 4 else f"g{u - 4}")
                    for k in range(2):
                        n = 2 * u + k
                        dve.wait_ge(*reach("seg_mm", n + 1))
                        if n >= 4:
                            dve.wait_ge(*reach("y_mm", (n - 4) // 2 + 1))
                        h0 = 8 * g + 4 * k
                        for h in range(4):
                            hc = slice(h * P, (h + 1) * P)
                            last = dve.tensor_scalar(EM(n)[:, hc], bank[n % 4][:, hc], ssm[:, 4 + t, h0 + h:h0 + h + 1], 0.0,
                                                     ALU.subtract, ALU.min)
                        last.then_inc(S("seg"), 1)
                    for k in range(2):
                        n = 2 * u + k
                        dve.wait_ge(*reach("seg_e", n + 1))
                        dve.wait_ge(*reach("cbm", 2))
                        e3 = EM(n).rearrange("p (h n) -> p h n", h=4)
                        dve.tensor_tensor(e3, e3, CBM[:, t, g].unsqueeze(1).to_broadcast([P, 4, P]), ALU.mult).then_inc(S("seg_m"), 1)
                if u >= 1:
                    v = u - 1
                    t, g = divmod(v, 4)
                    yv = XS[:, t, g * 512:(g + 1) * 512]
                    dve.wait_ge(*reach("xsd", v + 1))
                    dve.wait_ge(*reach("y_mm", v + 1))
                    dve.tensor_tensor(yv, yv, bank[4 + v % 2][:, :], ALU.add).then_inc(S("y"), 1)
                    if t:
                        n = 4 + 2 * g
                        if g:
                            dve.wait_ge(*reach("y", n))
                        dve.tensor_tensor(sgh[:, 0].rearrange("p (h n) -> p h n", h=8), bank[6].rearrange("p (h n) -> p h n", h=8),
                                          ssm[:, 9, 8 * g:8 * g + 8].unsqueeze(2).to_broadcast([P, 8, 64]), ALU.mult).then_inc(S("yo"), 1)
                        dve.wait_ge(*reach("yo", g + 1))
                        dve.wait_ge(*reach("y", n + 1))
                        dve.tensor_tensor(yv, yv, sgh[:, 0], ALU.add).then_inc(S("y"), 1)
            for c in range(8):
                lo_upto(f"z{c}")
                dve.wait_ge(*reach("z_s", c + 1))
                dve.wait_ge(*reach("y", 12))
                v = XS[:, :, c * 256:(c + 1) * 256]
                dve.tensor_tensor(v, v, sgh[:, c % 2].rearrange("p (t n) -> p t n", t=NT), ALU.mult).then_inc(S("yz"), 1)
            lo_upto("g4")
            dve.wait_ge(*reach("yg_r", 1))
            dve.wait_ge(*reach("yz", 8))
            for g in range(SG):
                for t in range(NT):
                    v = XS[:, t, g * 512:(g + 1) * 512]
                    dve.tensor_scalar(v, v, stat("yg", 8)[:, 4 * t + g:4 * t + g + 1], None, ALU.mult).then_inc(S("yn"), 1)
            lo_upto("g7")
            for j in range(8):
                dve.wait_ge(*reach("yt_hi", 2 * j + 2))
                for c in range(2):
                    dve.scalar_tensor_tensor(YTl[:, 2 * j + c], bank[j % 4][:, c * T:(c + 1) * T], gcol("ssd_norm_2", 2 * j + c),
                                             YTh[:, 2 * j + c].bitcast(F32), ALU.mult, ALU.subtract).then_inc(S("yt_lo"), 1)
            for q in range(4):
                lo_upto(f"ws{q}1")
                used(dve, f"ws{q}1")
                dve.wait_ge(*reach("g2sig", 4))
                ga, gb = (G2[:, 8 * k + 2 * q:8 * k + 2 * q + 2].rearrange("p c n -> p (c n)") for k in range(2))
                dve.tensor_tensor(ga, ga, BA[:, 2 * q:2 * q + 2].rearrange("p c n -> p (c n)"), ALU.mult).then_inc(S("m2_a"), 1)
                dve.tensor_tensor(gb, gb, bank[4 + q][:, :], ALU.mult).then_inc(S("m2_b"), 1)
                dve.wait_ge(*reach("m2_b", q + 1))
                dve.tensor_tensor(sgh[:, q % 2], ga, gb, ALU.add).then_inc(S("m2_s"), 1)
                dve.wait_ge(*reach("m2_hi", q + 1))
                u = slice(2 * q, 2 * q + 2)
                dve.tensor_tensor(Ul[:, u].rearrange("p c n -> p (c n)"), sgh[:, q % 2], Uh[:, u].rearrange("p c n -> p (c n)").bitcast(F32),
                                  ALU.subtract).then_inc(S("m2_lo"), 1)
            for i in range(4):
                lo_upto(f"wo{i}")
                used(dve, f"wo{i}")
                xs_ = X[:, :, i * 256:(i + 1) * 256]
                dve.tensor_tensor(xs_, xs_, bank[i].rearrange("p (t n) -> p t n", t=NT), ALU.add).then_inc(S("x5"), 1)
            dve.wait_ge(*reach("x5", 4))
            dve_norm("n6", "ffn_norm_2")
            lo_upto("re")
            used(dve, "re")
            n_r = [0]

            def rlink(ins):
                n_r[0] += 1
                ins.then_inc(S("route"), 1)
                dve.wait_ge(*reach("route", n_r[0]))

            tk = lambda b, n: bank[b].rearrange("p (t n) -> p t n", t=NT)[:, :, 0:n]
            bc = lambda v, axis, shape: v.unsqueeze(axis).to_broadcast(shape)
            gl, el = rt("gl", 8).rearrange("p (t g) -> p t g", t=NT), rt("el", 64).rearrange("p (t n) -> p t n", t=NT)
            rlink(dve.tensor_tensor(gl, tk(0, EG), bc(pb("b_route_group_2"), 1, [P, NT, EG]), ALU.add))
            rlink(dve.tensor_tensor(el, tk(1, NE), bc(pb("b_route_expert_2"), 1, [P, NT, NE]), ALU.add))
            gmax, gexp = rt("gmax", 2), rt("gexp", 8).rearrange("p (t g) -> p t g", t=NT)
            rlink(dve.tensor_reduce(gmax, gl, AX, ALU.max))
            dve.tensor_tensor(gexp, gl, bc(gmax, 2, [P, NT, EG]), ALU.subtract).then_inc(S("r_gl"), 1)

            def ranks(nm, v, n):
                a_, b_ = (rt(nm + x, NT * n * n).rearrange("p (t i j) -> p t i j", t=NT, i=n) for x in "ab")
                vj, vi = bc(v, 2, [P, NT, n, n]), bc(v, 3, [P, NT, n, n])
                before = const("before").rearrange("p (i j) -> p i j", i=EPG)[:, 0:n, 0:n]
                dve.tensor_tensor(a_, vj, vi, ALU.is_gt).then_inc(S("route"), 1)
                n_r[0] += 1
                rlink(dve.tensor_tensor(b_, vj, vi, ALU.is_equal))
                for t in range(NT):
                    dve.tensor_tensor(b_[:, t], b_[:, t], before, ALU.mult).then_inc(S("route"), 1)
                    n_r[0] += 1
                dve.wait_ge(*reach("route", n_r[0]))
                rlink(dve.tensor_tensor(a_, a_, b_, ALU.add))
                r_ = rt(nm + "r", NT * n).rearrange("p (t i) -> p t i", t=NT)
                rlink(dve.tensor_reduce(r_, a_, AX, ALU.add))
                return r_

            gr = ranks("g", gl, EG)
            oh = rt("oh", 8).rearrange("p (t g) -> p t g", t=NT)
            rlink(dve.tensor_scalar(oh, gr, 0.0, None, ALU.is_equal))
            e4 = rt("e4", 64).rearrange("p (t g e) -> p t g e", t=NT, g=EG)
            rlink(dve.tensor_tensor(e4, el.rearrange("p t (g e) -> p t g e", g=EG), bc(oh, 3, [P, NT, EG, EPG]), ALU.mult))
            ein = rt("ein", 16).rearrange("p (t e) -> p t e", t=NT)
            rlink(dve.tensor_reduce(ein, e4.rearrange("p t g e -> p t e g"), AX, ALU.add))
            er = ranks("e", ein, EPG)
            v01, picks = rt("v01", 4), []
            for k in range(2):
                pk = rt(f"pick{k}", 16).rearrange("p (t e) -> p t e", t=NT)
                rlink(dve.tensor_scalar(pk, er, float(k), None, ALU.is_equal))
                pe_ = rt(f"pv{k}", 16).rearrange("p (t e) -> p t e", t=NT)
                rlink(dve.tensor_tensor(pe_, pk, ein, ALU.mult))
                rlink(dve.tensor_reduce(v01[:, 2 * k:2 * k + 2], pe_, AX, ALU.add))
                picks.append(pk)
            dve.tensor_tensor(rt("d", 2), v01[:, 2:4], v01[:, 0:2], ALU.subtract).then_inc(S("r_d"), 1)
            dve.wait_ge(*reach("r_e", 2))
            den = rt("den", 4)
            rlink(dve.tensor_reduce(den[:, 0:2], gexp, AX, ALU.add))
            rlink(dve.tensor_scalar(den[:, 2:4], rt("d", 2), 1.0, None, ALU.add))
            rlink(dve.reciprocal(den, den))
            w01 = rt("w01", 4)
            rlink(dve.tensor_tensor(w01[:, 0:2], den[:, 0:2], den[:, 2:4], ALU.mult))
            rlink(dve.tensor_tensor(w01[:, 2:4], w01[:, 0:2], rt("d", 2), ALU.mult))
            for k in range(2):
                rlink(dve.tensor_tensor(picks[k], picks[k], bc(w01[:, 2 * k:2 * k + 2], 2, [P, NT, EPG]), ALU.mult))
            rlink(dve.tensor_tensor(picks[0], picks[0], picks[1], ALU.add))
            dve.tensor_tensor(rt("comb", 64).rearrange("p (t g e) -> p t g e", t=NT, g=EG), bc(oh, 3, [P, NT, EG, EPG]),
                              bc(picks[0], 2, [P, NT, EG, EPG]), ALU.mult).then_inc(S("comb"), 1)
            dve.wait_ge(*reach("ct_tr", 1))
            dve.tensor_copy(CT, bank[2][0:NE, 0:T]).then_inc(S("ct_ev"), 1)
            dve_ffn("moe", NE, True)

        @block.gpsimd
        def _(_e):
            pool.memset(halves, -0.5).then_inc(S("halves"), 1)
            pool.wait_ge(*reach("halves", 1))
            pool_norm("n1")
            pool.wait_ge(*reach("zeroed", 1))
            pool_ffn("ffn1", NF)

            pool_norm("n2")
            pool.wait_ge(*reach("lat_ev", 3))
            pool.tensor_copy(K1[:, :, :, NOPE:QK], CQ[:, :, QL + KVL:C1_SQ].unsqueeze(2).to_broadcast([P, NT, MH, ROPE])).then_inc(S("krope"), 1)
            pool.wait_ge(*reach("lat_ss", 4))
            for k, n in enumerate((QL, KVL)):
                v = stat("lat", 4)[:, 2 * k:2 * k + 2]
                pool_rsqrt(v, v, n, "lat_r")
            pool_head_rsqrt("hq", MH, QK)
            pool_head_rsqrt("hk", MH, QK)
            for i in range(8):
                pool.wait_ge(*reach("sb_sp", i + 1))
                pool.tensor_tensor(aw[:, 2 + i % 2], aw[:, 2 + i % 2], const("earlier"), ALU.mult).then_inc(S("sb_spm"), 1)
            pool_norm("n3")
            pool_ffn("ffn2", NF)
            pool_norm("n4")

            pool_norm("n5")
            pool_head_rsqrt("ik", 1, HD)
            pool_head_rsqrt("k2", KVH2, HD)
            pool_head_rsqrt("q2", H2, HD)
            per_head = lambda v: v.unsqueeze(2).to_broadcast([P, 8, SP])
            for u in range(8):
                t, g = divmod(u, 4)
                hs = slice(8 * g, 8 * g + 8)
                x3 = XS[:, t, g * 512:(g + 1) * 512].rearrange("p (h d) -> p h d", h=8)
                pool.wait_ge(*reach("xs_ev", 8))
                pool.wait_ge(*reach("fe", 1))
                if u >= 2:
                    pool.wait_ge(*reach("y_mm", u - 1))
                pool.tensor_tensor(Xd[:, u % 2].rearrange("p (h d) -> p h d", h=8), x3, per_head(ssm[:, t, hs]), ALU.mult).then_inc(S("xd"), 1)
                if t == 0:
                    if u:
                        pool.wait_ge(*reach("st_mm", u))
                    pool.tensor_tensor(Xe[:].rearrange("p (h d) -> p h d", h=8), x3, per_head(ssm[:, 7, hs]), ALU.mult).then_inc(S("xe"), 1)
                pool.tensor_tensor(x3, x3, per_head(pb("d_skip_2")[:, hs]), ALU.mult).then_inc(S("xsd"), 1)
            pool.wait_ge(*reach("yg_ss", 8))
            pool_rsqrt(stat("yg", 8), stat("yg", 8), DI // SG, "yg_r")
            pool_norm("n6")
            pool.wait_ge(*reach("ld_comb", 16))
            pool_ffn("moe", NE, True)

        @block.tensor
        def _(_e):
            pe.wait_ge(*reach("ld_const", 16))
            pe.wait_ge(*reach("ld_rows", 16 * (len(gain_rows) + 1)))
            for j, (rows, nr) in enumerate(((rows1, n_rows1), (rows2, n_rows2))):
                claim(j, "gains", j + 1)
                pe.transpose(bank[j][:, 0:nr], rows[0:nr, :], ident[0:nr, 0:nr]).then_inc(S("rows_tr"), 1)
            pe_norm("n1")
            pe.wait_ge(*reach("zeroed", 1))
            pe_ffn("ffn1", NF)

            pe_norm("n2")
            for i in range(3):
                s_ = need(f"lat{i}")
                claim(i, "lat_ev", i + 1)
                by_token(s_, i, Uh, Ul, KD, slabs[s_][2]).then_inc(S("slab_used"), 1)
            for j, nm in enumerate(("sq", "sk")):
                for i in range(2):
                    s_ = need(f"{nm}{i}")
                    claim(3 + 2 * j + i, "sqk_ev", 2 * j + i + 1)
                    by_feature(s_, 3 + 2 * j + i, Uh, Ul, KD, 256).then_inc(S("slab_used"), 1)
            for i in range(2):
                s_ = need(f"sv{i}")
                claim((7, 0)[i], "sv_ev", i + 1)
                by_token(s_, (7, 0)[i], Uh, Ul, KD, 256).then_inc(S("slab_used"), 1)
            pe.wait_ge(*reach("lat_n", 4))
            for c in range(5):
                if c % 2 == 0:
                    claim(1 + c // 2, "lt_lo", min(5, c + 2))
                for t in range(NT):
                    last = pe.transpose(bank[1 + c // 2][:, c % 2 * T + t * P:c % 2 * T + (t + 1) * P], CQ[:, t, c * P:(c + 1) * P], ident)
                if c in (1, 3, 4):
                    last.then_inc(S("lt_tr"), 1)
            pe.wait_ge(*reach("lt_lo", 5))
            for i in range(2):
                s_ = need(f"qup{i}")
                for t in range(NT):
                    b = 4 + t if i == 0 else t
                    claim(b, "q_ev", 2 * i + t + 1)
                    last = by_token(s_, b, Lh, Ll, 3, 384, tiles=[t])
                last.then_inc(S("slab_used"), 1)
            s_ = need("kvup")
            for t in range(NT):
                for half in range(2):
                    b = (2, 3, 6, 7)[2 * t + half]
                    claim(b, "kv_ev", 2 * (2 * t + half) + 2)
                    last = by_token(s_, b, Lh, Ll, 2, 1024, k0=3, c0=half * 512, c1=(half + 1) * 512, tiles=[t])
            last.then_inc(S("slab_used"), 1)

            def gate(g, b):
                s_ = need(f"gate{g}")
                claim(b, "gate_ev", g + 1)
                by_feature(s_, b, Uh, Ul, KD, 256).then_inc(S("slab_used"), 1)

            for g in range(3):
                gate(g, (4, 5, 4)[g])
            for nm, buf, banks, done in (("hq", Q1, (0, 1, 2, 3), "qt"), ("hk", K1[:], (6, 7, 0, 1), "kt")):
                pe.wait_ge(*reach(nm + "_turn", 6))
                for j in range(4):
                    claim(banks[j], done + "_ev", j + 1)
                    for h in range(2):
                        for t in range(NT):
                            last = pe.transpose(bank[banks[j]][0:QK, h * T + t * P:h * T + (t + 1) * P], buf[:, t, 2 * j + h], ident)
                    last.then_inc(S(done + "_tr"), 1)

            pe.wait_ge(*reach("sqk_ev", 4))
            pe.wait_ge(*reach("sv_ev", 2))
            for i in range(8 + 4):
                if i < 8:
                    claim(i % 4, "sb_m", i + 1)
                    rows, c = slice(64 * (i % 2), 64 * (i % 2) + 64), i // 2
                    pe.matmul(bank[i % 4][:, 0:T], skT[rows, c, 0:P], sqT[rows, c, :], start=True, stop=True, skip_group_check=True)
                    pe.matmul(bank[i % 4][:, T:3 * P], skT[rows, c, P:T], sqT[rows, c, P:T], start=False, stop=True,
                              skip_group_check=True).then_inc(S("sb_z"), 1)
                h = i - 2
                if 0 <= h < 8:
                    pe.wait_ge(*reach("sb_spm", h + 1))
                    b, sp_ = bank[h % 4], aw[:, 2 + h % 2]
                    pe.matmul(b[:, 0:T], const("neg_from"), sp_[:, 0:T], start=False, stop=True, skip_group_check=True)
                    pe.matmul(b[:, P:T], const("neg_ones"), sp_[:, T:3 * P], start=False, stop=True, skip_group_check=True)
                    pe.matmul(b[:, T:3 * P], const("neg_from"), sp_[:, T:3 * P], start=False, stop=True,
                              skip_group_check=True).then_inc(S("sb_t"), 1)
                h = i - 4
                if h >= 0:
                    b = 4 + (h // 2) % 2
                    if h % 2 == 0:
                        claim(b, "os_lo", h // 2 + 1)
                    pe.wait_ge(*reach("sb_a", h + 1))
                    o, w_ = bank[b][64 * (h % 2):64 * (h % 2) + 64, 0:T], aw[:, 4 + h % 2]
                    f = slice(h * 64, (h + 1) * 64)
                    pe.matmul(o, sv[:, 0, f], w_[:, 0:T], start=True, stop=False, skip_group_check=True)
                    pe.matmul(o[:, P:T], sv[:, 1, f], w_[:, T:3 * P], start=False, stop=True, skip_group_check=True).then_inc(S("sb_av"), 1)
                if i < 5:
                    gate(3 + i, 6 + i % 2)
            pe.wait_ge(*reach("qt_ev", 4))
            pe.wait_ge(*reach("kt_ev", 4))
            pe.wait_ge(*reach("kv_ev", 8))
            pe_attention("mla", MH, lambda h: QT1[:, h], lambda h: KT1[:, h], lambda h, t: V1[:, t, h])
            for j in range(2):
                for nm, oh, ol, b0, done in (("mla", OMh, OMl, 0, "mg_a"), ("sbr", OSh, OSl, 4, "mg_b")):
                    pe.wait_ge(*reach("mla_olo" if nm == "mla" else "os_lo", 4))
                    s_ = need(f"{nm}{j}")
                    for q in range(2):
                        claim(b0 + 2 * j + q, done, 2 * j + q + 1)
                        last = by_feature(s_, b0 + 2 * j + q, oh, ol, 4, 512, n0=2 * q, n1=2 * q + 2)
                    last.then_inc(S("slab_used"), 1)
            pe.wait_ge(*reach("mg_lo", 4))
            for i in range(4):
                s_ = need(f"wout{i}")
                claim(i, "x2", i + 1)
                by_token(s_, i, Uh, Ul, KD, 256).then_inc(S("slab_used"), 1)
            pe_norm("n3")
            pe_ffn("ffn2", NF)
            pe.wait_ge(*reach("ld_p", 16))
            claim(6, "p_lo", 1)
            for c in range(2):
                for t in range(NT):
                    last = pe.transpose(bank[6][:, c * T + t * P:c * T + (t + 1) * P], aw[:, t, c * P:(c + 1) * P], ident)
            last.then_inc(S("p_tr"), 1)
            pe_norm("n4")
            pe.wait_ge(*reach("p_lo", 1))
            s_ = need("pproj")
            for c in range(4):
                claim(c, "pp_ev", c + 1)
                last = by_token(s_, c, OMh, OMl, 2, 1024, c0=c * 256, c1=(c + 1) * 256)
            last.then_inc(S("slab_used"), 1)
            for c in range(4):
                s_ = need(f"pgate{c}")
                claim(4 + c, "pg", c + 1)
                by_token(s_, 4 + c, Uh, Ul, KD, 256).then_inc(S("slab_used"), 1)

            pe_norm("n5")
            for n, (nm, b) in enumerate((("q0", 0), ("q1", 1), ("q2", 2), ("q3", 3), ("k", 4), ("v", 5), ("iq0", 6), ("iq1", 7),
                                         ("ik", 0), ("dt", 1))):
                s_ = need(nm)
                claim(b, "b2_ev", n + 1)
                by_token(s_, b, Uh, Ul, KD, slabs[s_][2]).then_inc(S("slab_used"), 1)

            def xbc(j):
                s_ = need(f"xbc{j}")
                claim(xbc_bank(j), "xb_ev", 3 * j + 3)
                by_feature(s_, xbc_bank(j), Uh, Ul, KD, 256).then_inc(S("slab_used"), 1)

            def pairs(nm, src, n, banks, done, tr):
                for j in range(n // 2):
                    claim(banks[j], done, j + 1)
                    for c in range(2):
                        for t in range(NT):
                            last = pe.transpose(bank[banks[j]][:, c * T + t * P:c * T + (t + 1) * P], src(t, 2 * j + c), ident)
                    last.then_inc(S(tr), 1)

            xbc(0)
            pe.wait_ge(*reach("iq_turn", 6))
            pairs("iq", lambda t, c: IQ[:, t, 2 * c:2 * c + 2].rearrange("p h d -> p (h d)"), 4, (4, 5), "iqt_ev", "iqt_tr")
            pe.wait_ge(*reach("ikd", 1))
            claim(6, "ikt_ev", 1)
            for t in range(NT):
                last = pe.transpose(bank[6][:, t * P:(t + 1) * P], IKd[:, t].rearrange("p a d -> p (a d)"), ident)
            last.then_inc(S("ikt_tr"), 1)
            pe.wait_ge(*reach("k2d", 1))
            pairs("k", lambda t, c: K2d[:, t, c].rearrange("p a d -> p (a d)"), 4, (7, 0), "kt2_ev", "kt2_tr")
            xbc(1)
            pe.wait_ge(*reach("q2_turn", 6))
            pairs("q", lambda t, c: Q2[:, t, 2 * c:2 * c + 2].rearrange("p h d -> p (h d)"), 8, (1, 4, 5, 6), "qt2_ev", "qt2_tr")
            pe.wait_ge(*reach("iqt_ev", 2))
            pe.wait_ge(*reach("ikt_ev", 1))
            for h in range(IH):
                b, rows = (7, 0, 1, 4)[h % 4], slice(64 * (h % 2), 64 * (h % 2) + 64)
                claim(b, "ix_r", h + 1)
                q_, k_ = IQT[rows, h // 2], IKT[rows, :]
                pe.matmul(bank[b][:, 0:P], q_[:, 0:P], k_[:, 0:P], start=True, stop=True, skip_group_check=True)
                pe.matmul(bank[b][:, P:3 * P], q_[:, P:T], k_, start=False, stop=True, skip_group_check=True).then_inc(S("ix_s"), 1)
            xbc(2)
            xbc(3)
            pe.wait_ge(*reach("qt2_ev", 4))
            pe.wait_ge(*reach("kt2_ev", 2))
            half = lambda h: slice(64 * (h % 2), 64 * (h % 2) + 64)
            for i in range(H2 + 3):
                if i < H2:
                    claim(i % 3, "dsa_mx", 2 * i + 2)
                    b, q_, k_ = bank[i % 3], QT2[half(i), i // 2], KT2[half(i), i // 4]
                    pe.matmul(b[:, 0:P], q_[:, 0:P], k_[:, 0:P], start=True, stop=True, skip_group_check=True)
                    pe.matmul(b[:, P:3 * P], q_[:, P:T], k_, start=False, stop=True, skip_group_check=True).then_inc(S("dsa_s"), 1)
                if 2 <= i < H2 + 2:
                    h = i - 2
                    claim(3 + h % 2, "dsa_ptc", h + 1)
                    pe.wait_ge(*reach("dsa_pn", 2 * h + 2))
                    for k in range(3):
                        last = pe.transpose(bank[3 + h % 2][:, k * P:(k + 1) * P], aw[:, h % 3, k * P:(k + 1) * P], ident)
                    last.then_inc(S("dsa_pt"), 1)
                if i >= 3:
                    h = i - 3
                    b = 5 + (h // 2) % 2
                    if h % 2 == 0:
                        claim(b, "dsa_olo", h // 2 + 1)
                    pe.wait_ge(*reach("dsa_ptc", h + 1))
                    o, f = bank[b][half(h), 0:T], slice(h // 4 * HD, (h // 4 + 1) * HD)
                    pe.matmul(o, V2[:, 0, f], aw[:, 3 + h % 2, 0:T], start=True, stop=False, skip_group_check=True)
                    pe.matmul(o[:, P:T], V2[:, 1, f], aw[:, 3 + h % 2, T:3 * P], start=False, stop=True,
                              skip_group_check=True).then_inc(S("dsa_av"), 1)
                if 4 + i // 2 < NX // 2 and i % 2 == 0:
                    xbc(4 + i // 2)

            pe.wait_ge(*reach("dt_d", 2))
            claim(5, "acs", 1)
            pe.matmul(bank[5][:, 0:SH], const("upto"), ssm[:, 2], start=True, stop=True, skip_group_check=True)
            pe.matmul(bank[5][:, SH:2 * SH], const("upto"), ssm[:, 3], start=False, stop=True, skip_group_check=True)
            pe.matmul(bank[5][:, 2 * SH:3 * SH], const("ones"), ssm[:, 2], start=False, stop=True,
                      skip_group_check=True).then_inc(S("acs_mm"), 1)
            pe.wait_ge(*reach("xc", 6))
            for t in range(NT):
                claim(6 + t, "cbm", t + 1)
                tk_ = slice(t * P, (t + 1) * P)
                for g in range(SG):
                    last = pe.matmul(bank[6 + t][:, g * P:(g + 1) * P], XC[:, 16 + g, tk_], XC[:, 20 + g, tk_], start=g == 0,
                                     stop=True, skip_group_check=True)
                last.then_inc(S("cb_mm"), 1)
            for j in range(8):
                claim(j % 4, "xs_ev", j + 1)
                for t in range(NT):
                    for c in range(2):
                        last = pe.transpose(bank[j % 4][:, t * T + c * P:t * T + (c + 1) * P], XC[:, 2 * j + c, t * P:(t + 1) * P], ident)
                last.then_inc(S("xs_tr"), 1)
            claim(4, "bt_ev", 1)
            for g in range(SG):
                last = pe.transpose(bank[4][:, g * P:(g + 1) * P], XC[:, 16 + g, 0:P], ident)
            last.then_inc(S("bt_tr"), 1)
            for u in range(9):
                if u < 8:
                    t, g = divmod(u, 4)
                    for k in range(2):
                        n = 2 * u + k
                        claim(n % 4, "seg", n + 1)
                        for h in range(4):
                            col = ssm[:, 2 + t, 8 * g + 4 * k + h:8 * g + 4 * k + h + 1].to_broadcast([P, P])
                            last = pe.matmul(bank[n % 4][:, h * P:(h + 1) * P], col, const("upto"), start=h == 0, stop=True,
                                             skip_group_check=True)
                        last.then_inc(S("seg_mm"), 1)
                    if t == 0:
                        claim(6, "st_ev", g + 1)
                        pe.wait_ge(*reach("bt_ev", 1))
                        pe.wait_ge(*reach("xe", g + 1))
                        pe.matmul(bank[6][:, :], BTM[:, g], Xe[:], start=True, stop=True, skip_group_check=True).then_inc(S("st_mm"), 1)
                    nm = f"wa{u}" if u < 4 else f"g{u - 4}"
                    pe.wait_ge(*reach("dsa_olo", 8))
                    s_ = need(nm)
                    claim(7, "side_ev", u + 1)
                    src = (OAh, OAl) if u < 4 else (Uh, Ul)
                    by_feature(s_, 7, *src, KD, 256).then_inc(S("slab_used"), 1)
                if u >= 1:
                    v = u - 1
                    t, g = divmod(v, 4)
                    if t:
                        claim(6, "yo", g + 1)
                        pe.wait_ge(*reach("st_ev", 4))
                        pe.matmul(bank[6][:, :], XC[:, 20 + g, P:T], ST[:, g], start=True, stop=True, skip_group_check=True)
                    claim(4 + v % 2, "y", v + 1 if t == 0 else 4 + 2 * g + 1)
                    pe.wait_ge(*reach("seg_m", 2 * v + 2))
                    pe.wait_ge(*reach("xd", v + 1))
                    for h in range(8):
                        last = pe.matmul(bank[4 + v % 2][:, h * SP:(h + 1) * SP], EM(2 * v + h // 4)[:, h % 4 * P:(h % 4 + 1) * P],
                                         Xd[:, v % 2, h * SP:(h + 1) * SP], start=h == 0, stop=True, skip_group_check=True)
                    last.then_inc(S("y_mm"), 1)
            for c in range(8):
                s_ = need(f"z{c}")
                claim(c % 4, "z_s", c + 1)
                by_token(s_, c % 4, Uh, Ul, KD, 256).then_inc(S("slab_used"), 1)
            for g in range(4, 8):
                s_ = need(f"g{g}")
                claim(4 + g % 4, "g2_ev", g - 3)
                by_feature(s_, 4 + g % 4, Uh, Ul, KD, 256).then_inc(S("slab_used"), 1)
            for j in range(8):
                claim(j % 4, "yt_lo", 2 * j + 2)
                for c in range(2):
                    ch = 2 * j + c
                    for t in range(NT):
                        pe.wait_ge(*reach("yn", 2 * (ch // 4) + t + 1))
                        last = pe.transpose(bank[j % 4][:, c * T + t * P:c * T + (t + 1) * P], XS[:, t, ch * P:(ch + 1) * P], ident)
                last.then_inc(S("yt_tr"), 1)
            pe.wait_ge(*reach("yt_lo", 16))
            for q in range(4):
                claim(4 + q, "m2_b", q + 1)
                for k in range(2):
                    s_ = need(f"ws{q}{k}")
                    by_feature(s_, 4 + q, YTh, YTl, KD, 256, k0=KD * k, start=k == 0, stop=k == 1).then_inc(S("slab_used"), 1)
            pe.wait_ge(*reach("m2_lo", 4))
            for i in range(4):
                s_ = need(f"wo{i}")
                claim(i, "x5", i + 1)
                by_token(s_, i, Uh, Ul, KD, 256).then_inc(S("slab_used"), 1)
            pe_norm("n6")
            for nm, b in (("rg", 0), ("re", 1)):
                s_ = need(nm)
                claim(b, "comb", 1)
                by_token(s_, b, Uh, Ul, KD, slabs[s_][2]).then_inc(S("slab_used"), 1)
            pe.wait_ge(*reach("comb", 1))
            claim(2, "ct_ev", 1)
            for t in range(NT):
                last = pe.transpose(bank[2][0:NE, t * P:(t + 1) * P], rt("comb", 64)[:, t * NE:(t + 1) * NE], ident)
            last.then_inc(S("ct_tr"), 1)
            pe_ffn("moe", NE)


_INS = ["x", "p", "positions", "ffn1_norm", "ffn1_w_in", "ffn1_w_out", "mix_norm", "w_in", "q_latent_norm", "w_q_up",
        "kv_latent_norm", "w_kv_up", "q_head_norm", "k_head_norm", "w_branch_mla", "w_branch_sb", "w_out", "ffn2_norm",
        "ffn2_w_in", "ffn2_w_out", "ple_norm", "w_ple_gate", "w_ple_proj", "attn_norm_2", "w_in_2", "q_norm_2",
        "k_norm_2", "idx_k_norm_2", "conv_w_2", "conv_b_2", "dt_bias_2", "a_log_2", "d_skip_2", "ssd_norm_2",
        "w_attn_branch_2", "w_ssd_branch_2", "w_out_2", "ffn_norm_2", "w_route_group_2", "b_route_group_2",
        "w_route_expert_2", "b_route_expert_2", "w_gate_2", "w_up_2", "w_down_2"]


def kernel(**inputs):
    from concourse import bacc as _bacc
    from concourse.bass_utils import run_bass_kernel_spmd
    nc = _bacc.Bacc("TRN2", target_bir_lowering=False, num_devices=1)
    arrays = {"in_" + name: np.ascontiguousarray(inputs[name]) for name in _INS}
    arrays["const"] = constants()
    a = {name.removeprefix("in_"): nc.dram_tensor(name, v.shape, mybir.dt.from_np(v.dtype), kind="ExternalInput").ap()
         for name, v in arrays.items()}
    out = nc.dram_tensor("out", [1, T, D], F32, kind="ExternalOutput").ap()
    scratch = nc.dram_tensor("scratch", [NE, T], F32, kind="Internal").ap()
    two_blocks(nc, a, out, scratch)
    if not nc.is_finalized():
        nc.finalize()
    res = run_bass_kernel_spmd(nc, [arrays], core_ids=[0])
    return res.results[0]["out"]
```

```python
from contextlib import ExitStack

import numpy as np

import concourse.bass as bass
from concourse import mybir

ALU = mybir.AluOpType
ACT = mybir.ActivationFunctionType
F32 = mybir.dt.float32
F32R = mybir.dt.float32r
I32 = mybir.dt.int32
AX = mybir.AxisListType.X

P = 128
T = 256
NT = T // P
D = 1024
KD = D // P
FF = 2816
NF = FF // 256
PLE = 256
QL, KVL, ROPE = 384, 256, 32
MH, NOPE, QK = 8, 64, 96
SBW = 512
H2, KVH2, HD = 16, 4, 64
IH = 8
TOPK = 64
KCHUNK = 64
DI, SH, SP, SG, SN = 2048, 32, 64, 4, 128
NX = (DI + 2 * SG * SN) // P
TAPS = 4
NE, EG, EPG, EH = 32, 4, 8, 256
EPS = 1e-6
LOW = -1e30
FAR = 1000.0
TAKEN = -3e38

C1_SQ = QL + KVL + ROPE
C1_GATE = C1_SQ + 3 * SBW
C2_K = H2 * HD
C2_V = C2_K + KVH2 * HD
C2_IQ = C2_V + KVH2 * HD
C2_IK = C2_IQ + IH * HD
C2_Z = C2_IK + HD + IH
C2_XBC = C2_Z + DI
C2_DT = C2_XBC + NX * P
C2_GA = C2_DT + SH
C2_GB = C2_GA + D

NSLOT = 3
SLAB = 2048

CONST_AT = {}


def constants():
    j, i = np.arange(P)[:, None], np.arange(P)[None, :]
    wide = lambda a: np.broadcast_to(np.asarray(a, np.float64), (P, np.size(a)))
    ones, zeros = np.ones((P, P)), np.zeros((P, P))
    s = np.arange(T)[None, :]
    half = HD // 4 // 2
    inv2 = 500000.0 ** (-np.arange(half) * 2.0 / (2 * half))
    ang2 = [(np.float32(t * P + np.arange(P))[:, None] * inv2.astype(np.float32)[None, :]).astype(np.float64) for t in range(NT)]
    parts = [
        ("ident", np.eye(P)),
        ("upto", (j <= i) * 1.0),
        ("neg_from", (j >= i) * -1.0),
        ("neg_ones", -ones),
        ("ones", ones),
        ("causal", np.hstack([(i > j) * LOW, zeros, (i > j) * LOW])),
        ("earlier", np.hstack([(j < i) * 1.0, ones, (j < i) * 1.0])),
        ("earlier_bias", np.hstack([(j >= i) * LOW, zeros, (j >= i) * LOW])),
        ("admit", np.hstack([(s[:, :P] // KCHUNK > j // KCHUNK) * LOW, (s // KCHUNK > (j + P) // KCHUNK) * LOW])),
        ("invf", wide(10000.0 ** (-np.arange(0, ROPE, 2) / ROPE))),
        ("cos2", np.hstack([np.cos(a) for a in ang2])),
        ("sin2", np.hstack([np.sin(a) for a in ang2])),
        ("slot", wide(np.arange(P) - FAR)),
        ("group_base", wide(np.arange(EG) * EPG)),
        ("before", wide((np.arange(EPG)[None, :] < np.arange(EPG)[:, None]).ravel())),
    ]
    at = 0
    for name, a in parts:
        CONST_AT[name] = (at, a.shape[1])
        at += a.shape[1]
    return np.hstack([a for _, a in parts]).astype(np.float32)


NCONST = constants().shape[1]


def two_blocks(nc, a, out):
    with ExitStack() as ctx:
        def sb(name, shape, dt=F32, scope=ctx):
            return scope.enter_context(nc.sbuf_tensor("sb_" + name, shape, dt))

        bank = [ctx.enter_context(nc.psum_tensor(f"bank{i}", [P, 512], F32)) for i in range(8)]

        sems = {}

        norms = ("n1", "n2", "n3", "n4", "n5", "n6")
        ffns = (("ffn1", NF), ("ffn2", NF), ("moe", NE))
        heads = ("hq", "hk", "ik", "k2", "q2")
        turned = ("hq", "hk", "iq", "ik", "k2", "q2")
        attn = (("mla", MH), ("dsa", H2))
        shared = [[("norm_" + k, [(nm + "_" + k, c) for nm in norms]) for k, c in
                   (("ss", NT), ("tr", KD // 2), ("hi", KD), ("r", NT), ("xn", NT), ("lo", KD))],
                  [("ffn_" + k, [(nm + "_" + k, n) for nm, n in ffns]) for k in ("silu", "mul", "h", "hh")],
                  [("ffn_x", [("ffn1_x", 4), ("ffn2_x", 4)]), ("ffn_acc", [("ffn1_acc", 3), ("ffn2_acc", 3)])],
                  [("head_" + k, [(nm + "_" + k, c) for nm in heads]) for k, c in (("sq", NT), ("red", NT), ("r", 1), ("scaled", 2))],
                  [("head_turn", [(nm + "_turn", 6) for nm in turned])],
                  [("attn_" + k, [(nm + "_" + k, c * n // 2) for nm, n in attn]) for k, c in
                   (("s", 2), ("mx", 4), ("nm", 2), ("exp", 4), ("rs", 2), ("pn", 4), ("pt", 2), ("ptc", 2), ("av", 2),
                    ("ohi", 1), ("olo", 1))],
                  [("merge_" + k, [("mg_" + k, 4), ("m2_" + k, 4)]) for k in ("a", "b", "s", "hi", "lo")],
                  [("gate_sig", [("gsig", 4), ("g2sig", 4)]),
                   ("q_tr", [("qt_tr", 4), ("qt2_tr", 4)]), ("q_out", [("qt_ev", 4), ("qt2_ev", 4)]),
                   ("k_tr", [("kt_tr", 4), ("kt2_tr", 2)]), ("k_out", [("kt_ev", 4), ("kt2_ev", 2)]),
                   ("resid", [("x2", 4), ("x4", 4), ("x5", 4)]),
                   ("act_out", [("lat_ev", 3), ("sqk_ev", 4), ("sv_ev", 2), ("q_ev", 4), ("kv_ev", 8), ("gate_ev", 8),
                                ("pp_ev", 4), ("b2_ev", 10)]),
                   ("scores", [("sb_z", 8), ("seg_mm", 16)]), ("logs", [("sb_sp", 8), ("seg", 16)]),
                   ("expo", [("sb_a", 8), ("seg_e", 16)]), ("masked", [("sb_m", 8), ("seg_m", 16)]),
                   ("values", [("sb_av", 8), ("y_mm", 8)]),
                   ("tr", [("lt_tr", 3), ("xs_tr", 8), ("yt_tr", 8)]),
                   ("t_hi", [("lt_hi", 5), ("yt_hi", 16)]), ("t_lo", [("lt_lo", 5), ("yt_lo", 16)])]]
        place = {}
        for sem, stages in sum(shared, []):
            base = 0
            for nm, c in stages:
                place[nm] = sem, base
                base += c

        def S(name):
            sem = place.get(name, (name, 0))[0]
            if sem not in sems:
                sems[sem] = ctx.enter_context(nc.semaphore(sem))
            return sems[sem]

        def reach(name, count):
            base = place.get(name, (name, 0))[1]
            return S(name), count + base if base else count

        raw = sb("raw", [P, NSLOT, SLAB])
        whi = sb("whi", [P, NSLOT, SLAB], F32R)
        wlo = sb("wlo", [P, NSLOT, SLAB], F32R)
        X = sb("X", [P, NT, D])
        Uh = sb("Uh", [P, KD, T], F32R)
        Ul = sb("Ul", [P, KD, T], F32R)
        xn = sb("xn", [P, NT, D])
        C = sb("C", [P, NCONST])
        G = sb("G", [P, 256])
        PB = sb("PB", [P, 520])
        st = sb("st", [P, 320])
        sgh = sb("sgh", [P, 2, 512])
        hh = sb("hh", [P, 512], F32R)
        hl = sb("hl", [P, 512], F32R)
        zero = sb("zero", [P, 512], F32R)
        with ExitStack() as pa:
            sb("beside", [P, 1024], F32, pa)
            hh_last = sb("hh_last", [P, 512], F32R, pa)
            hl_last = sb("hl_last", [P, 512], F32R, pa)
        aw = sb("aw", [P, 6, 384])
        rows1, rows2 = sgh[:, 0, 0:P], sgh[:, 0, P:2 * P]
        pos = sb("pos", [P, NT], I32)
        rope1 = sb("rope1", [P, 8, NT, ROPE // 2])
        COS1, SIN1 = rope1[:, 6], rope1[:, 7]

        def const(name, lo=0, hi=None):
            at, n = CONST_AT[name]
            return C[:, at + lo:at + (n if hi is None else hi)]

        ident = const("ident")

        stat_at = {}

        def stat(name, n):
            if name not in stat_at:
                stat_at[name] = sum(v[1] for v in stat_at.values())
                stat_at[name] = (stat_at[name], n)
            at, _ = stat_at[name]
            assert at + n <= 320
            return st[:, at:at + n]

        gain_rows = [("ffn1_norm", KD), ("mix_norm", KD), ("q_latent_norm", QL // P), ("kv_latent_norm", KVL // P),
                     ("ffn2_norm", KD), ("ple_norm", KD), ("attn_norm_2", KD), ("ffn_norm_2", KD),
                     ("ssd_norm_2", DI // P), ("conv_b_2", NX)]
        gain_at, at = {}, 0
        for name, n in gain_rows:
            gain_at[name] = at
            at += n
        n_rows1 = at
        gain_at["conv_w_2"] = P
        n_rows2 = TAPS * NX

        def gcol(name, i):
            return G[:, gain_at[name] + i:gain_at[name] + i + 1]

        pb_list = [("q_head_norm", QK), ("k_head_norm", QK), ("q_norm_2", HD), ("k_norm_2", HD), ("idx_k_norm_2", HD),
                   ("dt_bias_2", SH), ("a_log_2", SH), ("d_skip_2", SH), ("b_route_group_2", EG), ("b_route_expert_2", NE)]
        pb_at, at = {}, 0
        for name, n in pb_list:
            pb_at[name] = (at, n)
            at += n

        def pb(name):
            at, n = pb_at[name]
            return PB[:, at:at + n]

        with ExitStack() as p1:
            with ExitStack() as pa:
                CQ = sb("CQ", [P, NT, C1_SQ], F32, pa)
                Lh = sb("Lh", [P, 5, T], F32R, pa)
                Ll = sb("Ll", [P, 5, T], F32R, pa)
            GT = sb("GT", [P, 16, T], F32, p1)
            sqT = sb("sqT", [P, 4, T], F32, p1)
            skT = sb("skT", [P, 4, T], F32, p1)
            sv = sb("sv", [P, NT, SBW], F32, p1)
            K1 = sb("K1", [P, NT, MH, QK], F32, p1)
            V1 = sb("V1", [P, NT, MH, 64], F32, p1)
            QT1 = sb("QT1", [QK, MH, T], F32, p1)
            KT1 = sb("KT1", [QK, MH, T], F32, p1)
            OMh = sb("OMh", [P, 4, T], F32R, p1)
            OMl = sb("OMl", [P, 4, T], F32R, p1)
            OSh = sb("OSh", [P, 4, T], F32R, p1)
            OSl = sb("OSl", [P, 4, T], F32R, p1)
        with ExitStack() as p2:
            with ExitStack() as pa:
                OAh = sb("OAh", [P, 8, T], F32R, pa)
                OAl = sb("OAl", [P, 8, T], F32R, pa)
            G2 = sb("G2", [P, 16, T], F32, p2)
            ssm = sb("ssm", [P, 10, SH], F32, p2)
            with ExitStack() as pa:
                QT2 = sb("QT2", [P, H2 // 2, T], F32, pa)
                KT2 = sb("KT2", [P, KVH2, T], F32, pa)
                IQT = sb("IQT", [P, IH // 2, T], F32, pa)
                IKT = sb("IKT", [P, T], F32, pa)
                V2 = sb("V2", [P, NT, KVH2 * HD], F32, pa)
                SELB = sb("SELB", [P, 384], F32, pa)
            XS = sb("XS", [P, NT, DI], F32, p2)
            CBM = sb("CBM", [P, NT, SG, P], F32, p2)
            pad = sb("pad", [P, P], F32, p2)
            with ExitStack() as pa:
                IQ = sb("IQ", [P, NT, IH, HD], F32, pa)
                K2 = sb("K2", [P, NT, KVH2, HD], F32, pa)
                K2d = sb("K2d", [P, NT, KVH2, 2, HD], F32, pa)
                IKd = sb("IKd", [P, NT, 2, HD], F32, pa)
                IKW = sb("IKW", [P, NT, HD + IH], F32, pa)
            with ExitStack() as pa:
                XC = sb("XC", [P, NX, T], F32, pa)
                G2a = sb("G2a", [P, 8, T], F32, pa)
            with ExitStack() as pa:
                ST = sb("ST", [P, SG, 512], F32, pa)
                Xd = sb("Xd", [P, 2, 512], F32, pa)
                Xe = sb("Xe", [P, 512], F32, pa)
                BTM = sb("BTM", [P, SG, SN], F32, pa)
            with ExitStack() as pa:
                YTh = sb("YTh", [P, DI // P, T], F32R, pa)
                YTl = sb("YTl", [P, DI // P, T], F32R, pa)
        with ExitStack() as p3:
            PICK = sb("PICK", [P, NT, EG + 1, P], F32R, p3)
            PICKT = sb("PICKT", [P, EG + 1, T], F32R, p3)
            SUh = sb("SUh", [P, KD, EG, P], F32R, p3)
            SUl = sb("SUl", [P, KD, EG, P], F32R, p3)
            CW = sb("CW", [P, (EG + 1) * EPG, 1], F32, p3)
            Yh = sb("Yh", [P, D], F32R, p3)
            Yl = sb("Yl", [P, D], F32R, p3)
            PUT = sb("PUT", [P, 4, 512], F32, p3)
            XNh = sb("XNh", [P, NT, D], F32R, p3)
            OV = sb("OV", [P, 2], I32, p3)
        Q2 = xn[:, :, :].rearrange("p t (h d) -> p t h d", d=HD)
        BA = xn[:, :, :].rearrange("p t (c n) -> p (t c) n", n=T)
        SCO = aw[:, 5]
        XNl = Ul[:].rearrange("p (t c) n -> p t (c n)", t=NT)
        PP = GT[:, 0:8].rearrange("p (t a) n -> p t (a n)", t=NT)
        Q1 = xn[:, :, 0:MH * QK].rearrange("p t (h d) -> p t h d", d=QK)

        def view(name):
            w = a[name]
            return w[0].rearrange("(k p) n -> p k n", p=P)

        slab_of, slabs, loops = {}, [], {}

        def slab(name, src, kc, ncol):
            slab_of[name] = len(slabs)
            slabs.append((src, kc, ncol))

        def slab_loop(name, n, gate, up, down):
            slab_of[name] = len(slabs)
            loops[len(slabs)] = (n, gate, up, down)
            slabs.extend([(None, KD, 256)] * (3 * n))

        def ffn_loop(name, w_in, w_out):
            wi = a[w_in][0].rearrange("(k p) (h c n) -> h c p k n", p=P, h=2, n=256)
            wo = a[w_out][0].rearrange("(c k p) n -> c p k n", p=P, k=2)
            slab_loop(name, NF, lambda i: wi[0, i], lambda i: wi[1, i], lambda i: wo[i])

        ffn_loop("ffn1", "ffn1_w_in", "ffn1_w_out")
        w = view("w_in")
        for i, (lo, hi) in enumerate([(0, 256), (256, 512), (512, C1_SQ)]):
            slab(f"lat{i}", w[:, :, lo:hi], KD, hi - lo)
        for j, nm in enumerate(("sq", "sk", "sv")):
            for i in range(2):
                lo = C1_SQ + j * SBW + i * 256
                slab(f"{nm}{i}", w[:, :, lo:lo + 256], KD, 256)
        for i in range(2):
            slab(f"qup{i}", view("w_q_up")[:, :, i * 384:(i + 1) * 384], 3, 384)
        slab("kvup", view("w_kv_up"), 2, 1024)
        for i in range(8):
            slab(f"gate{i}", w[:, :, C1_GATE + i * 256:C1_GATE + (i + 1) * 256], KD, 256)
        for i in range(2):
            for nm, src in (("mla", "w_branch_mla"), ("sbr", "w_branch_sb")):
                slab(f"{nm}{i}", view(src)[:, :, i * 512:(i + 1) * 512], 4, 512)
        for i in range(4):
            slab(f"wout{i}", view("w_out")[:, :, i * 256:(i + 1) * 256], KD, 256)
        ffn_loop("ffn2", "ffn2_w_in", "ffn2_w_out")
        slab("pproj", view("w_ple_proj"), 2, 1024)
        for i in range(4):
            slab(f"pgate{i}", view("w_ple_gate")[:, :, i * 256:(i + 1) * 256], KD, 256)

        w2 = view("w_in_2")
        for i in range(4):
            slab(f"q{i}", w2[:, :, i * 256:(i + 1) * 256], KD, 256)
        for nm, lo, hi in (("k", C2_K, C2_V), ("v", C2_V, C2_IQ), ("iq0", C2_IQ, C2_IQ + 256), ("iq1", C2_IQ + 256, C2_IK)):
            slab(nm, w2[:, :, lo:hi], KD, hi - lo)
        slab("ik_dt", (w2[:, :, C2_IK:C2_Z], w2[:, :, C2_DT:C2_GA]), KD, C2_Z - C2_IK + SH)

        def gate_slab2(i):
            slab(f"g{i}", w2[:, :, C2_GA + i * 256:C2_GA + (i + 1) * 256], KD, 256)

        for i in range(NX // 2):
            slab(f"xbc{i}", w2[:, :, C2_XBC + i * 256:C2_XBC + (i + 1) * 256], KD, 256)
            if i == 3:
                gate_slab2(0)
                gate_slab2(1)
        gate_slab2(2)
        gate_slab2(3)
        for i in range(4):
            slab(f"wa{i}", view("w_attn_branch_2")[:, :, i * 256:(i + 1) * 256], KD, 256)
        gate_slab2(4)
        gate_slab2(5)
        for i in range(8):
            slab(f"z{i}", w2[:, :, C2_Z + i * 256:C2_Z + (i + 1) * 256], KD, 256)
        gate_slab2(6)
        gate_slab2(7)
        for i in range(4):
            for k in range(2):
                slab(f"ws{i}{k}", view("w_ssd_branch_2")[:, KD * k:KD * (k + 1), i * 256:(i + 1) * 256], KD, 256)
        for i in range(4):
            slab(f"wo{i}", view("w_out_2")[:, :, i * 256:(i + 1) * 256], KD, 256)
        slab("router", (view("w_route_group_2"), view("w_route_expert_2")), KD, EG + NE)
        experts = lambda nm, k: a[nm].rearrange("o g e (k p) n -> (o g e) p k n", p=P)
        wg, wu, wd = (experts(nm, 0) for nm in ("w_gate_2", "w_up_2", "w_down_2"))
        slab_loop("moe", NE, lambda e: wg[e], lambda e: wu[e], lambda e: wd[e])
        over = slab_of["moe"] + 3 * NE

        range_of_loops = {j for b, l in loops.items() for j in range(b, b + 3 * l[0])} | set(range(over, over + 3 * EPG))

        def parts(kc):
            return (0, (kc + 1) // 2), ((kc + 1) // 2, kc)

        def part_cols(i):
            kc, ncol = slabs[i][1:] if i not in range_of_loops else (2, SLAB // 2)
            return [slice(lo * ncol, hi * ncol) for lo, hi in parts(kc)]

        def load(sp, i, q=None, src=None):
            if src is None and isinstance(slabs[i][0], tuple):
                at = 0
                for h, v in enumerate(slabs[i][0]):
                    sp.wait_ge(*reach("lo_done", 2 * (i - NSLOT) + 2))
                    dst = raw[:, i % NSLOT, 0:KD * slabs[i][2]].rearrange("p (k n) -> p k n", k=KD)[:, :, at:at + v.shape[2]]
                    sp.dma_start(dst, v).then_inc(S(f"raw_full{i % NSLOT}{h}"), 16)
                    at += v.shape[2]
                return
            kc, ncol = (src.shape[1], src.shape[2]) if src is not None else slabs[i][1:]
            src = slabs[i][0] if src is None else src
            for h, (lo, hi) in enumerate(parts(kc)):
                if i >= NSLOT or q is not None:
                    n = h + 1 if part_cols(i) == part_cols(i - NSLOT) else 2
                    sp.wait_ge(*reach("lo_done", 2 * (i - NSLOT) + n + (0 if q is None else q * 6)))
                dst = raw[:, i % NSLOT, lo * ncol:hi * ncol].rearrange("p (k n) -> p k n", n=ncol)
                sp.dma_start(dst, src[:, lo:hi]).then_inc(S(f"raw_full{i % NSLOT}{h}"), 16)

        def split_hi(i, q=None):
            off = 0 if q is None else q
            for h, c in enumerate(part_cols(i)):
                if h == 0 and (i >= NSLOT or q is not None):
                    nc.scalar.wait_ge(*reach("slab_used", i - NSLOT + 1 + 3 * off))
                nc.scalar.wait_ge(*reach(f"raw_full{i % NSLOT}{h}", 16 * (i // NSLOT + 1) + 16 * off))
                if h == 0 and i not in range_of_loops and isinstance(slabs[i][0], tuple):
                    nc.scalar.wait_ge(*reach(f"raw_full{i % NSLOT}1", 16 * (i // NSLOT + 1)))
                nc.scalar.activation(whi[:, i % NSLOT, c], raw[:, i % NSLOT, c], ACT.Copy).then_inc(S("hi_done"), 1)

        def split_lo(i, q=None):
            off = 0 if q is None else q
            for h, c in enumerate(part_cols(i)):
                nc.vector.wait_ge(*reach("hi_done", 2 * i + h + 1 + 6 * off))
                nc.vector.tensor_tensor(wlo[:, i % NSLOT, c], raw[:, i % NSLOT, c], whi[:, i % NSLOT, c].bitcast(F32),
                                        ALU.subtract).then_inc(S("lo_done"), 1)

        nxt = {"hi": 0, "lo": 0}

        def hi_upto(name, k=0):
            n = min((slab_of[name] if isinstance(name, str) else name) + k + NSLOT, len(slabs))
            while nxt["hi"] < n:
                split_hi(nxt["hi"])
                nxt["hi"] += 1

        def lo_upto(name, k=0):
            n = min((slab_of[name] if isinstance(name, str) else name) + k + NSLOT, len(slabs))
            while nxt["lo"] < n:
                split_lo(nxt["lo"])
                nxt["lo"] += 1

        def used(eng, name, k=0):
            eng.wait_ge(*reach("slab_used", slab_of[name] + k + 1))

        pe, act, dve, pool = nc.tensor, nc.scalar, nc.vector, nc.gpsimd
        owner = [None] * 8

        def claim(b, sem, count):
            if owner[b] is not None:
                pe.wait_ge(*reach(owner[b][0], owner[b][1]))
            owner[b] = (sem, count)

        def mm3(o, lh, ll, rh, rl, start, stop):
            pe.matmul(o, lh, rh, start=start, stop=False, skip_group_check=True)
            pe.matmul(o, lh, rl, start=False, stop=False, skip_group_check=True)
            return pe.matmul(o, ll, rh, start=False, stop=stop, skip_group_check=True)

        def wslab(i, kc, ncol):
            sl = i % NSLOT
            v = lambda w: w[:, sl, 0:kc * ncol].rearrange("p (k n) -> p k n", n=ncol)
            return v(whi), v(wlo)

        fresh = []

        def chunk_order(kc, outs, xh):
            if fresh and xh is fresh[0][2]:
                stage, step, _ = fresh.pop()
                for k in range(kc):
                    pe.wait_ge(*reach(stage, k // step + 1))
                    for n in outs:
                        yield k, n
            else:
                for n in outs:
                    for k in range(kc):
                        yield k, n

        def by_feature(i, b, xh, xl, kc, ncol, k0=0, n0=0, n1=None, start=True, stop=True):
            wh, wl = wslab(i, kc, ncol)
            n1 = ncol // P if n1 is None else n1
            for k, n in chunk_order(kc, range(n0, n1), xh):
                f = slice(n * P, (n + 1) * P)
                last = mm3(bank[b][:, (n - n0) * T:(n - n0 + 1) * T], wh[:, k, f], wl[:, k, f], xh[:, k0 + k], xl[:, k0 + k],
                           start and n == n0 and k == 0, stop and k == kc - 1)
            return last

        def by_token(i, b, xh, xl, kc, ncol, k0=0, c0=0, c1=None, tiles=range(NT), step=256, start=True):
            wh, wl = wslab(i, kc, ncol)
            c1 = ncol if c1 is None else c1
            for k, n in chunk_order(kc, range(len(tiles)), xh):
                tk = slice(tiles[n] * P, (tiles[n] + 1) * P)
                last = mm3(bank[b][:, n * step:n * step + c1 - c0], xh[:, k0 + k, tk], xl[:, k0 + k, tk], wh[:, k, c0:c1],
                           wl[:, k, c0:c1], start and n == 0 and k == 0, k == kc - 1)
            return last

        def need(name):
            pe.wait_ge(*reach("lo_done", 2 * slab_of[name] + 2))
            return slab_of[name]

        def act_norm(nm, ready, gain):
            for t in range(NT):
                act.wait_ge(*reach(ready[0], ready[1 + t]))
                act.activation(xn[:, t], X[:, t], ACT.Square, accum_out=stat("norm", 4)[:, t:t + 1]).then_inc(S(nm + "_ss"), 1)
            for j in range(KD // 2):
                act.wait_ge(*reach(nm + "_tr", j + 1))
                for c in range(2):
                    act.activation(Uh[:, 2 * j + c], bank[4 + j][:, c * T:(c + 1) * T], ACT.Copy,
                                   scale=gcol(gain, 2 * j + c)).then_inc(S(nm + "_hi"), 1)

        def pool_rsqrt(r, ss, n, done):
            pool.tensor_scalar(ss, ss, 1.0 / n, EPS, ALU.mult, ALU.add).then_inc(S("pool_chain"), 1)
            pool_chain[0] += 1
            pool.wait_ge(*reach("pool_chain", pool_chain[0]))
            w = ss.shape[1]
            pool.tensor_tensor(r, ss, halves[:, 0:w], ALU.pow).then_inc(S(done), 1)

        pool_chain = [0]
        halves = stat("halves", 32)

        def pool_norm(nm):
            for t in range(NT):
                pool.wait_ge(*reach(nm + "_ss", t + 1))
                pool_rsqrt(stat("norm", 4)[:, 2 + t:3 + t], stat("norm", 4)[:, t:t + 1], D, nm + "_r")

        def dve_norm(nm, gain):
            for t in range(NT):
                dve.wait_ge(*reach(nm + "_r", t + 1))
                dve.tensor_scalar(xn[:, t], X[:, t], stat("norm", 4)[:, 2 + t:3 + t], None, ALU.mult).then_inc(S(nm + "_xn"), 1)
            for j in range(KD // 2):
                dve.wait_ge(*reach(nm + "_hi", 2 * j + 2))
                for c in range(2):
                    dve.scalar_tensor_tensor(Ul[:, 2 * j + c], bank[4 + j][:, c * T:(c + 1) * T], gcol(gain, 2 * j + c),
                                             Uh[:, 2 * j + c].bitcast(F32), ALU.mult, ALU.subtract).then_inc(S(nm + "_lo"), 1)

        def pe_norm(nm):
            for t in range(NT):
                pe.wait_ge(*reach(nm + "_xn", t + 1))
                for j in range(KD // 2):
                    if t == 0:
                        claim(4 + j, nm + "_lo", 2 * j + 2)
                    for c in range(2):
                        last = pe.transpose(bank[4 + j][:, c * T + t * P:c * T + (t + 1) * P],
                                            xn[:, t, (2 * j + c) * P:(2 * j + c + 1) * P], ident)
                    if t == NT - 1:
                        last.then_inc(S(nm + "_tr"), 1)
            fresh.append((nm + "_lo", 1, Uh))

        def pe_ffn(nm, n):
            b = slab_of[nm]
            for k in range(4):
                claim(k, nm + "_x", k + 1)
                pe.matmul(bank[k][:, :], zero[:, 0:P], zero[:, :], start=True, stop=False, skip_group_check=True)
            claim(4, nm + "_silu", n)
            claim(5, nm + "_mul", n)

            def up(i, g, q=None):
                off = 0 if q is None else 3 * q
                for j, done in enumerate(("_silu", "_mul")):
                    pe.wait_ge(*reach("lo_done", 2 * (g + j + 1 + off)))
                    if i is not None:
                        pe.wait_ge(*reach(nm + done, i))
                    by_feature(g + j, 4 + j, Uh, Ul, KD, 256).then_inc(S("slab_used"), 1)

            def down(i, g, q=None, last=False):
                hh_, hl_ = (hh, hl) if not last else (hh_last, hl_last)
                pe.wait_ge(*reach("lo_done", 2 * (g + 1 + (0 if q is None else 3 * q))))
                pe.wait_ge(*reach(nm + "_h", i + 1))
                wh, wl = wslab(g, 2, 1024)
                for t in range(NT):
                    for half in range(2):
                        for k in range(2):
                            f = slice(k * T + t * P, k * T + (t + 1) * P)
                            c = slice(half * 512, (half + 1) * 512)
                            m = mm3(bank[2 * t + half][:, :], hh_[:, f], hl_[:, f], wh[:, k, c], wl[:, k, c], False, last and k == 1)
                        if last and 2 * t + half < 3:
                            m.then_inc(S(nm + "_acc"), 1)
                m.then_inc(S("slab_used"), 1)

            up(None, b)
            up(1, b + 2)
            down(0, b + 4)
            with pe.Fori(1, n - 1) as i:
                up(i + 1, b + 2, i)
                down(i, b + 4, i)
            down(n - 1, b + 3 * n - 1, None, True)

        def act_ffn(nm, n):
            b = slab_of[nm]

            def silu(i, used_by):
                act.wait_ge(*reach("slab_used", used_by))
                if not (isinstance(i, int) and i == 0):
                    act.wait_ge(*reach(nm + "_mul", i))
                act.activation(sgh[:, 0], bank[4][:, :], ACT.Silu).then_inc(S(nm + "_silu"), 1)

            hi_upto(nm)
            silu(0, b + 1)
            for k in range(3):
                split_hi(b + 3 + k)
            with act.Fori(1, n - 1) as i:
                silu(i, i * 3 + b)
                for k in range(3):
                    split_hi(b + 3 + k, i)
            nxt["hi"] = b + 3 * n
            silu(n - 1, b + 3 * (n - 1))
            hi_upto(b + 3 * n - 1)

        def dve_ffn(nm, n):
            b = slab_of[nm]

            def mul(i, used_by):
                dve.wait_ge(*reach("slab_used", used_by))
                dve.wait_ge(*reach(nm + "_silu", i + 1))
                if not (isinstance(i, int) and i == 0):
                    dve.wait_ge(*reach(nm + "_h", i))
                dve.tensor_tensor(sgh[:, 1], sgh[:, 0], bank[5][:, :], ALU.mult).then_inc(S(nm + "_mul"), 1)

            lo_upto(nm)
            mul(0, b + 2)
            for k in range(3):
                split_lo(b + 3 + k)
            with dve.Fori(1, n - 1) as i:
                mul(i, i * 3 + b + 1)
                for k in range(3):
                    split_lo(b + 3 + k, i)
            nxt["lo"] = b + 3 * n
            mul(n - 1, b + 3 * (n - 1) + 1)
            lo_upto(b + 3 * n - 1)
            for t in range(NT):
                for half in range(2):
                    if 2 * t + half < 3:
                        dve.wait_ge(*reach(nm + "_acc", 2 * t + half + 1))
                    else:
                        dve.wait_ge(*reach("slab_used", b + 3 * n))
                    dve.scalar_tensor_tensor(X[:, t, half * 512:(half + 1) * 512], bank[2 * t + half][:, :],
                                             0.5, X[:, t, half * 512:(half + 1) * 512],
                                             ALU.mult, ALU.add).then_inc(S(nm + "_x"), 1)

        def pool_ffn(nm, n):
            b = slab_of[nm]

            def hidden(i, first=False, last=False):
                hh_, hl_ = (hh, hl) if not last else (hh_last, hl_last)
                pool.wait_ge(*reach(nm + "_mul", i + 1))
                if not first and not last:
                    pool.wait_ge(*reach("slab_used", i * 3 + b + 2))
                pool.tensor_tensor(hh_[:, :], sgh[:, 1], zero[:, :].bitcast(F32), ALU.add).then_inc(S(nm + "_hh"), 1)
                pool.wait_ge(*reach(nm + "_hh", i + 1))
                pool.tensor_tensor(hl_[:, :], sgh[:, 1], hh_[:, :].bitcast(F32), ALU.subtract).then_inc(S(nm + "_h"), 1)

            hidden(0, True)
            with pool.Fori(1, n - 1) as i:
                hidden(i)
            hidden(n - 1, False, True)


        def runs(eng, body, n):
            for g in range(n // EPG):
                end = g == n // EPG - 1
                body(g * EPG, g, 0)
                body(g * EPG + 1, g, 1)
                with eng.Fori(2, EPG - end) as e:
                    body(g * EPG + e, g, 2)
                if end:
                    body(n - 1, g, 3)

        def pe_experts(b, n, e0, s0, slot_set):
            def turn(E):
                pe.wait_ge(*reach("moe_mul", E + e0))
                for c in range(2):
                    last = pe.transpose(bank[3][:, c * P:(c + 1) * P], sgh[:, 1, c * P:(c + 1) * P], ident)
                last.then_inc(S("moe_t"), 1)

            def project(j, i, E, u):
                pe.wait_ge(*reach("lo_done", 2 * (i + 1) + 6 * E))
                by_token(i, 4 + j, SUh[:, :, u], SUl[:, :, u], KD, 256, tiles=[0]).then_inc(S("slab_used"), 1)

            def down(i, E, first):
                pe.wait_ge(*reach("moe_h", E + e0))
                pe.wait_ge(*reach("lo_done", 2 * (i + 1) + 6 * E))
                wh, wl = wslab(i, 2, D)
                for half in range(2):
                    c = slice(half * 512, (half + 1) * 512)
                    for k in range(2):
                        f = slice(k * P, (k + 1) * P)
                        m = mm3(bank[6 + half][:, :], hh[:, f], hl[:, f], wh[:, k, c], wl[:, k, c], first and k == 0, k == 1)
                m.then_inc(S("slab_used"), 1)

            def put_back(s, parts):
                for n_, part in enumerate(parts):
                    t, half = divmod(part, 2)
                    if n_ == 0 and part == 0:
                        pe.wait_ge(*reach("y_lo", 2 * s + 2))
                    if part < 3:
                        if s:
                            pe.wait_ge(*reach("put_ev", 4 * s - 3 + (3, 1, 2)[part]))
                    else:
                        pe.wait_ge(*reach("put_ev", 4 * s + 1))
                    c, tk = slice(half * 512, (half + 1) * 512), slice(t * P, (t + 1) * P)
                    u = slot_set(s)
                    pe.matmul(bank[part % 3][:, :], PICKT[:, u, tk], Yh[:, c], start=True, stop=False, skip_group_check=True)
                    pe.matmul(bank[part % 3][:, :], PICKT[:, u, tk], Yl[:, c], start=False, stop=True,
                              skip_group_check=True).then_inc(S("put"), 1)

            def body(E, g, kind):
                first = isinstance(E, int) and E == 0
                u = g if n > EPG else 0
                if first:
                    project(0, b, 0, u)
                    project(1, b + 1, 0, u)
                    return
                turn(E)
                project(0, b - 1, E, u)
                project(1, b, E, u)
                again = kind == 1 and g > 0
                if again:
                    put_back(g - 1 + s0, (0, 1, 2))
                down(b + 1, E, kind == 1)
                if again:
                    put_back(g - 1 + s0, (3,))
                if kind == 3:
                    turn(E + 1)
                    down(b - 1, E + 1, False)
                    put_back(g + s0, (0, 1, 2, 3))

            runs(pe, body, n)

        def act_experts(b, n, e0, s0):
            def copy_out(s):
                for half in range(2):
                    if s:
                        act.wait_ge(*reach("put", 4 * s))
                    act.activation(Yh[:, half * 512:(half + 1) * 512], bank[6 + half][:, :], ACT.Copy).then_inc(S("y_hi"), 1)

            def copy_put(s):
                for part in range(4):
                    act.wait_ge(*reach("put", 4 * s + part + 1))
                    if s:
                        act.wait_ge(*reach("x_add", 4 * s - 3 + part))
                    act.activation(PUT[:, part], bank[part % 3][:, :], ACT.Copy).then_inc(S("put_ev"), 1)

            def body(E, g, kind):
                first = isinstance(E, int) and E == 0
                if first:
                    act.wait_ge(*reach("slab_used", b + 1))
                else:
                    act.wait_ge(*reach("slab_used", b + 3 * E))
                if not first or e0:
                    act.wait_ge(*reach("moe_mul", E + e0))
                act.activation(sgh[:, 0, 0:T], bank[4][:, 0:T], ACT.Silu).then_inc(S("moe_silu"), 1)
                more = kind != 3
                if more:
                    split_hi(b + 2, E)
                    split_hi(b + 3, E)
                else:
                    split_hi(b + 3 * n - 1)
                if kind == 0 and not first:
                    act.wait_ge(*reach("slab_used", b + 3 * E + 2))
                    copy_out(g - 1 + s0)
                if kind == 1 and g:
                    copy_put(g - 1 + s0)
                act.wait_ge(*reach("moe_t", E + e0 + 1))
                act.activation(hh[:, 0:T], bank[3][:, 0:T], ACT.Copy).then_inc(S("moe_hh"), 1)
                if more:
                    split_hi(b + 4, E)
                else:
                    act.wait_ge(*reach("slab_used", b + 3 * n))
                    copy_out(g + s0)
                    copy_put(g + s0)

            runs(act, body, n)

        def dve_experts(b, n, e0, s0):
            def low_out(s):
                for half in range(2):
                    dve.wait_ge(*reach("y_hi", 2 * s + half + 1))
                    c = slice(half * 512, (half + 1) * 512)
                    dve.tensor_tensor(Yl[:, c], bank[6 + half][:, :], Yh[:, c].bitcast(F32), ALU.subtract).then_inc(S("y_lo"), 1)

            def body(E, g, kind):
                first = isinstance(E, int) and E == 0
                dve.wait_ge(*reach("slab_used", (b + 2) if first else b + 1 + 3 * E))
                dve.wait_ge(*reach("moe_silu", E + e0 + 1))
                w = CW[:, E + s0 * EPG, :]
                dve.scalar_tensor_tensor(sgh[:, 1, 0:T], sgh[:, 0, 0:T], w, bank[5][:, 0:T], ALU.mult,
                                         ALU.mult).then_inc(S("moe_mul"), 1)
                more = kind != 3
                if more:
                    split_lo(b + 2, E)
                    split_lo(b + 3, E)
                else:
                    split_lo(b + 3 * n - 1)
                if kind == 0 and not first:
                    low_out(g - 1 + s0)
                dve.wait_ge(*reach("moe_hh", E + e0 + 1))
                dve.tensor_tensor(hl[:, 0:T], bank[3][:, 0:T], hh[:, 0:T].bitcast(F32), ALU.subtract).then_inc(S("moe_h"), 1)
                if more:
                    split_lo(b + 4, E)
                else:
                    low_out(g + s0)

            runs(dve, body, n)

        def pool_experts(n, s0):
            def add(s):
                for part in range(4):
                    t, half = divmod(part, 2)
                    xs_ = X[:, t, half * 512:(half + 1) * 512]
                    pool.wait_ge(*reach("put_ev", 4 * s + part + 1))
                    pool.tensor_tensor(xs_, xs_, PUT[:, part], ALU.add).then_inc(S("x_add"), 1)

            if n == 1:
                add(s0)
            else:
                with pool.Fori(0, n) as s:
                    add(s)

        scr = sgh[:, :, :].rearrange("p a n -> p (a n)")

        def act_head_squares(nm, buf, H, d, after):
            for t in range(NT):
                if t or after:
                    w = (nm + "_red", t) if t else after
                    act.wait_ge(*reach(w[0], w[1]))
                act.activation(scr[:, 0:H * d], buf[:, t].rearrange("p h d -> p (h d)"), ACT.Square).then_inc(S(nm + "_sq"), 1)

        def dve_head_sums(nm, H, d):
            for t in range(NT):
                dve.wait_ge(*reach(nm + "_sq", t + 1))
                dve.tensor_reduce(stat(nm, 2 * H)[:, t * H:(t + 1) * H], scr[:, 0:H * d].rearrange("p (h d) -> p h d", d=d),
                                  AX, ALU.add).then_inc(S(nm + "_red"), 1)

        def pool_head_rsqrt(nm, H, d):
            pool.wait_ge(*reach(nm + "_red", NT))
            pool_rsqrt(stat(nm, NT * H), stat(nm, NT * H), d, nm + "_r")

        def dve_head_scale(nm, buf, H, d, gain, out=None):
            dve.wait_ge(*reach(nm + "_r", 1))
            r = stat(nm, NT * H).rearrange("p (t h) -> p t h", t=NT).unsqueeze(3).to_broadcast([P, NT, H, d])
            g = pb(gain).unsqueeze(1).unsqueeze(1).to_broadcast([P, NT, H, d])
            dve.tensor_tensor(buf, buf, r, ALU.mult).then_inc(S(nm + "_scaled"), 1)
            dve.wait_ge(*reach(nm + "_scaled", 1))
            dve.tensor_tensor(buf, buf, g, ALU.mult).then_inc(S(nm + "_scaled"), 1)
            dve.wait_ge(*reach(nm + "_scaled", 2))

        def dve_rope(nm, buf, H, lo, half, cos, sin):
            n = NT * H * half
            m = [scr[:, k * 256:k * 256 + n].rearrange("p (t h d) -> p t h d", t=NT, h=H) for k in range(4)]
            x1, x2 = buf[:, :, :, lo:lo + half], buf[:, :, :, lo + half:lo + 2 * half]
            c = cos.unsqueeze(2).to_broadcast([P, NT, H, half])
            s_ = sin.unsqueeze(2).to_broadcast([P, NT, H, half])
            for k, (x, f) in enumerate(((x1, c), (x2, s_), (x2, c), (x1, s_))):
                dve.tensor_tensor(m[k], x, f, ALU.mult).then_inc(S(nm + "_turn"), 1)
            dve.wait_ge(*reach(nm + "_turn", 4))
            dve.tensor_tensor(x1, m[0], m[1], ALU.subtract).then_inc(S(nm + "_turn"), 1)
            dve.tensor_tensor(x2, m[2], m[3], ALU.add).then_inc(S(nm + "_turn"), 1)

        def pe_attention(nm, H, qt, kt, v):
            for i in range(-1, H + 3):
                if i + 1 < H:
                    n = i + 1
                    claim(n % 3, nm + "_mx", 2 * n + 2)
                    b = bank[n % 3]
                    pe.matmul(b[:, 0:P], qt(n)[:, 0:P], kt(n)[:, 0:P], start=True, stop=True, skip_group_check=True)
                    pe.matmul(b[:, P:3 * P], qt(n)[:, P:T], kt(n), start=False, stop=True,
                              skip_group_check=True).then_inc(S(nm + "_s"), 1)
                if 2 <= i < H + 2:
                    h = i - 2
                    claim(3 + h % 2, nm + "_ptc", h + 1)
                    pe.wait_ge(*reach(nm + "_pn", 2 * h + 2))
                    for k in range(3):
                        last = pe.transpose(bank[3 + h % 2][:, k * P:(k + 1) * P], aw[:, h % 3, k * P:(k + 1) * P], ident)
                    last.then_inc(S(nm + "_pt"), 1)
                if i >= 3:
                    h = i - 3
                    b = 5 + (h // 2) % 2
                    if h % 2 == 0:
                        claim(b, nm + "_olo", h // 2 + 1)
                    pe.wait_ge(*reach(nm + "_ptc", h + 1))
                    o = bank[b][64 * (h % 2):64 * (h % 2) + 64, 0:T]
                    pe.matmul(o, v(h, 0), aw[:, 3 + h % 2, 0:T], start=True, stop=False, skip_group_check=True)
                    pe.matmul(o[:, P:T], v(h, 1), aw[:, 3 + h % 2, T:3 * P], start=False, stop=True,
                              skip_group_check=True).then_inc(S(nm + "_av"), 1)

        def dve_attention(nm, H, bias, scale, outh, outl):
            mx, nmx, sm, rs = (stat(f"att_{k}", 32) for k in range(4))
            for i in range(H + 5):
                if i < H:
                    dve.wait_ge(*reach(nm + "_s", i + 1))
                    if i >= 3:
                        dve.wait_ge(*reach(nm + "_pt", i - 2))
                    for t, (lo, hi) in enumerate(((0, P), (P, 3 * P))):
                        dve.tensor_tensor_reduce(out=aw[:, i % 3, lo:hi], in0=bank[i % 3][:, lo:hi], in1=bias[:, lo:hi],
                                                 scale=1.0, scalar=-3e38, op0=ALU.add, op1=ALU.max,
                                                 accum_out=mx[:, 2 * i + t:2 * i + t + 1]).then_inc(S(nm + "_mx"), 1)
                    dve.wait_ge(*reach(nm + "_mx", 2 * i + 2))
                    dve.tensor_scalar(nmx[:, 2 * i:2 * i + 2], mx[:, 2 * i:2 * i + 2], -scale, None,
                                      ALU.mult).then_inc(S(nm + "_nm"), 1)
                if 1 <= i < H + 1:
                    h = i - 1
                    dve.wait_ge(*reach(nm + "_exp", 2 * h + 2))
                    dve.reciprocal(rs[:, 2 * h:2 * h + 2], sm[:, 2 * h:2 * h + 2]).then_inc(S(nm + "_rs"), 1)
                    dve.wait_ge(*reach(nm + "_rs", h + 1))
                    for t, (lo, hi) in enumerate(((0, P), (P, 3 * P))):
                        dve.tensor_scalar(aw[:, h % 3, lo:hi], aw[:, h % 3, lo:hi], rs[:, 2 * h + t:2 * h + t + 1], None,
                                          ALU.mult).then_inc(S(nm + "_pn"), 1)
                h = i - 4
                if h >= 0 and h % 2 == 1:
                    dve.wait_ge(*reach(nm + "_ohi", h // 2 + 1))
                    dve.tensor_tensor(outl[:, h // 2], bank[5 + (h // 2) % 2][:, 0:T], outh[:, h // 2].bitcast(F32),
                                      ALU.subtract).then_inc(S(nm + "_olo"), 1)

        def act_attention(nm, H, scale, outh):
            nmx, sm = stat("att_1", 32), stat("att_2", 32)
            for i in range(H + 5):
                if i < H:
                    act.wait_ge(*reach(nm + "_nm", i + 1))
                    for t, (lo, hi) in enumerate(((0, P), (P, 3 * P))):
                        act.activation(aw[:, i % 3, lo:hi], aw[:, i % 3, lo:hi], ACT.Exp, bias=nmx[:, 2 * i + t:2 * i + t + 1],
                                       scale=scale, accum_out=sm[:, 2 * i + t:2 * i + t + 1]).then_inc(S(nm + "_exp"), 1)
                if 2 <= i < H + 2:
                    h = i - 2
                    act.wait_ge(*reach(nm + "_pt", h + 1))
                    if h >= 2:
                        act.wait_ge(*reach(nm + "_av", h - 1))
                    act.activation(aw[:, 3 + h % 2, :], bank[3 + h % 2][:, 0:3 * P], ACT.Copy).then_inc(S(nm + "_ptc"), 1)
                h = i - 4
                if h >= 0 and h % 2 == 1:
                    act.wait_ge(*reach(nm + "_av", h + 1))
                    act.activation(outh[:, h // 2], bank[5 + (h // 2) % 2][:, 0:T], ACT.Copy).then_inc(S(nm + "_ohi"), 1)

        gate2_bank = (7, 4, 7, 0, None, None, 6, 7)

        def xbc_bank(j):
            return (2, 3, 5, 6)[j] if j < 4 else 7

        awf = aw[:, :].rearrange("p a n -> p (a n)")

        def EM(n):
            return awf[:, n % 4 * 512:(n % 4 + 1) * 512]

        rt_at = {}

        def rt(name, n):
            if name not in rt_at:
                rt_at[name] = sum(v[1] for v in rt_at.values()), n
            at, _ = rt_at[name]
            assert at + n <= 3 * 384
            return awf[:, at:at + n]

        def overflow(eng):
            return nc.values_load(OV[0:1, 0:1], engines=[eng.engine], min_val=0, max_val=1,
                                  skip_runtime_bounds_check_because="VectorE writes 0 or 1")

        def first_expert(eng):
            return nc.values_load(OV[0:1, 1:2], engines=[eng.engine], min_val=0, max_val=NE - EPG,
                                  skip_runtime_bounds_check_because="VectorE writes 0 or a group's first expert")

        block = ctx.enter_context(nc.Block())

        def load_experts(sp, i, n, gate, up, down):
            load(sp, i, None, gate(0))
            load(sp, i + 1, None, up(0))
            load(sp, i + 2, None, gate(1))
            load(sp, i + 3, None, up(1))
            load(sp, i + 4, None, down(0))
            with sp.Fori(1, n - 1) as q:
                load(sp, i + 2, q, gate(q + 1))
                load(sp, i + 3, q, up(q + 1))
                load(sp, i + 4, q, down(q))
            load(sp, i + 3 * n - 1, None, down(n - 1))

        @block.sync
        def _(sp):
            for t in range(NT):
                sp.dma_start(X[:, t], a["x"][0, t * P:(t + 1) * P, :]).then_inc(S(f"ld_x{t}"), 16)
            sp.wait_ge(*reach("ld_rows", 16 * (len(gain_rows) + 1)))
            i = 0
            while i < len(slabs):
                if i in loops:
                    load_experts(sp, i, *loops[i])
                    i += 3 * loops[i][0]
                else:
                    load(sp, i)
                    i += 1
            sp.wait_ge(*reach("over", 1))
            flag, first = overflow(sp), first_expert(sp)
            with sp.If(flag != 0):
                load_experts(sp, over, EPG, lambda e: wg[first + e], lambda e: wu[first + e], lambda e: wd[first + e])
                sp.wait_ge(*reach("x_add", 4 * EG + 4))
            for part in range(4):
                t, half = divmod(part, 2)
                c = slice(half * 512, (half + 1) * 512)
                sp.wait_ge(*reach("x_add", 4 * (EG - 1) + part + 1))
                sp.dma_start(out[0, t * P:(t + 1) * P, c], X[:, t, c]).then_inc(S("out"), 16)
            sp.wait_ge(*reach("out", 64))

        @block.scalar
        def _(_e):
            act.preload_act_table(ACT.Silu)
            act.dma_start(C[:, 0:P], a["const"][:, 0:P]).then_inc(S("ld_ident"), 16)
            for name, n in gain_rows:
                at = gain_at[name]
                act.dma_start(rows1[at:at + n, :], a[name].rearrange("o (c p) -> (o c) p", p=P)).then_inc(S("ld_rows"), 16)
            act.dma_start(rows2[0:n_rows2, :], a["conv_w_2"].rearrange("o t (c p) -> (o t c) p", p=P)).then_inc(S("ld_rows"), 16)
            for t in range(NT):
                act.wait_ge(*reach(f"ld_x{t}", 16))
                act.activation(xn[:, t], X[:, t], ACT.Square, accum_out=stat("norm", 4)[:, t:t + 1]).then_inc(S("n1_ss"), 1)
            act.wait_ge(*reach("gains", 2))
            for j in range(KD // 2):
                act.wait_ge(*reach("n1_tr", j + 1))
                for c in range(2):
                    act.activation(Uh[:, 2 * j + c], bank[4 + j][:, c * T:(c + 1) * T], ACT.Copy,
                                   scale=gcol("ffn1_norm", 2 * j + c)).then_inc(S("n1_hi"), 1)
            hi_upto("ffn1")
            act.dma_start(C[:, P:], a["const"][:, P:]).then_inc(S("ld_const"), 16)
            act.dma_start(pos[:], a["positions"].rearrange("o (t p) -> p (o t)", p=P),
                          allow_slow_non_contiguous=True).then_inc(S("ld_pos"), 16)
            for name, n in pb_list:
                at = pb_at[name][0]
                act.dma_start(PB[:, at:at + n], a[name][0].partition_broadcast(P)).then_inc(S("ld_pb"), 16)
            act.wait_ge(*reach("angles", 2))
            act.activation(SIN1, rope1[:, 4], ACT.Sin).then_inc(S("rope1"), 1)
            act.activation(COS1, rope1[:, 5], ACT.Sin).then_inc(S("rope1"), 1)
            act_ffn("ffn1", NF)

            act_norm("n2", ("ffn1_x", 2, 4), "mix_norm")
            for i in range(3):
                hi_upto(f"lat{i}")
                used(act, f"lat{i}")
                n = slabs[slab_of[f"lat{i}"]][2]
                act.activation(CQ[:, :, i * 256:i * 256 + n], bank[i].rearrange("p (t n) -> p t n", t=NT)[:, :, 0:n],
                               ACT.Copy).then_inc(S("lat_ev"), 1)
            act.preload_act_table_set("natural_log_exp_and_others")
            act.wait_ge(*reach("lat_ev", 3))
            for t in range(NT):
                act.activation(xn[:, t, 0:QL], CQ[:, t, 0:QL], ACT.Square, accum_out=stat("lat", 4)[:, t:t + 1]).then_inc(S("lat_ss"), 1)
                act.activation(xn[:, t, QL:QL + KVL], CQ[:, t, QL:QL + KVL], ACT.Square,
                               accum_out=stat("lat", 4)[:, 2 + t:3 + t]).then_inc(S("lat_ss"), 1)
            for j, (nm, dst) in enumerate((("sq", sqT), ("sk", skT))):
                for i in range(2):
                    hi_upto(f"{nm}{i}")
                    used(act, f"{nm}{i}")
                    act.activation(dst[:, 2 * i:2 * i + 2].rearrange("p c n -> p (c n)"), bank[3 + 2 * j + i][:, :], ACT.Copy,
                                   scale=0.125 if nm == "sq" else 1.0).then_inc(S("sqk_ev"), 1)
            for i in range(2):
                hi_upto(f"sv{i}")
                used(act, f"sv{i}")
                act.activation(sv[:, :, i * 256:(i + 1) * 256], bank[(7, 0)[i]].rearrange("p (t n) -> p t n", t=NT),
                               ACT.Copy).then_inc(S("sv_ev"), 1)
            for c in range(5):
                act.wait_ge(*reach("lt_tr", c // 2 + 1))
                gain = gcol("q_latent_norm", c) if c < 3 else gcol("kv_latent_norm", c - 3)
                act.activation(Lh[:, c], bank[1 + c // 2][:, c % 2 * T:(c % 2 + 1) * T], ACT.Copy, scale=gain).then_inc(S("lt_hi"), 1)
            for i in range(2):
                hi_upto(f"qup{i}")
                used(act, f"qup{i}")
                for t in range(NT):
                    act.activation(Q1[:, t, 4 * i:4 * i + 4].rearrange("p h d -> p (h d)"), bank[4 + 2 * i + t if i == 0 else t][:, 0:384],
                                   ACT.Copy).then_inc(S("q_ev"), 1)
            hi_upto("kvup")
            used(act, "kvup")
            for t in range(NT):
                for half in range(2):
                    b = bank[(2, 3, 6, 7)[2 * t + half]].rearrange("p (h d) -> p h d", d=P)
                    act.activation(K1[:, t, 4 * half:4 * half + 4, 0:NOPE], b[:, :, 0:NOPE], ACT.Copy).then_inc(S("kv_ev"), 1)
                    act.activation(V1[:, t, 4 * half:4 * half + 4, :], b[:, :, NOPE:P], ACT.Copy).then_inc(S("kv_ev"), 1)
            act.wait_ge(*reach("q_ev", 4))
            act_head_squares("hq", Q1, MH, QK, None)
            act.wait_ge(*reach("kv_ev", 8))
            act.wait_ge(*reach("krope", 1))
            act_head_squares("hk", K1[:], MH, QK, ("hq_red", 2))

            def gate_out(g, b):
                hi_upto(f"gate{g}")
                used(act, f"gate{g}")
                act.activation(GT[:, 2 * g:2 * g + 2].rearrange("p c n -> p (c n)"), bank[b][:, :], ACT.Copy).then_inc(S("gate_ev"), 1)

            for g in range(3):
                gate_out(g, (4, 5, 4)[g])
            for j in range(4):
                act.wait_ge(*reach("qt_tr", j + 1))
                act.activation(QT1[:, 2 * j:2 * j + 2].rearrange("p h n -> p (h n)"), bank[j][0:QK, :], ACT.Copy).then_inc(S("qt_ev"), 1)
            for i in range(8 + 6):
                if i < 8:
                    hi_upto(f"gate{min(7, 3 + i)}")
                    act.wait_ge(*reach("sb_z", i + 1))
                    if i >= 2:
                        act.wait_ge(*reach("sb_sp", i - 1))
                    act.activation(aw[:, i % 2], bank[i % 4][:, 0:384], ACT.Abs).then_inc(S("sb_l"), 1)
                    act.wait_ge(*reach("sb_l", 3 * i + 1))
                    act.activation(aw[:, i % 2], aw[:, i % 2], ACT.Exp, scale=-1.0).then_inc(S("sb_l"), 1)
                    act.wait_ge(*reach("sb_l", 3 * i + 2))
                    act.activation(aw[:, i % 2], aw[:, i % 2], ACT.Ln, bias=1.0).then_inc(S("sb_l"), 1)
                h = i - 3
                if 0 <= h < 8:
                    act.wait_ge(*reach("sb_m", h + 1))
                    act.activation(aw[:, 4 + h % 2], aw[:, 4 + h % 2], ACT.Exp).then_inc(S("sb_a"), 1)
                if i < 5:
                    gate_out(3 + i, 6 + i % 2)
                h = i - 5
                if h >= 0 and h % 2 == 1:
                    act.wait_ge(*reach("sb_av", h + 1))
                    act.activation(OSh[:, h // 2], bank[4 + (h // 2) % 2][:, 0:T], ACT.Copy).then_inc(S("os_hi"), 1)
            hi_upto("mla0")
            act_attention("mla", MH, QK ** -0.5, OMh)
            act.dma_start(aw[:, 0:2, 0:PLE], a["p"][0, 0].rearrange("(t p) n -> p t n", p=P)).then_inc(S("ld_p"), 16)
            act.preload_act_table(ACT.Sigmoid)
            act.wait_ge(*reach("gate_ev", 8))
            for q in range(4):
                act.activation(GT[:, 4 * q:4 * q + 4].rearrange("p c n -> p (c n)"), GT[:, 4 * q:4 * q + 4].rearrange("p c n -> p (c n)"),
                               ACT.Sigmoid).then_inc(S("gsig"), 1)
            for q in range(4):
                hi_upto(f"sbr{q // 2}")
                act.wait_ge(*reach("mg_s", q + 1))
                act.activation(Uh[:, 2 * q:2 * q + 2].rearrange("p c n -> p (c n)"), sgh[:, q % 2], ACT.Copy).then_inc(S("mg_hi"), 1)
            act.wait_ge(*reach("p_tr", 1))
            act.activation(OMh[:, 0:2].rearrange("p c n -> p (c n)"), bank[6][:, :], ACT.Copy).then_inc(S("p_hi"), 1)
            hi_upto("wout3")
            act_norm("n3", ("x2", 4, 4), "ffn2_norm")
            act.preload_act_table(ACT.Silu)
            act_ffn("ffn2", NF)
            act.preload_act_table(ACT.Sigmoid)
            act_norm("n4", ("ffn2_x", 2, 4), "ple_norm")
            hi_upto("pproj")
            used(act, "pproj")
            for c in range(4):
                act.activation(PP[:, :, c * 256:(c + 1) * 256], bank[c].rearrange("p (t n) -> p t n", t=NT), ACT.Copy).then_inc(S("pp_ev"), 1)
            for c in range(4):
                hi_upto(f"pgate{c}")
                used(act, f"pgate{c}")
                if c >= 2:
                    act.wait_ge(*reach("x4", c - 1))
                act.activation(sgh[:, c % 2], bank[4 + c][:, :], ACT.Sigmoid).then_inc(S("pg"), 1)

            act_norm("n5", ("x4", 4, 4), "attn_norm_2")
            act.preload_act_table_set("natural_log_exp_and_others")
            tok = lambda b, n, at=0: bank[b].rearrange("p (t n) -> p t n", t=NT)[:, :, at:at + n]
            outs = [(f"q{i}", i, xn[:, :, i * 256:(i + 1) * 256], 256) for i in range(4)]
            outs += [("k", 4, K2[:].rearrange("p t h d -> p t (h d)"), 256), ("v", 5, V2[:], 256),
                     ("iq0", 6, IQ[:, :, 0:4].rearrange("p t h d -> p t (h d)"), 256),
                     ("iq1", 7, IQ[:, :, 4:8].rearrange("p t h d -> p t (h d)"), 256),
                     ("ik_dt", 0, IKW[:], HD + IH), ("ik_dt", 0, ssm[:, 0:2], SH)]
            for nm, b, dst, n in outs:
                hi_upto(nm)
                used(act, nm)
                act.activation(dst, tok(b, n, HD + IH if n == SH else 0), ACT.Copy).then_inc(S("b2_ev"), 1)
            act.wait_ge(*reach("b2_ev", 9))
            act_head_squares("ik", IKW[:, :, 0:HD].unsqueeze(2), 1, HD, None)
            act_head_squares("k2", K2[:], KVH2, HD, ("ik_red", 2))
            act_head_squares("q2", Q2, H2, HD, ("k2_red", 2))
            act.wait_ge(*reach("dt_x", 1))
            act.activation(ssm[:, 2:4], ssm[:, 0:2], ACT.Abs).then_inc(S("dt_l"), 1)
            act.wait_ge(*reach("dt_l", 1))
            act.activation(ssm[:, 2:4], ssm[:, 2:4], ACT.Exp, scale=-1.0).then_inc(S("dt_l"), 1)
            act.wait_ge(*reach("dt_l", 2))
            act.activation(ssm[:, 2:4], ssm[:, 2:4], ACT.Ln, bias=1.0).then_inc(S("dt_l"), 1)
            act.activation(ssm[:, 8], pb("a_log_2"), ACT.Exp).then_inc(S("dt_l"), 1)

            def gate2_out(g):
                hi_upto(f"g{g}")
                used(act, f"g{g}")
                dst = (G2a if g < 4 else G2)[:, 2 * g:2 * g + 2]
                act.activation(dst.rearrange("p c n -> p (c n)"), bank[gate2_bank[g]][:, :],
                               ACT.Copy).then_inc(S("g2_ev"), 1)

            def conv_copy(j):
                hi_upto(f"xbc{j}")
                used(act, f"xbc{j}")
                if j >= 2:
                    act.wait_ge(*reach("conv", 6 * (j - 1)))
                act.activation(sgh[:, j % 2], bank[xbc_bank(j)][:, :], ACT.Copy).then_inc(S("xb_ev"), 1)

            def conv_first(j):
                act.wait_ge(*reach("xb_ev", 3 * j + 1))
                for c in range(2):
                    ch = 2 * j + c
                    act.activation(XC[:, ch], sgh[:, j % 2, c * T:(c + 1) * T], ACT.Identity, bias=gcol("conv_b_2", ch),
                                   scale=gcol("conv_w_2", (TAPS - 1) * NX + ch)).then_inc(S("xb_ev"), 1)

            hi_upto("xbc1")
            for i in range(2):
                act.wait_ge(*reach("iqt_tr", i + 1))
                act.activation(IQT[:, 2 * i:2 * i + 2].rearrange("p c n -> p (c n)"), bank[4 + i][:, :], ACT.Copy).then_inc(S("iqt_ev"), 1)
            hi_upto("xbc2")
            for i in range(4):
                act.wait_ge(*reach("qt2_tr", i + 1))
                act.activation(QT2[:, 2 * i:2 * i + 2].rearrange("p c n -> p (c n)"), bank[(1, 4, 5, 6)[i]][:, :],
                               ACT.Copy).then_inc(S("qt2_ev"), 1)
            for h in range(IH):
                act.wait_ge(*reach("ix_s", h + 1))
                if h >= 3:
                    act.wait_ge(*reach("ix_a", 2 * (h - 2)))
                act.activation(aw[:, h % 3], bank[(7, 0, 1, 4)[h % 4]][:, 0:384], ACT.Relu, scale=HD ** -0.5).then_inc(S("ix_r"), 1)
            for j in range(4):
                if j == 2:
                    hi_upto("xbc3")
                conv_copy(j)
                conv_first(j)
                if j >= 2:
                    gate2_out(j - 2)
            nmx, sm = stat("att_1", 32), stat("att_2", 32)
            for i in range(H2 + 5):
                if i < H2:
                    act.wait_ge(*reach("dsa_nm", i + 1))
                    for t, (lo, hi) in enumerate(((0, P), (P, 3 * P))):
                        act.activation(aw[:, i % 3, lo:hi], aw[:, i % 3, lo:hi], ACT.Exp, bias=nmx[:, 2 * i + t:2 * i + t + 1],
                                       scale=HD ** -0.5, accum_out=sm[:, 2 * i + t:2 * i + t + 1]).then_inc(S("dsa_exp"), 1)
                j = 4 + i // 2
                if j < NX // 2 and i % 2 == 1:
                    conv_copy(j)
                if 2 <= i < H2 + 2:
                    h = i - 2
                    act.wait_ge(*reach("dsa_pt", h + 1))
                    if h >= 2:
                        act.wait_ge(*reach("dsa_av", h - 1))
                    act.activation(aw[:, 3 + h % 2, :], bank[3 + h % 2][:, 0:3 * P], ACT.Copy).then_inc(S("dsa_ptc"), 1)
                h = i - 4
                if h >= 0 and h % 2 == 1:
                    act.wait_ge(*reach("dsa_av", h + 1))
                    act.activation(OAh[:, h // 2], bank[5 + (h // 2) % 2][:, 0:T], ACT.Copy).then_inc(S("dsa_ohi"), 1)
                if j < NX // 2:
                    if i % 2 == 0:
                        hi_upto(f"xbc{j}")
                    else:
                        conv_first(j)
                if i in (H2, H2 + 2):
                    hi_upto("g2" if i == H2 else "g3")
                if i in (H2 + 1, H2 + 3):
                    gate2_out(2 if i == H2 + 1 else 3)
            act.preload_act_table(ACT.Silu)
            act.wait_ge(*reach("conv", 6 * (NX // 2)))
            for q in (4, 5, 0, 1, 2, 3):
                v = XC[:, 4 * q:4 * q + 4].rearrange("p c n -> p (c n)")
                act.activation(v, v, ACT.Silu).then_inc(S("xc"), 1)
            act.preload_act_table(ACT.Exp)
            hi_upto("wa0")
            for j in range(8):
                act.wait_ge(*reach("xs_tr", j + 1))
                act.activation(XS[:, :, j * 256:(j + 1) * 256], tok(j % 4, 256), ACT.Copy).then_inc(S("xs_ev"), 1)
            act.wait_ge(*reach("bt_tr", 1))
            act.activation(BTM[:].rearrange("p g n -> p (g n)"), bank[4][:, :], ACT.Copy).then_inc(S("bt_ev"), 1)
            act.wait_ge(*reach("acs", 2))
            act.activation(ssm[:, 7], ssm[:, 7], ACT.Exp).then_inc(S("ee"), 1)
            act.activation(ssm[:, 9], ssm[:, 5], ACT.Exp).then_inc(S("ee"), 1)

            def side_out(u):
                nm = f"wa{u}" if u < 4 else f"g{u}"
                hi_upto(nm)
                used(act, nm)
                dst = BA[:, 2 * u:2 * u + 2] if u < 4 else G2[:, 2 * u:2 * u + 2]
                act.activation(dst.rearrange("p c n -> p (c n)"), bank[7][:, :], ACT.Copy).then_inc(S("side_ev"), 1)

            for u in range(8):
                if u < 6:
                    hi_upto(f"wa{u}" if u < 4 else f"g{u}")
                for k in range(2):
                    n = 2 * u + k
                    act.wait_ge(*reach("seg", n + 1))
                    act.activation(EM(n), EM(n), ACT.Exp).then_inc(S("seg_e"), 1)
                if u < 4:
                    act.wait_ge(*reach("st_mm", u + 1))
                    act.activation(ST[:, u], bank[6][:, :], ACT.Copy).then_inc(S("st_ev"), 1)
                if u < 6:
                    side_out(u)
            act.preload_act_table(ACT.Silu)
            for c in range(8):
                hi_upto(f"z{c}")
                used(act, f"z{c}")
                if c >= 2:
                    act.wait_ge(*reach("yz", c - 1))
                else:
                    act.wait_ge(*reach("y", 12))
                act.activation(sgh[:, c % 2], bank[c % 4][:, :], ACT.Silu).then_inc(S("z_s"), 1)
                if c % 2:
                    act.wait_ge(*reach("yz", c + 1))
                    for t in range(NT):
                        act.wait_ge(*reach("yg_ss", 2 * (c // 2) + t)) if c > 1 or t else act.wait_ge(*reach("seg_m", 16))
                        act.activation(awf[:, 0:512], XS[:, t, c // 2 * 512:c // 2 * 512 + 512], ACT.Square,
                                       accum_out=stat("yg", 8)[:, 4 * t + c // 2:4 * t + c // 2 + 1]).then_inc(S("yg_ss"), 1)

            gate2_out(6)
            gate2_out(7)
            for j in range(8):
                act.wait_ge(*reach("yt_tr", j + 1))
                for c in range(2):
                    act.activation(YTh[:, 2 * j + c], bank[j % 4][:, c * T:(c + 1) * T], ACT.Copy,
                                   scale=gcol("ssd_norm_2", 2 * j + c)).then_inc(S("yt_hi"), 1)
            act.preload_act_table(ACT.Sigmoid)
            act.wait_ge(*reach("side_ev", 6))
            act.wait_ge(*reach("g2_ev", 6))
            act.wait_ge(*reach("g2_moved", 1))
            for q in range(4):
                v = G2[:, 4 * q:4 * q + 4].rearrange("p c n -> p (c n)")
                act.activation(v, v, ACT.Sigmoid).then_inc(S("g2sig"), 1)
            for q in range(4):
                hi_upto(f"ws{q}1")
                act.wait_ge(*reach("m2_s", q + 1))
                act.activation(Uh[:, 2 * q:2 * q + 2].rearrange("p c n -> p (c n)"), sgh[:, q % 2], ACT.Copy).then_inc(S("m2_hi"), 1)
            hi_upto("wo3")
            act_norm("n6", ("x5", 4, 4), "ffn_norm_2")
            for t in range(NT):
                act.activation(XNh[:, t], xn[:, t], ACT.Copy).then_inc(S("xn_hi"), 1)
            hi_upto("router")
            act.preload_act_table(ACT.Exp)
            act.wait_ge(*reach("r_gl", 1))
            act.activation(rt("gexp", 8), rt("gexp", 8), ACT.Exp).then_inc(S("r_e"), 1)
            act.wait_ge(*reach("r_d", 1))
            act.activation(rt("d", 2), rt("d", 2), ACT.Exp).then_inc(S("r_e"), 1)
            for c in range(KD):
                act.wait_ge(*reach("su_mm", c + 1))
                act.activation(SUh[:, c].rearrange("p g n -> p (g n)"), bank[4 + c % 4][:, :], ACT.Copy,
                               scale=gcol("ffn_norm_2", c)).then_inc(S("su_hi"), 1)
            for j in range(3):
                act.wait_ge(*reach("pt_mm", j + 1))
                m = min(2, EG + 1 - 2 * j)
                act.activation(PICKT[:, 2 * j:2 * j + m].rearrange("p g n -> p (g n)"), bank[(0, 1, 3)[j]][:, 0:m * T],
                               ACT.Copy).then_inc(S("pt_ev"), 1)
            act.wait_ge(*reach("cw_mm", 1))
            act.activation(CW[:].rearrange("p e o -> p (e o)"), bank[2][:, 0:(EG + 1) * EPG], ACT.Copy).then_inc(S("cw_ev"), 1)
            act.preload_act_table(ACT.Silu)
            act_experts(slab_of["moe"], NE, 0, 0)
            act.wait_ge(*reach("over", 1))
            flag = overflow(act)
            with act.If(flag != 0):
                for c in range(KD):
                    act.wait_ge(*reach("su_mm", KD + c // 4 + 1))
                    act.activation(SUh[:, c, 0], bank[4 + c // 4][:, c % 4 * P:(c % 4 + 1) * P], ACT.Copy,
                                   scale=gcol("ffn_norm_2", c)).then_inc(S("su_hi"), 1)
                split_hi(over)
                split_hi(over + 1)
                act_experts(over, EPG, NE, EG)

        @block.vector
        def _(_e):
            dve.memset(zero[:, :].bitcast(F32), 0.0).then_inc(S("zeroed"), 1)
            n_ld = 16 * (len(gain_rows) + 1)
            for j, (rows, nr, sem) in enumerate(((rows1, n_rows1, "gains"), (rows2, n_rows2, "gains"))):
                dve.wait_ge(*reach("rows_tr", j + 1))
                dve.tensor_copy(G[:, j * P:j * P + nr], bank[j][:, 0:nr]).then_inc(S("gains"), 1)
            dve.wait_ge(*reach("gains", 2))
            dve_norm("n1", "ffn1_norm")
            lo_upto("ffn1")
            chain = [0]

            def link(ins):
                chain[0] += 1
                ins.then_inc(S("angle_chain"), 1)
                dve.wait_ge(*reach("angle_chain", chain[0]))

            dve.wait_ge(*reach("ld_pos", 16))
            posf = stat("posf", NT)
            link(dve.tensor_copy(posf, pos[:]))
            ang, k, r, r2 = rope1[:, 0], rope1[:, 1], rope1[:, 4], rope1[:, 5]
            dve.wait_ge(*reach("ld_const", 16))
            for t in range(NT):
                m = dve.tensor_scalar(ang[:, t], const("invf"), posf[:, t:t + 1], None, ALU.mult)
                link(m)
            link(dve.tensor_scalar(k, ang, float(1 / (2 * np.pi)), 12582912.0, ALU.mult, ALU.add))
            link(dve.tensor_scalar(k, k, 12582912.0, None, ALU.subtract))
            c1 = 6.28125
            c2 = float(np.float32(np.floor((2 * np.pi - c1) * 2 ** 17) / 2 ** 17))
            c3 = float(np.float32(2 * np.pi - c1 - c2))
            src = ang
            for n, part in enumerate((c1, c2, c3)):
                dst = (rope1[:, 2], rope1[:, 3], r)[n]
                link(dve.scalar_tensor_tensor(dst, k, -part, src, ALU.mult, ALU.add))
                src = dst
            lim = 3.1415925
            link(dve.tensor_scalar(r2, r, float(np.pi / 2), None, ALU.add))
            link(dve.tensor_scalar(rope1[:, 2], r2, float(np.pi), -float(2 * np.pi), ALU.is_gt, ALU.mult))
            link(dve.tensor_tensor(r2, r2, rope1[:, 2], ALU.add))
            for v in (r, r2):
                dve.tensor_scalar(v, v, lim, -lim, ALU.min, ALU.max).then_inc(S("angles"), 1)
            dve_ffn("ffn1", NF)

            dve_norm("n2", "mix_norm")
            lo_upto("lat2")
            dve.wait_ge(*reach("lat_r", 2))
            for t in range(NT):
                for k, (lo, hi) in enumerate(((0, QL), (QL, QL + KVL))):
                    dve.tensor_scalar(CQ[:, t, lo:hi], CQ[:, t, lo:hi], stat("lat", 4)[:, 2 * k + t:2 * k + t + 1], None,
                                      ALU.mult).then_inc(S("lat_n"), 1)
            lo_upto("sv1")
            for c in range(5):
                dve.wait_ge(*reach("lt_hi", min(5, c // 2 * 2 + 2)))
                gain = gcol("q_latent_norm", c) if c < 3 else gcol("kv_latent_norm", c - 3)
                dve.scalar_tensor_tensor(Ll[:, c], bank[1 + c // 2][:, c % 2 * T:(c % 2 + 1) * T], gain, Lh[:, c].bitcast(F32),
                                         ALU.mult, ALU.subtract).then_inc(S("lt_lo"), 1)
            lo_upto("kvup")
            dve.wait_ge(*reach("ld_pb", 16 * len(pb_list)))
            dve_head_sums("hq", MH, QK)
            dve_head_sums("hk", MH, QK)
            lo_upto("gate1")
            dve_head_scale("hq", Q1, MH, QK, "q_head_norm")
            dve.wait_ge(*reach("rope1", 2))
            dve_rope("hq", Q1, MH, NOPE, ROPE // 2, COS1, SIN1)
            lo_upto("gate2")
            dve_head_scale("hk", K1[:], MH, QK, "k_head_norm")
            dve.wait_ge(*reach("hq_turn", 6))
            dve_rope("hk", K1[:], MH, NOPE, ROPE // 2, COS1, SIN1)
            for j in range(4):
                dve.wait_ge(*reach("kt_tr", j + 1))
                dve.tensor_copy(KT1[:, 2 * j:2 * j + 2].rearrange("p h n -> p (h n)"), bank[(6, 7, 0, 1)[j]][0:QK, :]).then_inc(S("kt_ev"), 1)
            for i in range(8 + 6):
                if i < 8:
                    lo_upto(f"gate{min(7, 3 + i)}")
                    dve.wait_ge(*reach("sb_l", 3 * i + 3))
                    if i >= 2:
                        dve.wait_ge(*reach("sb_t", i - 1))
                    dve.scalar_tensor_tensor(aw[:, 2 + i % 2], bank[i % 4][:, 0:384], 0.0, aw[:, i % 2], ALU.max,
                                             ALU.add).then_inc(S("sb_sp"), 1)
                h = i - 2
                if 0 <= h < 8:
                    dve.wait_ge(*reach("sb_t", h + 1))
                    if h >= 2:
                        dve.wait_ge(*reach("sb_av", h - 1))
                    dve.scalar_tensor_tensor(aw[:, 4 + h % 2], bank[h % 4][:, 0:384], 0.0, const("earlier_bias"), ALU.min,
                                             ALU.add).then_inc(S("sb_m"), 1)
                h = i - 5
                if h >= 0 and h % 2 == 1:
                    dve.wait_ge(*reach("os_hi", h // 2 + 1))
                    dve.tensor_tensor(OSl[:, h // 2], bank[4 + (h // 2) % 2][:, 0:T], OSh[:, h // 2].bitcast(F32),
                                      ALU.subtract).then_inc(S("os_lo"), 1)
            lo_upto("mla0")
            dve.wait_ge(*reach("sb_av", 8))
            dve_attention("mla", MH, const("causal"), QK ** -0.5, OMh, OMl)
            for q in range(4):
                lo_upto(f"sbr{q // 2}")
                used(dve, f"sbr{q // 2}")
                dve.wait_ge(*reach("gsig", 4))
                ga, gb = (GT[:, 8 * k + 2 * q:8 * k + 2 * q + 2].rearrange("p c n -> p (c n)") for k in range(2))
                dve.tensor_tensor(ga, ga, bank[q][:, :], ALU.mult).then_inc(S("mg_a"), 1)
                dve.tensor_tensor(gb, gb, bank[4 + q][:, :], ALU.mult).then_inc(S("mg_b"), 1)
                dve.wait_ge(*reach("mg_b", q + 1))
                dve.tensor_tensor(sgh[:, q % 2], ga, gb, ALU.add).then_inc(S("mg_s"), 1)
                dve.wait_ge(*reach("mg_hi", q + 1))
                u = slice(2 * q, 2 * q + 2)
                dve.tensor_tensor(Ul[:, u].rearrange("p c n -> p (c n)"), sgh[:, q % 2], Uh[:, u].rearrange("p c n -> p (c n)").bitcast(F32),
                                  ALU.subtract).then_inc(S("mg_lo"), 1)
            dve.wait_ge(*reach("p_hi", 1))
            dve.tensor_tensor(OMl[:, 0:2].rearrange("p c n -> p (c n)"), bank[6][:, :],
                              OMh[:, 0:2].rearrange("p c n -> p (c n)").bitcast(F32), ALU.subtract).then_inc(S("p_lo"), 1)
            for i in range(4):
                lo_upto(f"wout{i}")
                used(dve, f"wout{i}")
                xs_ = X[:, :, i * 256:(i + 1) * 256]
                dve.tensor_tensor(xs_, xs_, bank[i].rearrange("p (t n) -> p t n", t=NT), ALU.add).then_inc(S("x2"), 1)
            dve.wait_ge(*reach("x2", 4))
            dve_norm("n3", "ffn2_norm")
            dve_ffn("ffn2", NF)
            dve_norm("n4", "ple_norm")
            for c in range(4):
                lo_upto(f"pgate{c}")
                dve.wait_ge(*reach("pg", c + 1))
                dve.wait_ge(*reach("pp_ev", c + 1))
                g3 = sgh[:, c % 2].rearrange("p (t n) -> p t n", t=NT)
                dve.tensor_tensor(g3, g3, PP[:, :, c * 256:(c + 1) * 256], ALU.mult).then_inc(S("pm"), 1)
                dve.wait_ge(*reach("pm", c + 1))
                xs_ = X[:, :, c * 256:(c + 1) * 256]
                dve.tensor_tensor(xs_, xs_, g3, ALU.add).then_inc(S("x4"), 1)

            dve.wait_ge(*reach("x4", 4))
            dve_norm("n5", "attn_norm_2")
            lo_upto("ik_dt")
            dve.wait_ge(*reach("b2_ev", 10))
            cos2, sin2 = (const(n).rearrange("p (t d) -> p t d", t=NT) for n in ("cos2", "sin2"))
            ik4 = IKW[:, :, 0:HD].unsqueeze(2)
            R2 = HD // 4 // 2
            dve_head_sums("ik", 1, HD)
            dve_head_sums("k2", KVH2, HD)
            dve_head_sums("q2", H2, HD)
            iws = stat("iws", NT * IH).rearrange("p (t h) -> p t h", t=NT)
            dve.tensor_scalar(iws, IKW[:, :, HD:], IH ** -0.5, None, ALU.mult).then_inc(S("iws"), 1)
            dve.tensor_tensor(ssm[:, 0:2], ssm[:, 0:2], pb("dt_bias_2").unsqueeze(1).to_broadcast([P, NT, SH]), ALU.add).then_inc(S("dt_x"), 1)
            dve.wait_ge(*reach("q2_red", 2))
            dve_rope("iq", IQ[:], IH, 0, R2, cos2, sin2)
            dve_head_scale("ik", ik4, 1, HD, "idx_k_norm_2")
            dve.wait_ge(*reach("iq_turn", 6))
            dve_rope("ik", ik4, 1, 0, R2, cos2, sin2)
            dve.wait_ge(*reach("ik_turn", 6))
            dve.tensor_copy(IKd[:], IKW[:, :, 0:HD].unsqueeze(2).to_broadcast([P, NT, 2, HD])).then_inc(S("ikd"), 1)
            dve_head_scale("k2", K2[:], KVH2, HD, "k_norm_2")
            dve_rope("k2", K2[:], KVH2, 0, R2, cos2, sin2)
            dve.wait_ge(*reach("k2_turn", 6))
            dve.tensor_copy(K2d[:].rearrange("p t h a d -> p (t h) a d"),
                            K2[:].rearrange("p t h d -> p (t h) d").unsqueeze(2).to_broadcast([P, NT * KVH2, 2, HD])).then_inc(S("k2d"), 1)
            lo_upto("ik_dt", 1)
            dve_head_scale("q2", Q2, H2, HD, "q_norm_2")
            dve_rope("q2", Q2, H2, 0, R2, cos2, sin2)
            dve.wait_ge(*reach("dt_l", 4))
            dve.scalar_tensor_tensor(ssm[:, 0:2], ssm[:, 0:2], 0.0, ssm[:, 2:4], ALU.max, ALU.add).then_inc(S("dt_d"), 1)
            dve.wait_ge(*reach("dt_d", 1))
            dve.scalar_tensor_tensor(ssm[:, 2:4], ssm[:, 0:2], -1.0, ssm[:, 8:9].to_broadcast([P, NT, SH]), ALU.mult,
                                     ALU.mult).then_inc(S("dt_d"), 1)
            lo_upto("xbc1")
            dve.wait_ge(*reach("ikt_tr", 1))
            dve.tensor_copy(IKT[:], bank[6][:, 0:T]).then_inc(S("ikt_ev"), 1)
            for i in range(2):
                dve.wait_ge(*reach("kt2_tr", i + 1))
                dve.tensor_copy(KT2[:, 2 * i:2 * i + 2].rearrange("p c n -> p (c n)"), bank[(7, 0)[i]][:, :]).then_inc(S("kt2_ev"), 1)
            for h in range(IH):
                dve.wait_ge(*reach("ix_r", h + 1))
                for t, (lo, hi) in enumerate(((0, P), (P, 3 * P))):
                    if h:
                        dve.wait_ge(*reach("ix_a", 2 * h - 1 + t))
                    else:
                        dve.wait_ge(*reach("iws", 1))
                    acc = const("admit") if h == 0 else SCO
                    dve.scalar_tensor_tensor(SCO[:, lo:hi], aw[:, h % 3, lo:hi], iws[:, t, h:h + 1], acc[:, lo:hi], ALU.mult,
                                             ALU.add).then_inc(S("ix_a"), 1)
            def conv(j):
                for s_ in range(1, TAPS):
                    for c in range(2):
                        ch = 2 * j + c
                        dve.wait_ge(*reach("xb_ev", 3 * j + 3))
                        if s_ > 1:
                            dve.wait_ge(*reach("conv", 6 * j + 2 * (s_ - 2) + c + 1))
                        dve.scalar_tensor_tensor(XC[:, ch, s_:T], sgh[:, j % 2, c * T:(c + 1) * T - s_],
                                                 gcol("conv_w_2", (TAPS - 1 - s_) * NX + ch), XC[:, ch, s_:T], ALU.mult,
                                                 ALU.add).then_inc(S("conv"), 1)

            top8 = stat("top8", 16)
            dve.wait_ge(*reach("ix_a", 2 * IH))
            for r in range(TOPK // 8):
                for t, (lo, hi) in enumerate(((0, P), (P, 3 * P))):
                    if r:
                        dve.wait_ge(*reach("topk_taken", 2 * r - 1 + t))
                    dve.max(top8[:, 8 * t:8 * t + 8], SCO[:, lo:hi]).then_inc(S("topk_max"), 1)
                for t, (lo, hi) in enumerate(((0, P), (P, 3 * P))):
                    dve.wait_ge(*reach("topk_max", 2 * r + 1 + t))
                    dve.match_replace(SCO[:, lo:hi], top8[:, 8 * t:8 * t + 8], SCO[:, lo:hi], TAKEN).then_inc(S("topk_taken"), 1)
                if r % 2 == 0:
                    if r:
                        conv(r // 2 - 1)
                    lo_upto(("xbc2", "xbc3", "g0", "g1")[r // 2])
            dve.wait_ge(*reach("topk_taken", 2 * (TOPK // 8)))
            dve.tensor_scalar(SELB[:], SCO, TAKEN / 2, LOW, ALU.is_gt, ALU.mult).then_inc(S("selb"), 1)
            dve.wait_ge(*reach("selb", 1))

            conv(3)
            mx, nmx, sm, rs = (stat(f"att_{k}", 32) for k in range(4))
            for i in range(H2 + 5):
                if i < H2:
                    dve.wait_ge(*reach("dsa_s", i + 1))
                    if i >= 3:
                        dve.wait_ge(*reach("dsa_pt", i - 2))
                    for t, (lo, hi) in enumerate(((0, P), (P, 3 * P))):
                        dve.tensor_tensor_reduce(out=aw[:, i % 3, lo:hi], in0=bank[i % 3][:, lo:hi], in1=SELB[:, lo:hi],
                                                 scale=1.0, scalar=-3e38, op0=ALU.add, op1=ALU.max,
                                                 accum_out=mx[:, 2 * i + t:2 * i + t + 1]).then_inc(S("dsa_mx"), 1)
                    dve.wait_ge(*reach("dsa_mx", 2 * i + 2))
                    dve.tensor_scalar(nmx[:, 2 * i:2 * i + 2], mx[:, 2 * i:2 * i + 2], -HD ** -0.5, None,
                                      ALU.mult).then_inc(S("dsa_nm"), 1)
                if 1 <= i < H2 + 1:
                    h = i - 1
                    dve.wait_ge(*reach("dsa_exp", 2 * h + 2))
                    dve.reciprocal(rs[:, 2 * h:2 * h + 2], sm[:, 2 * h:2 * h + 2]).then_inc(S("dsa_rs"), 1)
                    dve.wait_ge(*reach("dsa_rs", h + 1))
                    for t, (lo, hi) in enumerate(((0, P), (P, 3 * P))):
                        dve.tensor_scalar(aw[:, h % 3, lo:hi], aw[:, h % 3, lo:hi], rs[:, 2 * h + t:2 * h + t + 1], None,
                                          ALU.mult).then_inc(S("dsa_pn"), 1)
                h = i - 4
                if h >= 0 and h % 2 == 1:
                    dve.wait_ge(*reach("dsa_ohi", h // 2 + 1))
                    dve.tensor_tensor(OAl[:, h // 2], bank[5 + (h // 2) % 2][:, 0:T], OAh[:, h // 2].bitcast(F32),
                                      ALU.subtract).then_inc(S("dsa_olo"), 1)
                if 4 + i // 2 < NX // 2:
                    if i % 2 == 0:
                        lo_upto(f"xbc{4 + i // 2}")
                    else:
                        conv(4 + i // 2)
                if i in (H2, H2 + 2):
                    lo_upto("g2" if i == H2 else "g3")
            lo_upto("wa0")
            dve.wait_ge(*reach("acs_mm", 1))
            dve.tensor_copy(ssm[:, 4:7].rearrange("p a h -> p (a h)"), bank[5][:, 0:3 * SH]).then_inc(S("acs"), 1)
            dve.wait_ge(*reach("acs", 1))
            dve.tensor_tensor(ssm[:, 7], ssm[:, 6], ssm[:, 4], ALU.subtract).then_inc(S("acs"), 1)
            for t in range(NT):
                dve.wait_ge(*reach("cb_mm", t + 1))
                dve.tensor_tensor(CBM[:, t], bank[(6, 7)[t]].rearrange("p (g n) -> p g n", g=SG),
                                  const("upto").unsqueeze(1).to_broadcast([P, SG, P]), ALU.mult).then_inc(S("cbm"), 1)
            dve.wait_ge(*reach("ee", 1))
            dve.tensor_tensor(ssm[:, 7], ssm[:, 7], ssm[:, 0], ALU.mult).then_inc(S("fe"), 1)
            for u in range(9):
                if u < 8:
                    t, g = divmod(u, 4)
                    if u < 6:
                        lo_upto(f"wa{u}" if u < 4 else f"g{u}")
                    for k in range(2):
                        n = 2 * u + k
                        dve.wait_ge(*reach("seg_mm", n + 1))
                        if n >= 4:
                            dve.wait_ge(*reach("y_mm", (n - 4) // 2 + 1))
                        h0 = 8 * g + 4 * k
                        for h in range(4):
                            hc = slice(h * P, (h + 1) * P)
                            last = dve.tensor_scalar(EM(n)[:, hc], bank[n % 4][:, hc], ssm[:, 4 + t, h0 + h:h0 + h + 1], 0.0,
                                                     ALU.subtract, ALU.min)
                        last.then_inc(S("seg"), 1)
                    for k in range(2):
                        n = 2 * u + k
                        dve.wait_ge(*reach("seg_e", n + 1))
                        dve.wait_ge(*reach("cbm", 2))
                        e3 = EM(n).rearrange("p (h n) -> p h n", h=4)
                        dve.tensor_tensor(e3, e3, CBM[:, t, g].unsqueeze(1).to_broadcast([P, 4, P]), ALU.mult).then_inc(S("seg_m"), 1)
                if u >= 1:
                    v = u - 1
                    t, g = divmod(v, 4)
                    yv = XS[:, t, g * 512:(g + 1) * 512]
                    dve.wait_ge(*reach("xsd", v + 1))
                    dve.wait_ge(*reach("y_mm", v + 1))
                    dve.tensor_tensor(yv, yv, bank[4 + v % 2][:, :], ALU.add).then_inc(S("y"), 1)
                    if t:
                        n = 4 + 2 * g
                        if g:
                            dve.wait_ge(*reach("y", n))
                        dve.tensor_tensor(sgh[:, 0].rearrange("p (h n) -> p h n", h=8), bank[6].rearrange("p (h n) -> p h n", h=8),
                                          ssm[:, 9, 8 * g:8 * g + 8].unsqueeze(2).to_broadcast([P, 8, 64]), ALU.mult).then_inc(S("yo"), 1)
                        dve.wait_ge(*reach("yo", g + 1))
                        dve.wait_ge(*reach("y", n + 1))
                        dve.tensor_tensor(yv, yv, sgh[:, 0], ALU.add).then_inc(S("y"), 1)
            for c in range(8):
                lo_upto(f"z{c}")
                dve.wait_ge(*reach("z_s", c + 1))
                dve.wait_ge(*reach("y", 12))
                v = XS[:, :, c * 256:(c + 1) * 256]
                dve.tensor_tensor(v, v, sgh[:, c % 2].rearrange("p (t n) -> p t n", t=NT), ALU.mult).then_inc(S("yz"), 1)
            lo_upto("g6")
            dve.wait_ge(*reach("yg_r", 1))
            dve.wait_ge(*reach("yz", 8))
            for g in range(SG):
                for t in range(NT):
                    v = XS[:, t, g * 512:(g + 1) * 512]
                    dve.tensor_scalar(v, v, stat("yg", 8)[:, 4 * t + g:4 * t + g + 1], None, ALU.mult).then_inc(S("yn"), 1)
            lo_upto("g7")
            for j in range(8):
                dve.wait_ge(*reach("yt_hi", 2 * j + 2))
                for c in range(2):
                    dve.scalar_tensor_tensor(YTl[:, 2 * j + c], bank[j % 4][:, c * T:(c + 1) * T], gcol("ssd_norm_2", 2 * j + c),
                                             YTh[:, 2 * j + c].bitcast(F32), ALU.mult, ALU.subtract).then_inc(S("yt_lo"), 1)
            for q in range(4):
                lo_upto(f"ws{q}1")
                used(dve, f"ws{q}1")
                dve.wait_ge(*reach("g2sig", 4))
                ga, gb = (G2[:, 8 * k + 2 * q:8 * k + 2 * q + 2].rearrange("p c n -> p (c n)") for k in range(2))
                dve.tensor_tensor(ga, ga, BA[:, 2 * q:2 * q + 2].rearrange("p c n -> p (c n)"), ALU.mult).then_inc(S("m2_a"), 1)
                dve.tensor_tensor(gb, gb, bank[4 + q][:, :], ALU.mult).then_inc(S("m2_b"), 1)
                dve.wait_ge(*reach("m2_b", q + 1))
                dve.tensor_tensor(sgh[:, q % 2], ga, gb, ALU.add).then_inc(S("m2_s"), 1)
                dve.wait_ge(*reach("m2_hi", q + 1))
                u = slice(2 * q, 2 * q + 2)
                dve.tensor_tensor(Ul[:, u].rearrange("p c n -> p (c n)"), sgh[:, q % 2], Uh[:, u].rearrange("p c n -> p (c n)").bitcast(F32),
                                  ALU.subtract).then_inc(S("m2_lo"), 1)
            for i in range(4):
                lo_upto(f"wo{i}")
                used(dve, f"wo{i}")
                xs_ = X[:, :, i * 256:(i + 1) * 256]
                dve.tensor_tensor(xs_, xs_, bank[i].rearrange("p (t n) -> p t n", t=NT), ALU.add).then_inc(S("x5"), 1)
            dve.wait_ge(*reach("x5", 4))
            dve_norm("n6", "ffn_norm_2")
            lo_upto("router")
            used(dve, "router")
            n_r = [0]

            def rlink(ins):
                n_r[0] += 1
                ins.then_inc(S("route"), 1)
                dve.wait_ge(*reach("route", n_r[0]))

            tk = lambda at, n: bank[0].rearrange("p (t n) -> p t n", t=NT)[:, :, at:at + n]
            bc = lambda v, axis, shape: v.unsqueeze(axis).to_broadcast(shape)
            gl, el = rt("gl", 8).rearrange("p (t g) -> p t g", t=NT), rt("el", 64).rearrange("p (t n) -> p t n", t=NT)
            rlink(dve.tensor_tensor(gl, tk(0, EG), bc(pb("b_route_group_2"), 1, [P, NT, EG]), ALU.add))
            rlink(dve.tensor_tensor(el, tk(EG, NE), bc(pb("b_route_expert_2"), 1, [P, NT, NE]), ALU.add))
            gmax, gexp = rt("gmax", 2), rt("gexp", 8).rearrange("p (t g) -> p t g", t=NT)
            rlink(dve.tensor_reduce(gmax, gl, AX, ALU.max))
            dve.tensor_tensor(gexp, gl, bc(gmax, 2, [P, NT, EG]), ALU.subtract).then_inc(S("r_gl"), 1)

            def ranks(nm, v, n):
                a_, b_ = (rt(nm + x, NT * n * n).rearrange("p (t i j) -> p t i j", t=NT, i=n) for x in "ab")
                vj, vi = bc(v, 2, [P, NT, n, n]), bc(v, 3, [P, NT, n, n])
                before = const("before").rearrange("p (i j) -> p i j", i=EPG)[:, 0:n, 0:n]
                dve.tensor_tensor(a_, vj, vi, ALU.is_gt).then_inc(S("route"), 1)
                n_r[0] += 1
                rlink(dve.tensor_tensor(b_, vj, vi, ALU.is_equal))
                for t in range(NT):
                    dve.tensor_tensor(b_[:, t], b_[:, t], before, ALU.mult).then_inc(S("route"), 1)
                    n_r[0] += 1
                dve.wait_ge(*reach("route", n_r[0]))
                rlink(dve.tensor_tensor(a_, a_, b_, ALU.add))
                r_ = rt(nm + "r", NT * n).rearrange("p (t i) -> p t i", t=NT)
                rlink(dve.tensor_reduce(r_, a_, AX, ALU.add))
                return r_

            gr = ranks("g", gl, EG)
            oh = rt("oh", 8).rearrange("p (t g) -> p t g", t=NT)
            dve.tensor_scalar(oh, gr, 0.0, None, ALU.is_equal).then_inc(S("oh"), 1)
            dve.wait_ge(*reach("oh", 1))
            for t in range(NT):
                dve.wait_ge(*reach("xn_hi", t + 1))
                dve.tensor_tensor(XNl[:, t], xn[:, t], XNh[:, t].bitcast(F32), ALU.subtract).then_inc(S("xn_lo"), 1)
            dve.wait_ge(*reach("rank_mm", 1))
            ahead = bank[2][:, 0:NT * EG]
            key, mine = rt("key", NT * EG), rt("mine", NT * EG)
            rlink(dve.scalar_tensor_tensor(key, rt("oh", 8), -FAR, ahead, ALU.mult, ALU.add))
            for t in range(NT):
                for g in range(EG):
                    dve.tensor_scalar(PICK[:, t, g], const("slot"), key[:, EG * t + g:EG * t + g + 1], None,
                                      ALU.is_equal).then_inc(S("pick"), 1)
            rlink(dve.tensor_tensor(mine, rt("oh", 8), ahead, ALU.mult))
            rlink(dve.tensor_reduce(rt("rank", NT), mine.rearrange("p (t g) -> p t g", t=NT), AX, ALU.add))
            rlink(dve.tensor_scalar(rt("rank", NT), rt("rank", NT), -FAR - P, None, ALU.add))
            for t in range(NT):
                dve.tensor_scalar(PICK[:, t, EG], const("slot"), rt("rank", NT)[:, t:t + 1], None, ALU.is_equal).then_inc(S("pick"), 1)
            big, ov = rt("big", 2 * EG), rt("ov", 2)
            rlink(dve.tensor_scalar(big[:, 0:EG], bank[2][:, NT * EG:(NT + 1) * EG], float(P), None, ALU.is_gt))
            rlink(dve.tensor_tensor(big[:, EG:], big[:, 0:EG], const("group_base"), ALU.mult))
            rlink(dve.tensor_reduce(ov, big.rearrange("p (a g) -> p a g", a=2), AX, ALU.add))
            dve.tensor_copy(OV[:], ov).then_inc(S("over"), 1)
            e4 = rt("e4", 64).rearrange("p (t g e) -> p t g e", t=NT, g=EG)
            rlink(dve.tensor_tensor(e4, el.rearrange("p t (g e) -> p t g e", g=EG), bc(oh, 3, [P, NT, EG, EPG]), ALU.mult))
            ein = rt("ein", 16).rearrange("p (t e) -> p t e", t=NT)
            rlink(dve.tensor_reduce(ein, e4.rearrange("p t g e -> p t e g"), AX, ALU.add))
            er = ranks("e", ein, EPG)
            v01, picks = rt("v01", 4), []
            for k in range(2):
                pk = rt(f"pick{k}", 16).rearrange("p (t e) -> p t e", t=NT)
                rlink(dve.tensor_scalar(pk, er, float(k), None, ALU.is_equal))
                pe_ = rt(f"pv{k}", 16).rearrange("p (t e) -> p t e", t=NT)
                rlink(dve.tensor_tensor(pe_, pk, ein, ALU.mult))
                rlink(dve.tensor_reduce(v01[:, 2 * k:2 * k + 2], pe_, AX, ALU.add))
                picks.append(pk)
            dve.tensor_tensor(rt("d", 2), v01[:, 2:4], v01[:, 0:2], ALU.subtract).then_inc(S("r_d"), 1)
            dve.wait_ge(*reach("r_e", 2))
            den = rt("den", 4)
            rlink(dve.tensor_reduce(den[:, 0:2], gexp, AX, ALU.add))
            rlink(dve.tensor_scalar(den[:, 2:4], rt("d", 2), 1.0, None, ALU.add))
            rlink(dve.reciprocal(den, den))
            w01 = rt("w01", 4)
            rlink(dve.tensor_tensor(w01[:, 0:2], den[:, 0:2], den[:, 2:4], ALU.mult))
            rlink(dve.tensor_tensor(w01[:, 2:4], w01[:, 0:2], rt("d", 2), ALU.mult))
            for k in range(2):
                rlink(dve.tensor_tensor(picks[k], picks[k], bc(w01[:, 2 * k:2 * k + 2], 2, [P, NT, EPG]), ALU.mult))
            dve.tensor_tensor(picks[0], picks[0], picks[1], ALU.add).then_inc(S("cw"), 1)
            for c in range(KD):
                dve.wait_ge(*reach("su_hi", c + 1))
                dve.scalar_tensor_tensor(SUl[:, c].rearrange("p g n -> p (g n)"), bank[4 + c % 4][:, :], gcol("ffn_norm_2", c),
                                         SUh[:, c].rearrange("p g n -> p (g n)").bitcast(F32), ALU.mult,
                                         ALU.subtract).then_inc(S("su_lo"), 1)
            dve.wait_ge(*reach("cw_ev", 1))
            dve_experts(slab_of["moe"], NE, 0, 0)
            flag = overflow(dve)
            with dve.If(flag != 0):
                for c in range(KD):
                    dve.wait_ge(*reach("su_hi", KD + c // 4 * 4 + 4))
                    dve.scalar_tensor_tensor(SUl[:, c, 0], bank[4 + c // 4][:, c % 4 * P:(c % 4 + 1) * P], gcol("ffn_norm_2", c),
                                             SUh[:, c, 0].bitcast(F32), ALU.mult, ALU.subtract).then_inc(S("su_lo"), 1)
                split_lo(over)
                split_lo(over + 1)
                dve_experts(over, EPG, NE, EG)

        @block.gpsimd
        def _(_e):
            pool.memset(halves, -0.5).then_inc(S("halves"), 1)
            pool.wait_ge(*reach("halves", 1))
            pool_norm("n1")
            pool.wait_ge(*reach("zeroed", 1))
            pool_ffn("ffn1", NF)

            pool_norm("n2")
            pool.wait_ge(*reach("lat_ev", 3))
            pool.tensor_copy(K1[:, :, :, NOPE:QK], CQ[:, :, QL + KVL:C1_SQ].unsqueeze(2).to_broadcast([P, NT, MH, ROPE])).then_inc(S("krope"), 1)
            pool.wait_ge(*reach("lat_ss", 4))
            for k, n in enumerate((QL, KVL)):
                v = stat("lat", 4)[:, 2 * k:2 * k + 2]
                pool_rsqrt(v, v, n, "lat_r")
            pool_head_rsqrt("hq", MH, QK)
            pool_head_rsqrt("hk", MH, QK)
            for i in range(8):
                pool.wait_ge(*reach("sb_sp", i + 1))
                pool.tensor_tensor(aw[:, 2 + i % 2], aw[:, 2 + i % 2], const("earlier"), ALU.mult).then_inc(S("sb_spm"), 1)
            pool_norm("n3")
            pool_ffn("ffn2", NF)
            pool_norm("n4")

            pool_norm("n5")
            pool_head_rsqrt("ik", 1, HD)
            pool_head_rsqrt("k2", KVH2, HD)
            pool_head_rsqrt("q2", H2, HD)
            per_head = lambda v: v.unsqueeze(2).to_broadcast([P, 8, SP])
            for u in range(8):
                t, g = divmod(u, 4)
                hs = slice(8 * g, 8 * g + 8)
                x3 = XS[:, t, g * 512:(g + 1) * 512].rearrange("p (h d) -> p h d", h=8)
                pool.wait_ge(*reach("xs_ev", 8))
                pool.wait_ge(*reach("fe", 1))
                if u >= 2:
                    pool.wait_ge(*reach("y_mm", u - 1))
                pool.tensor_tensor(Xd[:, u % 2].rearrange("p (h d) -> p h d", h=8), x3, per_head(ssm[:, t, hs]), ALU.mult).then_inc(S("xd"), 1)
                if t == 0:
                    if u:
                        pool.wait_ge(*reach("st_mm", u))
                    pool.tensor_tensor(Xe[:].rearrange("p (h d) -> p h d", h=8), x3, per_head(ssm[:, 7, hs]), ALU.mult).then_inc(S("xe"), 1)
                pool.tensor_tensor(x3, x3, per_head(pb("d_skip_2")[:, hs]), ALU.mult).then_inc(S("xsd"), 1)
                if u == 4:
                    pool.wait_ge(*reach("g2_ev", 4))
                    pool.wait_ge(*reach("side_ev", 4))
                    pool.tensor_copy(G2[:, 0:8].rearrange("p c n -> p (c n)"), G2a[:].rearrange("p c n -> p (c n)")).then_inc(S("g2_moved"), 1)
            pool.wait_ge(*reach("yg_ss", 8))
            pool_rsqrt(stat("yg", 8), stat("yg", 8), DI // SG, "yg_r")
            pool_norm("n6")
            pool_experts(EG, 0)
            pool.wait_ge(*reach("over", 1))
            flag = overflow(pool)
            with pool.If(flag != 0):
                pool_experts(1, EG)

        @block.tensor
        def _(_e):
            pe.wait_ge(*reach("ld_ident", 16))
            pe.wait_ge(*reach("ld_rows", 16 * (len(gain_rows) + 1)))
            for j, (rows, nr) in enumerate(((rows1, n_rows1), (rows2, n_rows2))):
                claim(j, "gains", j + 1)
                pe.transpose(bank[j][:, 0:nr], rows[0:nr, :], ident[0:nr, 0:nr]).then_inc(S("rows_tr"), 1)
            pe_norm("n1")
            pe.wait_ge(*reach("zeroed", 1))
            pe_ffn("ffn1", NF)
            pe.wait_ge(*reach("ld_const", 16))

            pe_norm("n2")
            for i in range(3):
                s_ = need(f"lat{i}")
                claim(i, "lat_ev", i + 1)
                by_token(s_, i, Uh, Ul, KD, slabs[s_][2]).then_inc(S("slab_used"), 1)
            for j, nm in enumerate(("sq", "sk")):
                for i in range(2):
                    s_ = need(f"{nm}{i}")
                    claim(3 + 2 * j + i, "sqk_ev", 2 * j + i + 1)
                    by_feature(s_, 3 + 2 * j + i, Uh, Ul, KD, 256).then_inc(S("slab_used"), 1)
            for i in range(2):
                s_ = need(f"sv{i}")
                claim((7, 0)[i], "sv_ev", i + 1)
                by_token(s_, (7, 0)[i], Uh, Ul, KD, 256).then_inc(S("slab_used"), 1)
            pe.wait_ge(*reach("lat_n", 4))
            for c in range(5):
                if c % 2 == 0:
                    claim(1 + c // 2, "lt_lo", min(5, c + 2))
                for t in range(NT):
                    last = pe.transpose(bank[1 + c // 2][:, c % 2 * T + t * P:c % 2 * T + (t + 1) * P], CQ[:, t, c * P:(c + 1) * P], ident)
                if c in (1, 3, 4):
                    last.then_inc(S("lt_tr"), 1)
            fresh.append(("lt_lo", 1, Lh))
            for i in range(2):
                s_ = need(f"qup{i}")
                for t in range(NT):
                    b = 4 + t if i == 0 else t
                    claim(b, "q_ev", 2 * i + t + 1)
                    last = by_token(s_, b, Lh, Ll, 3, 384, tiles=[t])
                last.then_inc(S("slab_used"), 1)
            pe.wait_ge(*reach("lt_lo", 5))
            s_ = need("kvup")
            for t in range(NT):
                for half in range(2):
                    b = (2, 3, 6, 7)[2 * t + half]
                    claim(b, "kv_ev", 2 * (2 * t + half) + 2)
                    last = by_token(s_, b, Lh, Ll, 2, 1024, k0=3, c0=half * 512, c1=(half + 1) * 512, tiles=[t])
            last.then_inc(S("slab_used"), 1)

            def gate(g, b):
                s_ = need(f"gate{g}")
                claim(b, "gate_ev", g + 1)
                by_feature(s_, b, Uh, Ul, KD, 256).then_inc(S("slab_used"), 1)

            for g in range(3):
                gate(g, (4, 5, 4)[g])
            for nm, buf, banks, done in (("hq", Q1, (0, 1, 2, 3), "qt"), ("hk", K1[:], (6, 7, 0, 1), "kt")):
                pe.wait_ge(*reach(nm + "_turn", 6))
                for j in range(4):
                    claim(banks[j], done + "_ev", j + 1)
                    for h in range(2):
                        for t in range(NT):
                            last = pe.transpose(bank[banks[j]][0:QK, h * T + t * P:h * T + (t + 1) * P], buf[:, t, 2 * j + h], ident)
                    last.then_inc(S(done + "_tr"), 1)

            pe.wait_ge(*reach("sqk_ev", 4))
            pe.wait_ge(*reach("sv_ev", 2))
            for i in range(8 + 4):
                if i < 8:
                    claim(i % 4, "sb_m", i + 1)
                    rows, c = slice(64 * (i % 2), 64 * (i % 2) + 64), i // 2
                    pe.matmul(bank[i % 4][:, 0:T], skT[rows, c, 0:P], sqT[rows, c, :], start=True, stop=True, skip_group_check=True)
                    pe.matmul(bank[i % 4][:, T:3 * P], skT[rows, c, P:T], sqT[rows, c, P:T], start=False, stop=True,
                              skip_group_check=True).then_inc(S("sb_z"), 1)
                h = i - 2
                if 0 <= h < 8:
                    pe.wait_ge(*reach("sb_spm", h + 1))
                    b, sp_ = bank[h % 4], aw[:, 2 + h % 2]
                    pe.matmul(b[:, 0:T], const("neg_from"), sp_[:, 0:T], start=False, stop=True, skip_group_check=True)
                    pe.matmul(b[:, P:T], const("neg_ones"), sp_[:, T:3 * P], start=False, stop=True, skip_group_check=True)
                    pe.matmul(b[:, T:3 * P], const("neg_from"), sp_[:, T:3 * P], start=False, stop=True,
                              skip_group_check=True).then_inc(S("sb_t"), 1)
                h = i - 4
                if h >= 0:
                    b = 4 + (h // 2) % 2
                    if h % 2 == 0:
                        claim(b, "os_lo", h // 2 + 1)
                    pe.wait_ge(*reach("sb_a", h + 1))
                    o, w_ = bank[b][64 * (h % 2):64 * (h % 2) + 64, 0:T], aw[:, 4 + h % 2]
                    f = slice(h * 64, (h + 1) * 64)
                    pe.matmul(o, sv[:, 0, f], w_[:, 0:T], start=True, stop=False, skip_group_check=True)
                    pe.matmul(o[:, P:T], sv[:, 1, f], w_[:, T:3 * P], start=False, stop=True, skip_group_check=True).then_inc(S("sb_av"), 1)
                if i < 5:
                    gate(3 + i, 6 + i % 2)
            pe.wait_ge(*reach("qt_ev", 4))
            pe.wait_ge(*reach("kt_ev", 4))
            pe.wait_ge(*reach("kv_ev", 8))
            pe_attention("mla", MH, lambda h: QT1[:, h], lambda h: KT1[:, h], lambda h, t: V1[:, t, h])
            for j in range(2):
                for nm, oh, ol, b0, done in (("mla", OMh, OMl, 0, "mg_a"), ("sbr", OSh, OSl, 4, "mg_b")):
                    pe.wait_ge(*reach("mla_olo" if nm == "mla" else "os_lo", 4))
                    s_ = need(f"{nm}{j}")
                    for q in range(2):
                        claim(b0 + 2 * j + q, done, 2 * j + q + 1)
                        last = by_feature(s_, b0 + 2 * j + q, oh, ol, 4, 512, n0=2 * q, n1=2 * q + 2)
                    last.then_inc(S("slab_used"), 1)
            pe.wait_ge(*reach("ld_p", 16))
            claim(6, "p_lo", 1)
            for c in range(2):
                for t in range(NT):
                    last = pe.transpose(bank[6][:, c * T + t * P:c * T + (t + 1) * P], aw[:, t, c * P:(c + 1) * P], ident)
            last.then_inc(S("p_tr"), 1)
            fresh.append(("mg_lo", 2, Uh))
            for i in range(4):
                s_ = need(f"wout{i}")
                claim(i, "x2", i + 1)
                by_token(s_, i, Uh, Ul, KD, 256).then_inc(S("slab_used"), 1)
            pe_norm("n3")
            pe_ffn("ffn2", NF)
            pe_norm("n4")
            pe.wait_ge(*reach("p_lo", 1))
            s_ = need("pproj")
            for c in range(4):
                claim(c, "pp_ev", c + 1)
                last = by_token(s_, c, OMh, OMl, 2, 1024, c0=c * 256, c1=(c + 1) * 256)
            last.then_inc(S("slab_used"), 1)
            for c in range(4):
                s_ = need(f"pgate{c}")
                claim(4 + c, "pg", c + 1)
                by_token(s_, 4 + c, Uh, Ul, KD, 256).then_inc(S("slab_used"), 1)

            pe_norm("n5")
            for n, (nm, b) in enumerate((("q0", 0), ("q1", 1), ("q2", 2), ("q3", 3), ("k", 4), ("v", 5), ("iq0", 6), ("iq1", 7),
                                         ("ik_dt", 0))):
                s_ = need(nm)
                claim(b, "b2_ev", n + 1 if n < 8 else 10)
                by_token(s_, b, Uh, Ul, KD, slabs[s_][2]).then_inc(S("slab_used"), 1)

            def xbc(j):
                s_ = need(f"xbc{j}")
                claim(xbc_bank(j), "xb_ev", 3 * j + 1)
                by_feature(s_, xbc_bank(j), Uh, Ul, KD, 256).then_inc(S("slab_used"), 1)

            def pairs(nm, src, n, banks, done, tr):
                for j in range(n // 2):
                    claim(banks[j], done, j + 1)
                    for c in range(2):
                        for t in range(NT):
                            last = pe.transpose(bank[banks[j]][:, c * T + t * P:c * T + (t + 1) * P], src(t, 2 * j + c), ident)
                    last.then_inc(S(tr), 1)

            xbc(0)
            pe.wait_ge(*reach("iq_turn", 6))
            pairs("iq", lambda t, c: IQ[:, t, 2 * c:2 * c + 2].rearrange("p h d -> p (h d)"), 4, (4, 5), "iqt_ev", "iqt_tr")
            pe.wait_ge(*reach("ikd", 1))
            claim(6, "ikt_ev", 1)
            for t in range(NT):
                last = pe.transpose(bank[6][:, t * P:(t + 1) * P], IKd[:, t].rearrange("p a d -> p (a d)"), ident)
            last.then_inc(S("ikt_tr"), 1)
            pe.wait_ge(*reach("k2d", 1))
            pairs("k", lambda t, c: K2d[:, t, c].rearrange("p a d -> p (a d)"), 4, (7, 0), "kt2_ev", "kt2_tr")
            xbc(1)
            pe.wait_ge(*reach("q2_turn", 6))
            pairs("q", lambda t, c: Q2[:, t, 2 * c:2 * c + 2].rearrange("p h d -> p (h d)"), 8, (1, 4, 5, 6), "qt2_ev", "qt2_tr")
            pe.wait_ge(*reach("iqt_ev", 2))
            pe.wait_ge(*reach("ikt_ev", 1))
            for h in range(IH):
                b, rows = (7, 0, 1, 4)[h % 4], slice(64 * (h % 2), 64 * (h % 2) + 64)
                claim(b, "ix_r", h + 1)
                q_, k_ = IQT[rows, h // 2], IKT[rows, :]
                pe.matmul(bank[b][:, 0:P], q_[:, 0:P], k_[:, 0:P], start=True, stop=True, skip_group_check=True)
                pe.matmul(bank[b][:, P:3 * P], q_[:, P:T], k_, start=False, stop=True, skip_group_check=True).then_inc(S("ix_s"), 1)
            xbc(2)
            xbc(3)

            def gate2(g):
                s_ = need(f"g{g}")
                claim(gate2_bank[g], "g2_ev", g + 1)
                by_feature(s_, gate2_bank[g], Uh, Ul, KD, 256).then_inc(S("slab_used"), 1)

            gate2(0)
            gate2(1)
            pe.wait_ge(*reach("qt2_ev", 4))
            pe.wait_ge(*reach("kt2_ev", 2))
            half = lambda h: slice(64 * (h % 2), 64 * (h % 2) + 64)
            for i in range(-1, H2 + 3):
                if i + 1 < H2:
                    n = i + 1
                    claim(n % 3, "dsa_mx", 2 * n + 2)
                    b, q_, k_ = bank[n % 3], QT2[half(n), n // 2], KT2[half(n), n // 4]
                    pe.matmul(b[:, 0:P], q_[:, 0:P], k_[:, 0:P], start=True, stop=True, skip_group_check=True)
                    pe.matmul(b[:, P:3 * P], q_[:, P:T], k_, start=False, stop=True, skip_group_check=True).then_inc(S("dsa_s"), 1)
                if 2 <= i < H2 + 2:
                    h = i - 2
                    claim(3 + h % 2, "dsa_ptc", h + 1)
                    pe.wait_ge(*reach("dsa_pn", 2 * h + 2))
                    for k in range(3):
                        last = pe.transpose(bank[3 + h % 2][:, k * P:(k + 1) * P], aw[:, h % 3, k * P:(k + 1) * P], ident)
                    last.then_inc(S("dsa_pt"), 1)
                if i >= 3:
                    h = i - 3
                    b = 5 + (h // 2) % 2
                    if h % 2 == 0:
                        claim(b, "dsa_olo", h // 2 + 1)
                    pe.wait_ge(*reach("dsa_ptc", h + 1))
                    o, f = bank[b][half(h), 0:T], slice(h // 4 * HD, (h // 4 + 1) * HD)
                    pe.matmul(o, V2[:, 0, f], aw[:, 3 + h % 2, 0:T], start=True, stop=False, skip_group_check=True)
                    pe.matmul(o[:, P:T], V2[:, 1, f], aw[:, 3 + h % 2, T:3 * P], start=False, stop=True,
                              skip_group_check=True).then_inc(S("dsa_av"), 1)
                if i >= 0 and 4 + i // 2 < NX // 2 and i % 2 == 0:
                    xbc(4 + i // 2)
                if i == H2:
                    gate2(2)
            gate2(3)

            pe.wait_ge(*reach("dt_d", 2))
            claim(5, "acs", 1)
            pe.matmul(bank[5][:, 0:SH], const("upto"), ssm[:, 2], start=True, stop=True, skip_group_check=True)
            pe.matmul(bank[5][:, SH:2 * SH], const("upto"), ssm[:, 3], start=False, stop=True, skip_group_check=True)
            pe.matmul(bank[5][:, 2 * SH:3 * SH], const("ones"), ssm[:, 2], start=False, stop=True,
                      skip_group_check=True).then_inc(S("acs_mm"), 1)
            pe.wait_ge(*reach("xc", 2))
            for t in range(NT):
                claim(6 + t, "cbm", t + 1)
                tk_ = slice(t * P, (t + 1) * P)
                for g in range(SG):
                    last = pe.matmul(bank[6 + t][:, g * P:(g + 1) * P], XC[:, 16 + g, tk_], XC[:, 20 + g, tk_], start=g == 0,
                                     stop=True, skip_group_check=True)
                last.then_inc(S("cb_mm"), 1)
            for j in range(8):
                pe.wait_ge(*reach("xc", 3 + j // 2))
                claim(j % 4, "xs_ev", j + 1)
                for t in range(NT):
                    for c in range(2):
                        last = pe.transpose(bank[j % 4][:, t * T + c * P:t * T + (c + 1) * P], XC[:, 2 * j + c, t * P:(t + 1) * P], ident)
                last.then_inc(S("xs_tr"), 1)
            claim(4, "bt_ev", 1)
            for g in range(SG):
                last = pe.transpose(bank[4][:, g * P:(g + 1) * P], XC[:, 16 + g, 0:P], ident)
            last.then_inc(S("bt_tr"), 1)
            for u in range(9):
                if u < 8:
                    t, g = divmod(u, 4)
                    for k in range(2):
                        n = 2 * u + k
                        claim(n % 4, "seg", n + 1)
                        for h in range(4):
                            col = ssm[:, 2 + t, 8 * g + 4 * k + h:8 * g + 4 * k + h + 1].to_broadcast([P, P])
                            last = pe.matmul(bank[n % 4][:, h * P:(h + 1) * P], col, const("upto"), start=h == 0, stop=True,
                                             skip_group_check=True)
                        last.then_inc(S("seg_mm"), 1)
                    if t == 0:
                        claim(6, "st_ev", g + 1)
                        pe.wait_ge(*reach("bt_ev", 1))
                        pe.wait_ge(*reach("xe", g + 1))
                        pe.matmul(bank[6][:, :], BTM[:, g], Xe[:], start=True, stop=True, skip_group_check=True).then_inc(S("st_mm"), 1)
                    if u < 6:
                        pe.wait_ge(*reach("dsa_olo", 8))
                        s_ = need(f"wa{u}" if u < 4 else f"g{u}")
                        claim(7, "side_ev", u + 1)
                        src = (OAh, OAl) if u < 4 else (Uh, Ul)
                        by_feature(s_, 7, *src, KD, 256).then_inc(S("slab_used"), 1)
                if u >= 1:
                    v = u - 1
                    t, g = divmod(v, 4)
                    if t:
                        claim(6, "yo", g + 1)
                        pe.wait_ge(*reach("st_ev", 4))
                        pe.matmul(bank[6][:, :], XC[:, 20 + g, P:T], ST[:, g], start=True, stop=True, skip_group_check=True)
                    claim(4 + v % 2, "y", v + 1 if t == 0 else 4 + 2 * g + 1)
                    pe.wait_ge(*reach("seg_m", 2 * v + 2))
                    pe.wait_ge(*reach("xd", v + 1))
                    for h in range(8):
                        last = pe.matmul(bank[4 + v % 2][:, h * SP:(h + 1) * SP], EM(2 * v + h // 4)[:, h % 4 * P:(h % 4 + 1) * P],
                                         Xd[:, v % 2, h * SP:(h + 1) * SP], start=h == 0, stop=True, skip_group_check=True)
                    last.then_inc(S("y_mm"), 1)
            for c in range(8):
                s_ = need(f"z{c}")
                claim(c % 4, "z_s", c + 1)
                by_token(s_, c % 4, Uh, Ul, KD, 256).then_inc(S("slab_used"), 1)
            for g in (6, 7):
                s_ = need(f"g{g}")
                claim(gate2_bank[g], "g2_ev", g - 1)
                by_feature(s_, gate2_bank[g], Uh, Ul, KD, 256).then_inc(S("slab_used"), 1)
            for j in range(8):
                claim(j % 4, "yt_lo", 2 * j + 2)
                for c in range(2):
                    ch = 2 * j + c
                    for t in range(NT):
                        pe.wait_ge(*reach("yn", 2 * (ch // 4) + t + 1))
                        last = pe.transpose(bank[j % 4][:, c * T + t * P:c * T + (t + 1) * P], XS[:, t, ch * P:(ch + 1) * P], ident)
                last.then_inc(S("yt_tr"), 1)
            fresh.append(("yt_lo", 1, YTh))
            for q in range(4):
                claim(4 + q, "m2_b", q + 1)
                for k in range(2):
                    if q == 0 and k == 1:
                        pe.wait_ge(*reach("yt_lo", 16))
                    s_ = need(f"ws{q}{k}")
                    by_feature(s_, 4 + q, YTh, YTl, KD, 256, k0=KD * k, start=k == 0, stop=k == 1).then_inc(S("slab_used"), 1)
            fresh.append(("m2_lo", 2, Uh))
            for i in range(4):
                s_ = need(f"wo{i}")
                claim(i, "x5", i + 1)
                by_token(s_, i, Uh, Ul, KD, 256).then_inc(S("slab_used"), 1)
            pe_norm("n6")
            s_ = need("router")
            claim(0, "oh", 1)
            by_token(s_, 0, Uh, Ul, KD, EG + NE).then_inc(S("slab_used"), 1)
            pe.wait_ge(*reach("oh", 1))
            claim(2, "over", 1)
            oh = [rt("oh", 8)[:, EG * t:EG * (t + 1)] for t in range(NT)]
            ahead = const("earlier", 0, P)
            for n, (cols, w_, t) in enumerate(((0, ahead, 0), (1, const("ones"), 0), (1, ahead, 1), (2, const("ones"), 0),
                                               (2, const("ones"), 1))):
                last = pe.matmul(bank[2][:, cols * EG:(cols + 1) * EG], w_, oh[t], start=n == 0, stop=True, skip_group_check=True)
            last.then_inc(S("rank_mm"), 1)
            pe.wait_ge(*reach("pick", NT * EG))
            pe.wait_ge(*reach("xn_lo", NT))
            for c in range(KD):
                claim(4 + c % 4, "su_lo", c + 1)
                for t in range(NT):
                    for k, x_ in enumerate((XNh, XNl)):
                        last = pe.matmul(bank[4 + c % 4][:, :], x_[:, t, c * P:(c + 1) * P], PICK[:, t, 0:EG].rearrange("p g n -> p (g n)"),
                                         start=t + k == 0, stop=t + k == 2, skip_group_check=True)
                last.then_inc(S("su_mm"), 1)
            pe.wait_ge(*reach("pick", NT * (EG + 1)))
            for j in range(3):
                claim((0, 1, 3)[j], "pt_ev", j + 1)
                for g in range(2 * j, min(EG + 1, 2 * j + 2)):
                    for t in range(NT):
                        last = pe.transpose(bank[(0, 1, 3)[j]][:, (g - 2 * j) * T + t * P:(g - 2 * j) * T + (t + 1) * P], PICK[:, t, g].bitcast(F32), ident)
                last.then_inc(S("pt_mm"), 1)
            pe.wait_ge(*reach("cw", 1))
            claim(2, "cw_ev", 1)
            for g in range(EG + 1):
                for t in range(NT):
                    last = pe.matmul(bank[2][:, g * EPG:(g + 1) * EPG], PICK[:, t, g].bitcast(F32), rt("pick0", 16)[:, t * EPG:(t + 1) * EPG],
                                     start=g == 0 and t == 0, stop=t == 1, skip_group_check=True)
            last.then_inc(S("cw_mm"), 1)
            pe.wait_ge(*reach("su_lo", KD))
            pe.wait_ge(*reach("pt_ev", 3))
            pe.wait_ge(*reach("cw_ev", 1))
            pe_experts(slab_of["moe"], NE, 0, 0, lambda s: s)
            flag = overflow(pe)
            with pe.If(flag != 0):
                for c in range(KD):
                    for t in range(NT):
                        for k, x_ in enumerate((XNh, XNl)):
                            last = pe.matmul(bank[4 + c // 4][:, c % 4 * P:(c % 4 + 1) * P], x_[:, t, c * P:(c + 1) * P], PICK[:, t, EG],
                                             start=c % 4 + t + k == 0, stop=t + k == 2, skip_group_check=True)
                    if c % 4 == 3:
                        last.then_inc(S("su_mm"), 1)
                pe.wait_ge(*reach("su_lo", 2 * KD))
                pe_experts(over, EPG, NE, EG, lambda s: s)


_INS = ["x", "p", "positions", "ffn1_norm", "ffn1_w_in", "ffn1_w_out", "mix_norm", "w_in", "q_latent_norm", "w_q_up",
        "kv_latent_norm", "w_kv_up", "q_head_norm", "k_head_norm", "w_branch_mla", "w_branch_sb", "w_out", "ffn2_norm",
        "ffn2_w_in", "ffn2_w_out", "ple_norm", "w_ple_gate", "w_ple_proj", "attn_norm_2", "w_in_2", "q_norm_2",
        "k_norm_2", "idx_k_norm_2", "conv_w_2", "conv_b_2", "dt_bias_2", "a_log_2", "d_skip_2", "ssd_norm_2",
        "w_attn_branch_2", "w_ssd_branch_2", "w_out_2", "ffn_norm_2", "w_route_group_2", "b_route_group_2",
        "w_route_expert_2", "b_route_expert_2", "w_gate_2", "w_up_2", "w_down_2"]


def kernel(**inputs):
    from concourse import bacc as _bacc
    from concourse.bass_utils import run_bass_kernel_spmd
    nc = _bacc.Bacc("TRN2", target_bir_lowering=False, num_devices=1)
    arrays = {"in_" + name: np.ascontiguousarray(inputs[name]) for name in _INS}
    arrays["const"] = constants()
    a = {name.removeprefix("in_"): nc.dram_tensor(name, v.shape, mybir.dt.from_np(v.dtype), kind="ExternalInput").ap()
         for name, v in arrays.items()}
    out = nc.dram_tensor("out", [1, T, D], F32, kind="ExternalOutput").ap()
    two_blocks(nc, a, out)
    if not nc.is_finalized():
        nc.finalize()
    res = run_bass_kernel_spmd(nc, [arrays], core_ids=[0])
    return res.results[0]["out"]
```
